# Optimizing a Trainium2 kernel written in Bass

```python
import math
import jax, jax.numpy as jnp
from jax import lax
import numpy as np

D_MODEL = 1024
BATCH = 1
SEQ = 2048
DEPTH = 1
DEC_BATCH = 1
DEC_SEQ = 64
PAST_LEN = 256

CHUNK = 64
N_META = 16
HEAD_DIM = 64
SWA_HEADS = 8
SWA_KV_HEADS = 2
SWA_GROUP = SWA_HEADS // SWA_KV_HEADS
WINDOW = 128
WINDOW_CHUNKS = WINDOW // CHUNK
DIFF_HEADS = 4
DIFF_V_DIM = 2 * HEAD_DIM
SWA_Q_W = SWA_HEADS * HEAD_DIM
SWA_KV_W = SWA_KV_HEADS * HEAD_DIM
DIFF_QK_W = DIFF_HEADS * 2 * HEAD_DIM
DIFF_V_W = DIFF_HEADS * DIFF_V_DIM
PROJ_W = SWA_Q_W + 2 * SWA_KV_W + 2 * DIFF_QK_W + DIFF_V_W
MIX_W = SWA_Q_W + DIFF_V_W
D_FF = -(-8 * D_MODEL // (3 * 256)) * 256
ROPE_THETA = 10000.0
NORM_EPS = 1e-6
Q_BLOCK = 128
ATTN_SCALE = HEAD_DIM ** -0.5

kernel_name = 'hymba_swa_sink_diff_attn_stream_step'

def rms_norm(x, g):
    xf = x.astype(jnp.float32)
    y = xf * lax.rsqrt(jnp.mean(xf * xf, axis=-1, keepdims=True) + NORM_EPS)
    return (y * g.astype(jnp.float32)).astype(x.dtype)

def rotate_half(x):
    x1, x2 = jnp.split(x, 2, axis=-1)
    return jnp.concatenate([-x2, x1], axis=-1)

def rope(x, pos):
    inv = ROPE_THETA ** (-jnp.arange(0, HEAD_DIM, 2, dtype=jnp.float32) / HEAD_DIM)
    ang = pos.astype(jnp.float32)[:, None] * inv[None, :]
    ang = jnp.concatenate([ang, ang], axis=-1)
    shape = (ang.shape[0],) + (1,) * (x.ndim - 3) + (HEAD_DIM,)
    cos = jnp.cos(ang).reshape(shape)
    sin = jnp.sin(ang).reshape(shape)
    xf = x.astype(jnp.float32)
    return (xf * cos + rotate_half(xf) * sin).astype(x.dtype)

def mixer_inputs(h, pos, w_in):
    b, s, _ = h.shape
    z = jnp.einsum('bsd,dp->bsp', h, w_in)
    cuts = [SWA_Q_W, SWA_Q_W + SWA_KV_W, SWA_Q_W + 2 * SWA_KV_W,
            SWA_Q_W + 2 * SWA_KV_W + DIFF_QK_W, SWA_Q_W + 2 * SWA_KV_W + 2 * DIFF_QK_W]
    qa, ka, va, qd, kd, vd = jnp.split(z, cuts, axis=-1)
    qa = rope(qa.reshape(b, s, SWA_HEADS, HEAD_DIM), pos)
    ka = rope(ka.reshape(b, s, SWA_KV_HEADS, HEAD_DIM), pos)
    va = va.reshape(b, s, SWA_KV_HEADS, HEAD_DIM)
    qd = rope(qd.reshape(b, s, DIFF_HEADS, 2, HEAD_DIM), pos)
    kd = rope(kd.reshape(b, s, DIFF_HEADS, 2, HEAD_DIM), pos)
    vd = vd.reshape(b, s, DIFF_HEADS, DIFF_V_DIM)
    return qa, ka, va, qd, kd, vd

def attn_mask(q_idx, k_idx, chunks_back):
    qi = q_idx[..., :, None]
    ki = k_idx[..., None, :]
    qc = qi // CHUNK
    kc = ki // CHUNK
    vis = (ki >= 0) & (kc <= qc)
    if chunks_back is not None:
        vis = vis & (kc > qc - chunks_back)
    meta = jnp.ones(vis.shape[:-1] + (N_META,), dtype=bool)
    return jnp.concatenate([meta, vis], axis=-1)

def sink_attention(q, k, v, mask, sinks):
    s = jnp.einsum('...qhgd,...khd->...hgqk', q, k).astype(jnp.float32) * ATTN_SCALE
    s = jnp.where(mask, s, -jnp.inf)
    sink_col = jnp.broadcast_to(sinks.astype(jnp.float32).reshape(SWA_KV_HEADS, SWA_GROUP, 1, 1),
                                s.shape[:-1] + (1,))
    p = jax.nn.softmax(jnp.concatenate([s, sink_col], axis=-1), axis=-1)[..., :-1]
    return jnp.einsum('...hgqk,...khd->...qhgd', p.astype(v.dtype), v)

def diff_attention(q, k, v, mask, lam, subln_g, lam_init):
    s = jnp.einsum('...qhcd,...khcd->...hcqk', q, k).astype(jnp.float32) * ATTN_SCALE
    s = jnp.where(mask, s, -jnp.inf)
    p = jax.nn.softmax(s, axis=-1)
    w = p[..., 0, :, :] - lam * p[..., 1, :, :]
    o = jnp.einsum('...hqk,...khe->...qhe', w.astype(v.dtype), v)
    return rms_norm(o, subln_g) * (1.0 - lam_init)

def chunk_band(x, x_meta):
    b, s = x.shape[:2]
    nc = s // CHUNK
    xc = x.reshape((b, nc, CHUNK) + x.shape[2:])
    parts = [jnp.broadcast_to(x_meta[:, None], (b, nc) + x_meta.shape[1:])]
    for w in range(WINDOW_CHUNKS - 1, -1, -1):
        pw = [(0, 0)] * xc.ndim
        pw[1] = (w, 0)
        parts.append(jnp.pad(xc, pw)[:, :nc])
    return jnp.concatenate(parts, axis=2)

def swa_prompt(qa, ka, va, ka_m, va_m, sinks):
    b, s = qa.shape[:2]
    nc = s // CHUNK
    q = qa.reshape(b, nc, CHUNK, SWA_KV_HEADS, SWA_GROUP, HEAD_DIM)
    k_band = chunk_band(ka, ka_m)
    v_band = chunk_band(va, va_m)
    c = jnp.arange(nc)
    offs = jnp.arange(WINDOW_CHUNKS - 1, -1, -1)
    j = jnp.arange(CHUNK)
    k_idx = ((c[:, None, None] - offs[None, :, None]) * CHUNK + j[None, None, :]).reshape(nc, WINDOW_CHUNKS * CHUNK)
    q_idx = jnp.arange(s).reshape(nc, CHUNK)
    mask = attn_mask(q_idx, k_idx, WINDOW_CHUNKS)[None, :, None, None]
    o = sink_attention(q, k_band, v_band, mask, sinks)
    return o.reshape(b, s, SWA_Q_W)

def diff_prompt(qd, kd_all, vd_all, lam, subln_g, lam_init):
    b, s = qd.shape[:2]
    nb = s // Q_BLOCK
    frames = jnp.arange(s)
    q_blocks = jnp.moveaxis(qd.reshape((b, nb, Q_BLOCK) + qd.shape[2:]), 1, 0)
    idx_blocks = frames.reshape(nb, Q_BLOCK)

    def block(args):
        q_blk, q_idx = args
        return diff_attention(q_blk, kd_all, vd_all, attn_mask(q_idx, frames, None), lam, subln_g, lam_init)

    o = lax.map(block, (q_blocks, idx_blocks))
    return jnp.moveaxis(o, 0, 1).reshape(b, s, DIFF_V_W)

def mix_out(a, d, w_out):
    return jnp.einsum('bsm,md->bsd', jnp.concatenate([a, d], axis=-1), w_out)

def swiglu(h, w_gate, w_up, w_down):
    g = jnp.einsum('bsd,df->bsf', h, w_gate)
    u = jnp.einsum('bsd,df->bsf', h, w_up)
    return jnp.einsum('bsf,fd->bsd', jax.nn.silu(g) * u, w_down)

def bcast(x, b):
    return jnp.broadcast_to(x, (b,) + x.shape[1:])

def setup_inputs(seed: int = 0) -> dict:
    key = jax.random.key(seed)
    ks = jax.random.split(key, 24)
    nrm = jax.random.normal
    f32 = jnp.float32
    swa_rows = min(WINDOW, PAST_LEN)
    return {
        'x_prompt': nrm(ks[0], (BATCH, SEQ, D_MODEL), f32),
        'x_sample': nrm(ks[1], (DEC_BATCH, DEC_SEQ, D_MODEL), f32),
        'cache_swa_k': nrm(ks[2], (DEPTH, DEC_BATCH, N_META + swa_rows, SWA_KV_HEADS, HEAD_DIM), f32),
        'cache_swa_v': nrm(ks[3], (DEPTH, DEC_BATCH, N_META + swa_rows, SWA_KV_HEADS, HEAD_DIM), f32),
        'cache_diff_k': nrm(ks[4], (DEPTH, DEC_BATCH, N_META + PAST_LEN, DIFF_HEADS, 2, HEAD_DIM), f32),
        'cache_diff_v': nrm(ks[5], (DEPTH, DEC_BATCH, N_META + PAST_LEN, DIFF_HEADS, DIFF_V_DIM), f32),
        'meta_tokens': nrm(ks[6], (N_META, D_MODEL), f32),
        'norm_mix_g': 1.0 + 0.02 * nrm(ks[7], (DEPTH, D_MODEL), f32),
        'w_in': nrm(ks[8], (DEPTH, D_MODEL, PROJ_W), f32) * D_MODEL ** -0.5,
        'attn_sinks': 0.5 * nrm(ks[9], (DEPTH, SWA_HEADS), f32),
        'lambda_q1': 0.1 * nrm(ks[10], (DEPTH, HEAD_DIM), f32),
        'lambda_k1': 0.1 * nrm(ks[11], (DEPTH, HEAD_DIM), f32),
        'lambda_q2': 0.1 * nrm(ks[12], (DEPTH, HEAD_DIM), f32),
        'lambda_k2': 0.1 * nrm(ks[13], (DEPTH, HEAD_DIM), f32),
        'subln_g': 1.0 + 0.02 * nrm(ks[14], (DEPTH, DIFF_V_DIM), f32),
        'w_out': nrm(ks[15], (DEPTH, MIX_W, D_MODEL), f32) * MIX_W ** -0.5,
        'norm_ffn_g': 1.0 + 0.02 * nrm(ks[16], (DEPTH, D_MODEL), f32),
        'w_gate': nrm(ks[17], (DEPTH, D_MODEL, D_FF), f32) * D_MODEL ** -0.5,
        'w_up': nrm(ks[18], (DEPTH, D_MODEL, D_FF), f32) * D_MODEL ** -0.5,
        'w_down': nrm(ks[19], (DEPTH, D_FF, D_MODEL), f32) * D_FF ** -0.5,
        'final_norm_g': 1.0 + 0.02 * nrm(ks[20], (D_MODEL,), f32),
    }

def reference(x_prompt, x_sample, cache_swa_k, cache_swa_v, cache_diff_k, cache_diff_v,
              meta_tokens, norm_mix_g, w_in, attn_sinks, lambda_q1, lambda_k1, lambda_q2, lambda_k2,
              subln_g, w_out, norm_ffn_g, w_gate, w_up, w_down, final_norm_g):
    b, seq = x_prompt.shape[:2]
    db, dseq = x_sample.shape[:2]
    past_len = cache_diff_k.shape[2] - N_META
    swa_rows_s = cache_swa_k.shape[2] - N_META
    swa_rows_p = min(WINDOW, seq)

    pos_meta = jnp.arange(N_META)
    frame_p = jnp.arange(seq)
    frame_s = past_len + jnp.arange(dseq)
    pos_p = N_META + frame_p
    pos_s = N_META + frame_s
    keys_s_swa = jnp.concatenate([past_len - swa_rows_s + jnp.arange(swa_rows_s), frame_s])
    keys_s_diff = jnp.concatenate([jnp.arange(past_len), frame_s])
    mask_s_swa = attn_mask(frame_s, keys_s_swa, WINDOW_CHUNKS)
    mask_s_diff = attn_mask(frame_s, keys_s_diff, None)
    mask_meta = jnp.ones((N_META, N_META), dtype=bool)

    meta_h = meta_tokens[None]
    hp = x_prompt
    hs = x_sample
    p_swa_k, p_swa_v, p_diff_k, p_diff_v = [], [], [], []
    s_swa_k, s_swa_v, s_diff_k, s_diff_v = [], [], [], []

    for l in range(DEPTH):
        lam_init = 0.8 - 0.6 * math.exp(-0.3 * l)
        lam = (jnp.exp(jnp.sum(lambda_q1[l].astype(jnp.float32) * lambda_k1[l].astype(jnp.float32)))
               - jnp.exp(jnp.sum(lambda_q2[l].astype(jnp.float32) * lambda_k2[l].astype(jnp.float32)))
               + lam_init)
        g_mix = norm_mix_g[l]

        qa_m, ka_m, va_m, qd_m, kd_m, vd_m = mixer_inputs(rms_norm(meta_h, g_mix), pos_meta, w_in[l])

        qa, ka, va, qd, kd, vd = mixer_inputs(rms_norm(hp, g_mix), pos_p, w_in[l])
        a_p = swa_prompt(qa, ka, va, ka_m, va_m, attn_sinks[l])
        kd_all = jnp.concatenate([bcast(kd_m, b), kd], axis=1)
        vd_all = jnp.concatenate([bcast(vd_m, b), vd], axis=1)
        d_p = diff_prompt(qd, kd_all, vd_all, lam, subln_g[l], lam_init)
        hp = hp + mix_out(a_p, d_p, w_out[l])
        hp = hp + swiglu(rms_norm(hp, norm_ffn_g[l]), w_gate[l], w_up[l], w_down[l])
        p_swa_k.append(jnp.concatenate([bcast(ka_m, b), ka[:, seq - swa_rows_p:]], axis=1))
        p_swa_v.append(jnp.concatenate([bcast(va_m, b), va[:, seq - swa_rows_p:]], axis=1))
        p_diff_k.append(kd_all)
        p_diff_v.append(vd_all)

        qa_s, ka_s, va_s, qd_s, kd_s, vd_s = mixer_inputs(rms_norm(hs, g_mix), pos_s, w_in[l])
        ksw = jnp.concatenate([cache_swa_k[l], ka_s], axis=1)
        vsw = jnp.concatenate([cache_swa_v[l], va_s], axis=1)
        a_s = sink_attention(qa_s.reshape(db, dseq, SWA_KV_HEADS, SWA_GROUP, HEAD_DIM),
                             ksw, vsw, mask_s_swa, attn_sinks[l]).reshape(db, dseq, SWA_Q_W)
        kds = jnp.concatenate([cache_diff_k[l], kd_s], axis=1)
        vds = jnp.concatenate([cache_diff_v[l], vd_s], axis=1)
        d_s = diff_attention(qd_s, kds, vds, mask_s_diff, lam, subln_g[l], lam_init).reshape(db, dseq, DIFF_V_W)
        hs = hs + mix_out(a_s, d_s, w_out[l])
        hs = hs + swiglu(rms_norm(hs, norm_ffn_g[l]), w_gate[l], w_up[l], w_down[l])
        n_rows = ksw.shape[1]
        s_swa_k.append(jnp.concatenate([ksw[:, :N_META], ksw[:, n_rows - swa_rows_s:]], axis=1))
        s_swa_v.append(jnp.concatenate([vsw[:, :N_META], vsw[:, n_rows - swa_rows_s:]], axis=1))
        s_diff_k.append(kd_s)
        s_diff_v.append(vd_s)

        if l < DEPTH - 1:
            a_m = sink_attention(qa_m.reshape(1, N_META, SWA_KV_HEADS, SWA_GROUP, HEAD_DIM),
                                 ka_m, va_m, mask_meta, attn_sinks[l]).reshape(1, N_META, SWA_Q_W)
            d_m = diff_attention(qd_m, kd_m, vd_m, mask_meta, lam, subln_g[l], lam_init).reshape(1, N_META, DIFF_V_W)
            meta_h = meta_h + mix_out(a_m, d_m, w_out[l])
            meta_h = meta_h + swiglu(rms_norm(meta_h, norm_ffn_g[l]), w_gate[l], w_up[l], w_down[l])

    y_prompt = rms_norm(hp, final_norm_g)
    y_sample = rms_norm(hs, final_norm_g)
    new_p_swa_k = jnp.stack(p_swa_k)
    new_p_swa_v = jnp.stack(p_swa_v)
    new_p_diff_k = jnp.stack(p_diff_k)
    new_p_diff_v = jnp.stack(p_diff_v)
    new_s_swa_k = jnp.stack(s_swa_k)
    new_s_swa_v = jnp.stack(s_swa_v)
    new_s_diff_k = jnp.stack(s_diff_k)
    new_s_diff_v = jnp.stack(s_diff_v)
    return (y_prompt, y_sample, new_p_swa_k, new_p_swa_v, new_p_diff_k, new_p_diff_v,
            new_s_swa_k, new_s_swa_v, new_s_diff_k, new_s_diff_v)


_drawn_inputs = setup_inputs


def setup_inputs(seed=0):
    import zlib

    import numpy as np

    out = dict(_drawn_inputs(seed))
    spreads = {}
    factors = {'attn_sinks': 26.12,
     'lambda_q1': 8.0,
     'subln_g': 5.259,
     'norm_ffn_g': 4.312,
     'final_norm_g': 8.667}
    for name, (base, spread) in spreads.items():
        noise = np.random.default_rng([zlib.crc32(name.encode()), seed]).standard_normal(out[name].shape)
        drawn = base * np.exp(spread * noise) if base else spread * noise
        out[name] = __import__('jax').numpy.asarray(drawn.astype(out[name].dtype))
    for name, factor in factors.items():
        out[name] = (out[name] * factor).astype(out[name].dtype)
    return out
```

```python
import math
from contextlib import ExitStack

import numpy as np

import concourse.bass as bass
from concourse import mybir

f32 = mybir.dt.float32
f16 = mybir.dt.float16
bf16 = mybir.dt.bfloat16
i32 = mybir.dt.int32
ACT = mybir.ActivationFunctionType
ALU = mybir.AluOpType
AX = mybir.AxisListType
RMAX = bass.bass_isa.ReduceOp.max

P = 128
D = 1024
KC = D // P
SEQ = 2048
META = 16
DEC = 64
PAST = 256
HD = 64
HS = 8
KVS = 2
GRP = HS // KVS
HDIF = 4
HC = 2 * HDIF
VD = 2 * HD
FF = 2816
WIN = 128
CH = 64
EPS = 1e-6
PROJ = 2304
NT = SEQ // P
TS = NT
NTT = NT + 1
C_QA, C_KA, C_VA, C_QD, C_KD, C_VD = 0, 512, 640, 768, 1280, 1792
SCR = C_KD
LAM_INIT = 0.8 - 0.6 * math.exp(-0.3 * 0)
XSC = 256.0
MROW = 32768.0
NKT = NT + 4
VW = VD + 1
WCH = 1408


class Prog:

    def __init__(self, nc, dram, ctx):
        self.nc, self.dram, self.ctx, self.sems = nc, dram, ctx, []

    def sb(self, name, shape, dt, ctx=None):
        return (ctx or self.ctx).enter_context(self.nc.sbuf_tensor(name, shape, dt))

    def ps(self, name, shape, dt, ctx):
        return ctx.enter_context(self.nc.psum_tensor(name, shape, dt))

    def sem(self, name):
        self.sems.append(self.nc.alloc_semaphore(name=name))
        return self.sems[-1]

    def phase_end(self):
        self.nc.clear_and_free_semaphores(self.sems)
        self.nc.all_engine_barrier()
        self.sems = []


class Chain:

    def __init__(self, eng, sem, start=0):
        self.eng, self.sem, self.n = eng, sem, start

    def __call__(self, ins):
        self.n += 1
        ins.then_inc(self.sem, 1)
        self.eng.wait_ge(self.sem, self.n)


def pow2(nc, link, out, field, tmp_f, tmp_i, src_f, mult, add, lo=1.0, hi=254.0):
    link(nc.vector.tensor_scalar(tmp_f, src_f, float(mult), float(add), ALU.mult, ALU.add))
    link(nc.vector.tensor_scalar(field, tmp_f, float(lo), float(hi), ALU.max, ALU.min))
    pow2_of(nc, link, out, field, tmp_i)


def pow2_of(nc, link, out, field, tmp_i):
    link(nc.vector.tensor_copy(tmp_i, field))
    link(nc.vector.tensor_scalar(out.bitcast(i32), tmp_i, 23, None, ALU.arith_shift_left))


def exponent(nc, link, out_f, tmp_i, value):
    link(nc.vector.tensor_scalar(tmp_i, value.bitcast(i32), 23, None, ALU.arith_shift_right))
    link(nc.vector.tensor_copy(out_f, tmp_i))


(S_MXW, S_MXC, S_AW, S_AC, S_EW, S_EC, S_W, S_ZI, S_A, S_AI, S_SC, S_F0, S_F1, S_F2, S_F3, S_T, S_LAM,
 S_L1, S_L2, S_L3, S_GMX, S_EG, S_G, S_GI, S_ACT, S_CU, S_D, S_YI, S_F4, S_F5, S_F6, S_MXO, S_O, S_OA, S_OD,
 S_AO, S_SUM, S_F7, S_F8, S_NAI, S_MX3, S_MX4, S_MX5, S_AG, S_AGU, S_AD, S_EGU, S_ED, S_GI2) = range(49)
NSC = 56


def phase_weights_in(g, W32, WH, WL):
    nc, dram = g.nc, g.dram
    with ExitStack() as ctx:
        CA = g.sb("cache_rows", [P, 2464], f32, ctx)
        GM = g.sb("gain_mix", [P, KC], f32, ctx)
        LV = g.sb("lambda_vecs", [P, 4, HD], f32, ctx)
        LP = g.sb("lambda_prod", [P, 2, HD], f32, ctx)
        MK = g.sb("max_by_chunk", [P, KC], f32, ctx)
        TI = g.sb("tmp_int", [P, 2], i32, ctx)
        SC = g.SC
        small_in, cache_in = (g.sem(n) for n in ("w0_small_in", "w0_cache_in"))
        max_local, max_all, dve_step = (g.sem(n) for n in ("w0_max_local", "w0_max_all", "w0_dve_step"))
        scales_ok, hi_ok, lam_dot, lam_exp = (g.sem(n) for n in ("w0_scales", "w0_hi", "w0_lam_dot", "w0_lam_exp"))
        col = lambda c: SC[:, c:c + 1]
        with nc.Block() as block:
            @block.sync
            def _(sp):
                sp.dma_start(GM[:, :], dram["norm_mix_g"]).then_inc(small_in, 16)
                sp.dma_start(g.ident[:, :], dram["ident"]).then_inc(small_in, 16)
                sp.dma_start(LV[:, :, :], dram["lambdas"].rearrange("a n d -> a (n d)").broadcast_to([P, 4 * HD])
                             .rearrange("p (n d) -> p n d", n=4)).then_inc(small_in, 16)
                for k in range(KC):
                    sp.dma_start(W32[:, k, :], dram["w_in"][0, k * P:(k + 1) * P, :]).then_inc(g.w0_k[k], 16)
                at = 0
                for name, width in (("cache_diff_k", 1088), ("cache_diff_v", 1088), ("cache_swa_k", 144), ("cache_swa_v", 144)):
                    sp.dma_start(CA[:, at:at + width], dram[name]
                                 .rearrange("a b r h c d -> (a b r h c d)" if name == "cache_diff_k" else
                                            "a b r h d -> (a b r h d)")
                                 .rearrange("(p n) -> p n", p=P)).then_inc(cache_in, 16)
                    at += width

            @block.gpsimd
            def _(pool):
                for n, (src, dst) in enumerate(((S_MXC, S_AC), (S_MXW, S_AW))):
                    pool.wait_ge(max_local, n + 1)
                    nc.gpsimd.partition_all_reduce(col(dst), col(src), P, RMAX).then_inc(max_all, 1)

            @block.vector
            def _(dve):
                link = Chain(dve, dve_step)
                dve.wait_ge(small_in, 48)
                for n in range(2):
                    link(nc.vector.tensor_tensor(LP[:, n, :], LV[:, 2 * n, :], LV[:, 2 * n + 1, :], ALU.mult))
                    nc.vector.tensor_reduce(col(S_L1 + n), LP[:, n, :], AX.X, ALU.add).then_inc(lam_dot, 1)
                for k in range(KC):
                    dve.wait_ge(g.w0_k[k], 16)
                    link(nc.vector.tensor_scalar(W32[:, k, :], W32[:, k, :], GM[:, k:k + 1], None, ALU.mult))
                    link(nc.vector.tensor_reduce(MK[:, k:k + 1], W32[:, k, :], AX.X, ALU.max,
                                                 apply_absolute_value=True))
                    if k == 4:
                        dve.wait_ge(cache_in, 64)
                        nc.vector.tensor_reduce(col(S_MXC), CA[:, :], AX.X, ALU.max,
                                                apply_absolute_value=True).then_inc(max_local, 1)
                nc.vector.tensor_reduce(col(S_MXW), MK[:, :], AX.X, ALU.max).then_inc(max_local, 1)
                dve.wait_ge(lam_exp, 2)
                link(nc.vector.scalar_tensor_tensor(col(S_LAM), col(S_L1), -1.0, col(S_L2), ALU.mult, ALU.add))
                link(nc.vector.tensor_scalar(col(S_LAM), col(S_LAM), -LAM_INIT, None, ALU.add))
                dve.wait_ge(max_all, 2)
                exponent(nc, link, col(S_EW), TI[:, 0:1], col(S_AW))
                exponent(nc, link, col(S_EC), TI[:, 0:1], col(S_AC))
                link(nc.vector.tensor_scalar(col(S_EW), col(S_EW), 30.0, 220.0, ALU.max, ALU.min))
                pow2(nc, link, col(S_W), col(S_F0), col(S_T), TI[:, 0:1], col(S_EW), -1.0, 265.0)
                pow2(nc, link, col(S_ZI), col(S_F0), col(S_T), TI[:, 0:1], col(S_EW), 1.0, -19.0)
                link(nc.vector.tensor_scalar(col(S_F1), col(S_EW), -1.0, 254.0, ALU.mult, ALU.add))
                link(nc.vector.tensor_scalar(col(S_F2), col(S_EC), -1.0, 265.0, ALU.mult, ALU.add))
                link(nc.vector.tensor_tensor(col(S_F2), col(S_F1), col(S_F2), ALU.min))
                pow2(nc, link, col(S_A), col(S_F1), col(S_T), TI[:, 0:1], col(S_F2), 1.0, 0.0, 97.0, 157.0)
                pow2(nc, link, col(S_AI), col(S_F2), col(S_T), TI[:, 0:1], col(S_F1), -1.0, 254.0)
                pow2(nc, link, col(S_SC), col(S_F2), col(S_T), TI[:, 0:1], col(S_F1), -2.0, 378.0)
                nc.vector.tensor_scalar(col(S_NAI), col(S_SC), MROW, None, ALU.mult).then_inc(scales_ok, 1)
                for k in range(KC):
                    dve.wait_ge(hi_ok, k + 1)
                    link(nc.vector.scalar_tensor_tensor(WL[:, k, :], W32[:, k, :], col(S_W), WH[:, k, :],
                                                        ALU.mult, ALU.subtract))

            @block.scalar
            def _(act):
                for n in range(2):
                    act.wait_ge(lam_dot, n + 1)
                    nc.scalar.activation(col(S_L1 + n), col(S_L1 + n), ACT.Exp).then_inc(lam_exp, 1)
                act.wait_ge(scales_ok, 1)
                for k in range(KC):
                    nc.scalar.activation(WH[:, k, :], W32[:, k, :], ACT.Copy, scale=col(S_W)).then_inc(hi_ok, 1)


V_COUNT = {0: 0, 1: 1, 2: 1, 3: 1, 4: 2, 5: 3}


def phase_project(g, WH, WL, K1, VH, VL, MW):
    nc, dram = g.nc, g.dram
    with ExitStack() as ctx:
        X = [g.sb(f"x_tile{n}", [P, D], f32, ctx) for n in range(2)]
        CS = [g.sb(f"cos_sin{n}", [P, 2 * HD], f32, ctx) for n in range(2)]
        NH, NL = (g.sb(n, [P, D], f16, ctx) for n in ("norm_hi", "norm_lo"))
        XT = [[g.sb(f"normT_{h}{n}", [P, KC, P], f16, ctx) for h in ("hi", "lo")] for n in range(2)]
        Z = g.sb("z_tile", [P, PROJ], f32, ctx)
        RT = [g.sb(f"rot_tmp{n}", [P, 384], f32, ctx) for n in range(2)]
        KN = g.sb("k_split", [P, HC, P], f16, ctx)
        WS = [g.sb(f"w_scan{n}", [P, WCH], f32, ctx) for n in range(2)]
        ST = g.sb("row_stats", [P, 8], f32, ctx)
        TH = g.ps("xT_hi_ps", [P, KC * P], f16, ctx)
        TL = g.ps("xT_lo_ps", [P, KC * P], f16, ctx)
        ZP = [g.ps(f"z_ps{n}", [P, 512], f32, ctx) for n in range(3)]
        KT = g.ps("kT_ps", [P, HC * P], f16, ctx)
        SC = g.SC
        col = lambda c: SC[:, c:c + 1]
        s = g.sem
        x_in = [s(f"p1_x_in{n}") for n in range(2)]
        ws_in = [s(f"p1_wscan_in{n}") for n in range(2)]
        stat_ok, rs_ok = s("p1_stat"), s("p1_rs")
        hi_ok, lo_ok, t_ok, th_out, tl_out = s("p1_hi"), s("p1_lo"), s("p1_transposed"), s("p1_th_out"), s("p1_tl_out")
        z_ok, rot_mul, rot_add, v_ok, stored = s("p1_z"), s("p1_rot_mul"), s("p1_rot_add"), s("p1_v"), s("p1_stored")
        kv_hi, kv_lo, kt_ok, kt_out, scanned = s("p1_kv_hi"), s("p1_kv_lo"), s("p1_kt"), s("p1_kt_out"), s("p1_scanned")
        pool_step, ones_ok, cache_in, tile_done = s("p1_pool_step"), s("p1_ones"), s("p1_cache_in"), s("p1_mm_done")
        STORES = 16 * 3
        sp_turns = s("p1_sp_turns")
        vtile = lambda V, i: V[:, bass.ds(i * HDIF * VW, HDIF * VW)].rearrange("p (h e) -> p h e", h=HDIF)
        scan = [dram[n].rearrange("a r c -> (a r c)").rearrange("(p n) -> p n", p=P) for n in ("w_gate", "w_up", "w_down")]

        with nc.Block() as block:
            @block.sync
            def _(sp):
                def reg(x):
                    return x if isinstance(x, int) else sp.snap(x)

                def load(i, b):
                    row = reg(i * P)
                    if not isinstance(i, int) or i > 1:
                        n_lo, n_rot = reg(i - 1), reg(5 * i - 5)
                        sp.wait_ge(lo_ok, n_lo)
                        sp.wait_ge(rot_mul, n_rot)
                    sp.dma_start(X[b][:, :], dram["x"][bass.ds(row, P), :]).then_inc(x_in[b], 16)
                    sp.dma_start(CS[b][:, :], dram["cos_sin"][bass.ds(row, P), :]).then_inc(x_in[b], 16)

                def store(i, last):
                    row, row_kv, n_rot, n_v = (reg(x) for x in (i * P, META + i * P, 5 * i + 5, 3 * i + 3))
                    sp.wait_ge(rot_add, n_rot)
                    sp.sem_inc(sp_turns, 1)
                    sp.wait_ge(v_ok, n_v)
                    sp.dma_start(g.scr[bass.ds(row, P), :], Z[:, 0:SCR]).then_inc(stored, 16)
                    if not last:
                        sp.dma_start(dram["p_diff_k"][bass.ds(row_kv, P), :], Z[:, C_KD:C_VD]).then_inc(stored, 16)
                        sp.dma_start(dram["p_diff_v"][bass.ds(row_kv, P), :], Z[:, C_VD:PROJ]).then_inc(stored, 16)
                        return
                    m = slice(DEC, DEC + META)
                    for name, a, b in (("diff_k", C_KD, C_VD), ("diff_v", C_VD, PROJ)):
                        sp.dma_start(dram[f"s_{name}"], Z[0:DEC, a:b]).then_inc(stored, 16)
                        sp.dma_start(dram[f"p_{name}"][0:META, :], Z[m, a:b]).then_inc(stored, 16)
                    for name, a, b in (("swa_k", C_KA, C_VA), ("swa_v", C_VA, C_QD)):
                        sp.dma_start(dram[f"p_{name}"][0:META, :], Z[m, a:b]).then_inc(stored, 16)
                        sp.dma_start(dram[f"s_{name}"][META + WIN - DEC:META + WIN, :], Z[0:DEC, a:b]).then_inc(stored, 16)

                load(0, 0)

                def step(i, b, first, last):
                    if last:
                        return store(i, True)
                    load(i + 1, 1 - b)
                    for w in range(3):
                        n = (b + w) % 2
                        at, used = reg(i * WCH), reg(3 * i + w - 1)
                        if not (first and w == 0):
                            sp.wait_ge(scanned, used)
                        sp.dma_start(WS[n][:, :], scan[w][:, bass.ds(at, WCH)]).then_inc(ws_in[n], 16)
                    store(i, False)
                row_tiles(sp, step)
                sp.wait_ge(stored, STORES * NT + 16 * 9)
                for n, (at, rows) in enumerate(((0, P), (P, P), (2 * P, META))):
                    sp.wait_ge(kv_hi, NTT + n)
                    sp.wait_ge(kv_lo, NTT + n)
                    for name, a, b in (("cache_diff_k", C_KD, C_VD), ("cache_diff_v", C_VD, PROJ)):
                        src = dram[name].rearrange("a b r h c d -> (a b r) (h c d)" if name[-1] == "k"
                                                   else "a b r h d -> (a b r) (h d)")
                        sp.dma_start(Z[0:rows, a:b], src[at:at + rows, :]).then_inc(cache_in, 16)
                n = 0
                for name, c in (("swa_k", C_KA), ("swa_v", C_VA)):
                    sp.dma_start(dram[f"p_{name}"][META:META + WIN, :],
                                 g.scr[SEQ - WIN:SEQ, c:c + KVS * HD]).then_inc(stored, 16)
                    old = dram[f"cache_{name}"].rearrange("a b r h d -> (a b r) (h d)")
                    sp.dma_start(dram[f"s_{name}"][0:META, :], old[0:META, :]).then_inc(stored, 16)
                    sp.dma_start(dram[f"s_{name}"][META:META + WIN - DEC, :],
                                 old[META + DEC:META + WIN, :]).then_inc(stored, 16)
                    n += 3
                sp.wait_ge(stored, STORES * NT + 16 * (9 + n))

            @block.gpsimd
            def _(pool):
                for c, value in ((4, -0.5), (5, EPS), (6, XSC)):
                    nc.gpsimd.memset(ST[:, c:c + 1], value).then_inc(ones_ok, 1)
                nc.gpsimd.memset(VH[:, :].rearrange("p (n e) -> p n e", e=VW)[:, :, VD:VW], 1.0).then_inc(ones_ok, 1)
                nc.gpsimd.memset(VL[:, :].rearrange("p (n e) -> p n e", e=VW)[:, :, VD:VW], 0.0).then_inc(ones_ok, 1)
                pool.wait_ge(ones_ok, 5)

                def rstd(i):
                    pool.wait_ge(stat_ok, i + 1)
                    nc.gpsimd.tensor_tensor(ST[:, 1:2], ST[:, 0:1], ST[:, 5:6], ALU.add).then_inc(pool_step, 1)
                    pool.wait_ge(pool_step, 2 * i + 1)
                    nc.gpsimd.tensor_tensor(ST[:, 2:3], ST[:, 1:2], ST[:, 4:5], ALU.pow).then_inc(pool_step, 1)
                    pool.wait_ge(pool_step, 2 * i + 2)
                    pool.wait_ge(lo_ok, i)
                    nc.gpsimd.tensor_tensor(ST[:, 3:4], ST[:, 2:3], ST[:, 6:7], ALU.mult).then_inc(rs_ok, 1)
                rstd(0)

                def step(i, b, first, last):
                    if not last:
                        rstd(i + 1)
                    for k, n in enumerate((384, 256, 384, 384, 256)):
                        pool.wait_ge(rot_mul, 5 * i + k + 1)
                        nc.gpsimd.tensor_tensor(Z[:, 384 * k:384 * k + n], Z[:, 384 * k:384 * k + n],
                                                RT[(b + k) % 2][:, 0:n], ALU.add).then_inc(rot_add, 1)
                row_tiles(pool, step)

            @block.vector
            def _(dve):
                def norm_lo(i, b):
                    dve.wait_ge(hi_ok, i + 1)
                    dve.wait_ge(t_ok, i)
                    nc.vector.scalar_tensor_tensor(NL[:, :], X[b][:, :], ST[:, 3:4], NH[:, :],
                                                   ALU.mult, ALU.subtract).then_inc(lo_ok, 1)

                def xT_lo_out(i, b, early):
                    dve.wait_ge(t_ok, i + 1)
                    if not early:
                        dve.wait_ge(tile_done, i - 1)
                    nc.vector.tensor_copy(XT[b][1][:, :, :], TL[:, :].rearrange("p (k n) -> p k n", k=KC)).then_inc(tl_out, 1)

                def rotary(i, k, b):
                    n = 256 if k in (1, 4) else 384
                    q = (b + k) % 2
                    dve.wait_ge(z_ok, 6 * i + k + 1)
                    cos = CS[b][:, 0:HD].unsqueeze(1).broadcast_to([P, n // HD, HD])
                    src = ZP[k % 3][:, 0:n].rearrange("p (h d) -> p h d", d=HD)
                    dst = Z[:, 384 * k:384 * k + n].rearrange("p (h d) -> p h d", d=HD)
                    tmp = RT[q][:, 0:n].rearrange("p (h d) -> p h d", d=HD)
                    nc.vector.scalar_tensor_tensor(dst, src, col(S_ZI), cos, ALU.mult, ALU.mult)
                    H2 = HD // 2
                    for half in range(2):
                        sin = CS[b][:, HD + half * H2:HD + (half + 1) * H2].unsqueeze(1).broadcast_to([P, n // HD, H2])
                        last = nc.vector.scalar_tensor_tensor(tmp[:, :, half * H2:(half + 1) * H2],
                                                              src[:, :, (1 - half) * H2:(2 - half) * H2],
                                                              col(S_ZI), sin, ALU.mult, ALU.mult)
                    last.then_inc(rot_mul, 1)

                def scan_max(i, b, w):
                    n = (b + w) % 2
                    dve.wait_ge(ws_in[n], scan_count(i, b, w) * 16)
                    nc.vector.tensor_reduce(MW[:, bass.ds(i * 3 + w, 1)], WS[n][:, :], AX.X, ALU.max,
                                            apply_absolute_value=True).then_inc(scanned, 1)

                def split_lo(i, v_first):
                    dve.wait_ge(kv_hi, i + 1)
                    nc.vector.scalar_tensor_tensor(KN[:, :, HD:P], Z[:, C_KD:C_VD].rearrange("p (h d) -> p h d", d=HD),
                                                   col(S_A), KN[:, :, 0:HD], ALU.mult, ALU.subtract)
                    nc.vector.scalar_tensor_tensor(vtile(VL, i)[:, :, 0:VD],
                                                   Z[:, C_VD:PROJ].rearrange("p (h e) -> p h e", e=VD), col(S_A),
                                                   vtile(VH, i)[:, :, 0:VD], ALU.mult, ALU.subtract).then_inc(kv_lo, 1)

                dve.wait_ge(x_in[0], 32)
                dve.wait_ge(ones_ok, 5)
                norm_lo(0, 0)
                xT_lo_out(0, 0, True)

                def step(i, b, first, last):
                    if not last:
                        norm_lo(i + 1, 1 - b)
                    if not first:
                        dve.wait_ge(stored, STORES * i)
                        dve.wait_ge(kt_ok, i)
                    for k in range(5):
                        if k >= 2:
                            dve.wait_ge(rot_add, 5 * i + k - 1)
                        elif not first:
                            dve.wait_ge(rot_add, 5 * i + k - 1)
                        rotary(i, k, b)
                        if k == 2 and not last:
                            xT_lo_out(i + 1, 1 - b, first)
                        if k < 3 and not last:
                            scan_max(i, b, k)
                    dve.wait_ge(rot_add, 5 * i + 5)
                    dve.wait_ge(v_ok, 3 * i + 3)
                    split_lo(i, False)
                row_tiles(dve, step)
                for n in range(3):
                    dve.wait_ge(cache_in, 32 * (n + 1))
                    dve.wait_ge(kt_ok, NTT + n)
                    split_lo(NTT + n, False)

            @block.scalar
            def _(act):
                def norm_hi(i, b):
                    act.wait_ge(x_in[b], x_count(i, b) * 32)
                    if not isinstance(i, int) or i > 0:
                        act.wait_ge(t_ok, i)
                    nc.scalar.activation(NH[:, :].bitcast(bf16), X[b][:, :], ACT.Square, scale=D ** -0.5,
                                         accum_out=ST[:, 0:1]).then_inc(stat_ok, 1)
                    act.wait_ge(rs_ok, i + 1)
                    nc.scalar.activation(NH[:, :], X[b][:, :], ACT.Copy, scale=ST[:, 3:4]).then_inc(hi_ok, 1)

                def xT_hi_out(i, b, early):
                    act.wait_ge(t_ok, i + 1)
                    if not early:
                        act.wait_ge(tile_done, i - 1)
                    nc.scalar.activation(XT[b][0][:, :, :], TH[:, :].rearrange("p (k n) -> p k n", k=KC), ACT.Copy).then_inc(th_out, 1)

                def values(i, k):
                    lo, hi = {1: (C_VA, C_QD), 4: (C_VD, 1920), 5: (1920, PROJ)}[k]
                    act.wait_ge(z_ok, 6 * i + k + 1)
                    if k < 5:
                        act.wait_ge(rot_mul, 5 * i + k + 1)
                    nc.scalar.activation(Z[:, lo:hi], ZP[k % 3][:, lo - 384 * k:hi - 384 * k], ACT.Copy,
                                         scale=col(S_ZI)).then_inc(v_ok, 1)

                def split_hi(i):
                    nc.scalar.activation(KN[:, :, 0:HD], Z[:, C_KD:C_VD].rearrange("p (h d) -> p h d", d=HD),
                                         ACT.Copy, scale=col(S_A))
                    nc.scalar.activation(vtile(VH, i)[:, :, 0:VD], Z[:, C_VD:PROJ].rearrange("p (h e) -> p h e", e=VD),
                                         ACT.Copy, scale=col(S_A)).then_inc(kv_hi, 1)

                def kT_out(i):
                    act.wait_ge(kt_ok, i + 1)
                    nc.scalar.activation(K1[:, :, bass.ds(i * P, P)], KT[:, :].rearrange("p (h n) -> p h n", h=HC),
                                         ACT.Copy).then_inc(kt_out, 1)

                norm_hi(0, 0)
                xT_hi_out(0, 0, True)

                def step(i, b, first, last):
                    if not last:
                        norm_hi(i + 1, 1 - b)
                    if not first:
                        act.wait_ge(stored, STORES * i)
                        act.wait_ge(kv_lo, i)
                    values(i, 1)
                    if not first:
                        kT_out(i - 1)
                    if not last:
                        xT_hi_out(i + 1, 1 - b, first)
                    values(i, 4)
                    values(i, 5)
                    act.wait_ge(rot_add, 5 * i + 5)
                    act.wait_ge(v_ok, 3 * i + 3)
                    if not first:
                        act.wait_ge(kt_ok, i)
                    split_hi(i)
                row_tiles(act, step)
                kT_out(NT)
                for n in range(3):
                    act.wait_ge(cache_in, 32 * (n + 1))
                    act.wait_ge(kv_lo, NTT + n)
                    split_hi(NTT + n)
                    kT_out(NTT + n)

            @block.tensor
            def _(pe):
                def transposes(i):
                    pe.wait_ge(hi_ok, i + 1)
                    pe.wait_ge(th_out, i)
                    for k in range(KC):
                        nc.tensor.transpose(TH[:, k * P:(k + 1) * P], NH[:, k * P:(k + 1) * P], g.ident[:, :])
                    pe.wait_ge(lo_ok, i + 1)
                    pe.wait_ge(tl_out, i)
                    for k in range(KC):
                        last = nc.tensor.transpose(TL[:, k * P:(k + 1) * P], NL[:, k * P:(k + 1) * P], g.ident[:, :])
                    last.then_inc(t_ok, 1)

                def k_transposes(i):
                    pe.wait_ge(kv_lo, i + 1)
                    pe.wait_ge(kt_out, i)
                    for h in range(HC):
                        last = nc.tensor.transpose(KT[:, h * P:(h + 1) * P], KN[:, h, :], g.ident[:, :])
                    last.then_inc(kt_ok, 1)

                def product(i, b, k, first):
                    if k >= 3:
                        pe.wait_ge(rot_mul, 5 * i + k - 2)
                        pe.wait_ge(v_ok, 3 * i + V_COUNT[k - 3])
                    elif not first:
                        pe.wait_ge(rot_mul, 5 * i - 5 + min(k + 3, 4) + 1)
                        pe.wait_ge(v_ok, 3 * i - 3 + V_COUNT[k + 3])
                    out = ZP[k % 3][:, 0:384]
                    c = slice(384 * k, 384 * (k + 1))
                    for kc in range(KC):
                        xh, xl = XT[b][0][:, kc, :], XT[b][1][:, kc, :]
                        nc.tensor.matmul(out, xh, WH[:, kc, c], start=kc == 0, stop=False)
                        nc.tensor.matmul(out, xh, WL[:, kc, c], start=False, stop=False)
                        last = nc.tensor.matmul(out, xl, WH[:, kc, c], start=False, stop=kc == KC - 1)
                    last.then_inc(z_ok, 1)

                transposes(0)

                def step(i, b, first, last):
                    pe.wait_ge(th_out, i + 1)
                    pe.wait_ge(tl_out, i + 1)
                    for k in range(3):
                        product(i, b, k, first)
                    if not first:
                        k_transposes(i - 1)
                    if not last:
                        transposes(i + 1)
                    for k in range(3, 6):
                        product(i, b, k, first)
                    pe.wait_ge(z_ok, 6 * i + 6)
                    pe.sem_inc(tile_done, 1)
                row_tiles(pe, step)
                for n in range(4):
                    k_transposes(NT + n)


def x_count(i, b):
    return (i - b) // 2 + 1 if isinstance(i, int) else (i - b + 2) // 2


def scan_count(i, b, w):
    before = {0: {0: 1, 1: 1, 2: 2}, 1: {0: 2, 1: 3, 2: 3}}[b][w]
    return ((i - b) // 2) * 3 + before


def row_tiles(eng, body):
    body(0, 0, True, False)
    with eng.Fori(1, NT - 1, 2) as i:
        body(i, 1, False, False)
        body(i + 1, 0, False, False)
    body(NT - 1, 1, False, False)
    body(NT, 0, False, True)


def phase_window(g):
    nc, dram = g.nc, g.dram
    with ExitStack() as ctx:
        NW = NT + 4
        W_S, W_CW, W_CM = NT + 1, NT + 2, NT + 3
        SVW = HD + 1
        QF = [g.sb(f"wq_rows{n}", [P, HS * HD], f32, ctx) for n in range(2)]
        KR = g.sb("wkv_rows", [P, NW, 2 * KVS * HD], f32, ctx)
        KN = g.sb("wk_split", [P, NW, KVS, P], f16, ctx)
        SVH, SVL = (g.sb(n, [P, NW * KVS * SVW], f16, ctx) for n in ("wv_hi", "wv_lo"))
        SK = g.sb("wkT_hi_lo", [P, KVS, NW * P], f16, ctx)
        SK2 = g.sb("wkT_hi_max", [HD + 2, KVS, NW * P], f16, ctx)
        QH = g.sb("wq_hi_hi", [P, HS, P], f16, ctx)
        QL = g.sb("wq_lo_max", [P, HS, HD + 2], f16, ctx)
        Q1 = [g.sb(f"wqT_hi_hi{n}", [P, HS, P], f16, ctx) for n in range(2)]
        Q2 = [g.sb(f"wqT_lo_max{n}", [HD + 2, HS, P], f16, ctx) for n in range(2)]
        PF = [g.sb(f"wp{n}", [P, GRP, P], f32, ctx) for n in range(6)]
        PH = [g.sb(f"wp_hi{n}", [P, GRP, P], f16, ctx) for n in range(6)]
        PL = [g.sb(f"wp_lo{n}", [P, GRP, P], f16, ctx) for n in range(6)]
        SINK = g.sb("sinks", [P, HS], f32, ctx)
        MX = g.sb("wrow_max", [P, HS], f32, ctx)
        MU = g.sb("wrow_max_used", [P, 3, HS], f32, ctx)
        SX = [g.sb(f"wsink_exps{n}", [P, 2, HS], f32, ctx) for n in range(2)]
        DN = g.sb("wden", [P, 4, GRP], f32, ctx)
        AO = [g.sb(f"wout{n}", [P, HS * HD], f32, ctx) for n in range(2)]
        TQ = g.ps("wqT_ps", [P, HS * P], f16, ctx)
        MP = [g.ps(f"wmax_ps{n}", [P, 512], f32, ctx) for n in range(2)]
        SP = [g.ps(f"ws_ps{n}", [P, 512], f32, ctx) for n in range(3)]
        OP = [g.ps(f"wo_ps{n}", [P, 512], f32, ctx) for n in range(2)]
        SC = g.SC
        col = lambda c: SC[:, c:c + 1]
        s = lambda n: g.sem("w_" + n)
        q_in = [s("q_in0"), s("q_in1")]
        zero_ok, kv_in, kv_hi, kv_lo, kt_ok, kt_out, pad_ok, k2_ok = (
            s(n) for n in ("zero", "kv_in", "kv_hi", "kv_lo", "kt", "kt_out", "pad", "k2"))
        qh_ok, ql_ok, t1_ok, t2_ok, q1_out, q2_out = (s(n) for n in ("qh", "ql", "q1T", "q2T", "q1_out", "q2_out"))
        mx_ok, red_ok, m_ok, m_step, sx_ok, ex_ok = (s(n) for n in ("max_ps", "reduced", "max", "max_step", "sx", "ex"))
        s_ok, e_ok, pl_ok, av_ok, o_out, n_step = (
            s(n) for n in ("scores", "exp", "p_lo", "av", "o_out", "norm_step"))
        stored = [s("stored0"), s("stored1")]
        vt = lambda V, t, j: V[:, bass.ds((t * KVS + j) * SVW, SVW)]
        v4 = lambda V: V[:, :].rearrange("p (t j e) -> p t j e", t=NW, j=KVS)

        def key_tiles(i):
            if isinstance(i, int) and i == TS:
                return W_S, W_CW, W_CM
            return i + 1, i, W_S

        def unit_tile(i, u):
            own, before, meta = key_tiles(i)
            return (meta, before, own)[u % 3]

        with nc.Block() as block:
            @block.sync
            def _(sp):
                sp.dma_start(KR[:, 1:NT + 2, :], g.scr[:, C_KA:C_QD].rearrange("(t p) c -> p t c", p=P)).then_inc(kv_in, 16)
                sp.dma_start(SINK[:, :], dram["attn_sinks"].broadcast_to([P, HS])).then_inc(kv_in, 16)
                sp.wait_ge(zero_ok, 1)
                for c, name in ((0, "cache_swa_k"), (KVS * HD, "cache_swa_v")):
                    old = dram[name].rearrange("a b r h d -> (a b r) (h d)")
                    sp.dma_start(KR[:, W_CW, c:c + KVS * HD], old[META:META + WIN, :]).then_inc(kv_in, 16)
                    sp.dma_start(KR[DEC:DEC + META, W_CM, c:c + KVS * HD], old[0:META, :]).then_inc(kv_in, 16)

                def load(i, b):
                    row = i * P if isinstance(i, int) else sp.snap(i * P)
                    if not isinstance(i, int) or i > 1:
                        sp.wait_ge(ql_ok, i - 1)
                    sp.dma_start(QF[b][:, :], g.scr[bass.ds(row, P), 0:C_KA]).then_inc(q_in[b], 16)

                load(0, 0)

                def store(i, b):
                    row = i * P if isinstance(i, int) else sp.snap(i * P)
                    sp.wait_ge(o_out, 2 * i + 2)
                    sp.dma_start(g.mix[bass.ds(row, P), 0:HS * HD], AO[b][:, :]).then_inc(stored[b], 16)

                def step(i, b, first, last):
                    if not last:
                        load(i + 1, 1 - b)
                    if not first:
                        store(i - 1, 1 - b)
                row_tiles(sp, step)
                store(NT, 0)
                sp.wait_ge(stored[0], 16 * (NT // 2 + 1))
                sp.wait_ge(stored[1], 16 * (NT // 2))

            @block.gpsimd
            def _(pool):
                link = Chain(pool, zero_ok)
                link(nc.gpsimd.memset(KR[:, W_CM, :], 0.0))
                link(nc.gpsimd.memset(v4(SVH)[:, :, :, HD:SVW], 1.0))
                link(nc.gpsimd.memset(v4(SVL)[:, :, :, HD:SVW], 0.0))
                link(nc.gpsimd.memset(SK2[HD:HD + 2, :, :], MROW))
                link(nc.gpsimd.memset(KR[:, 0, :], 0.0))
                for n in range(6):
                    for buf in (PF, PH, PL):
                        link(nc.gpsimd.memset(buf[n][:, :, :], 0.0))

            @block.vector
            def _(dve):
                dve.wait_ge(kv_hi, 1)
                for j in range(KVS):
                    nc.vector.scalar_tensor_tensor(KN[:, :, j, HD:P], KR[:, :, j * HD:(j + 1) * HD], col(S_A),
                                                   KN[:, :, j, 0:HD], ALU.mult, ALU.subtract)
                    c = (KVS + j) * HD
                    last = nc.vector.scalar_tensor_tensor(v4(SVL)[:, :, j, 0:HD], KR[:, :, c:c + HD], col(S_A),
                                                          v4(SVH)[:, :, j, 0:HD], ALU.mult, ALU.subtract)
                last.then_inc(kv_lo, 1)
                dve.wait_ge(kt_out, KVS * 3)
                nc.vector.tensor_copy(SK[:, :, HD:P], SK[:, :, P:P + HD]).then_inc(pad_ok, 1)
                nc.vector.memset(v4(SVH)[:, 0, :, HD:SVW], 0.0).then_inc(pad_ok, 1)
                dve.wait_ge(pad_ok, 2)
                nc.vector.tensor_copy(SK2[0:HD, :, :], SK[0:HD, :, :]).then_inc(k2_ok, 1)

                def q_lo(i, b):
                    dve.wait_ge(qh_ok, i + 1)
                    if not isinstance(i, int) or i > 0:
                        dve.wait_ge(t2_ok, i)
                    nc.vector.scalar_tensor_tensor(QL[:, :, 0:HD], QF[b][:, :].rearrange("p (h d) -> p h d", h=HS),
                                                   col(S_A), QH[:, :, 0:HD], ALU.mult, ALU.subtract).then_inc(ql_ok, 1)

                def reduce_pair(i, r):
                    dve.wait_ge(mx_ok, 4 * i + r + 1)
                    v = MP[r % 2][:, 0:416].rearrange("p (h n) -> p h n", h=2)
                    nc.vector.tensor_reduce(MX[0:HD, 2 * r:2 * r + 2], v[0:HD, :, 0:144], AX.X, ALU.max)
                    nc.vector.tensor_reduce(MX[HD:P, 2 * r:2 * r + 2], v[HD:P, :, 64:208], AX.X, ALU.max).then_inc(red_ok, 1)

                def maxima(i, b):
                    dve.wait_ge(red_ok, 4 * i + 4)
                    nc.vector.tensor_scalar(QL[:, :, HD:HD + 1], MX[:, :].unsqueeze(2), -1.0 / MROW, None, ALU.mult).then_inc(m_step, 1)
                    dve.wait_ge(m_step, 3 * i + 1)
                    nc.vector.scalar_tensor_tensor(QL[:, :, HD + 1:HD + 2], MX[:, :].unsqueeze(2), -1.0 / MROW,
                                                   QL[:, :, HD:HD + 1], ALU.mult, ALU.subtract).then_inc(m_ok, 1)
                    dve.wait_ge(m_ok, i + 1)
                    nc.vector.tensor_tensor(MU[:, 0, :].unsqueeze(2), QL[:, :, HD:HD + 1], QL[:, :, HD + 1:HD + 2], ALU.add).then_inc(m_step, 1)
                    dve.wait_ge(m_step, 3 * i + 2)
                    nc.vector.tensor_scalar(MU[:, 1, :], MU[:, 0, :], col(S_NAI), -1.0, ALU.mult, ALU.mult).then_inc(m_step, 1)
                    dve.wait_ge(m_step, 3 * i + 3)
                    nc.vector.tensor_tensor(MU[:, 2, :], MU[:, 1, :], SINK[:, :], ALU.max).then_inc(n_step, 1)

                def sink_args(i, b):
                    if not isinstance(i, int) or i > 1:
                        dve.wait_ge(o_out, 2 * i - 2)
                    nc.vector.tensor_tensor(SX[b][:, 0, :], MU[:, 1, :], MU[:, 2, :], ALU.subtract)
                    nc.vector.tensor_tensor(SX[b][:, 1, :], SINK[:, :], MU[:, 2, :], ALU.subtract).then_inc(sx_ok, 1)

                def p_lo(i, u):
                    v = slice(0, HD) if u % 3 == 1 else slice(0, P)
                    dve.wait_ge(e_ok, 6 * i + u + 1)
                    nc.vector.tensor_tensor(PL[u][:, :, v], PF[u][:, :, v], PH[u][:, :, v], ALU.subtract).then_inc(pl_ok, 1)

                def normalise(i, b, j, first):
                    n0 = 6 * i + 3 * j
                    dve.wait_ge(av_ok, n0 + 3)
                    dve.wait_ge(ex_ok, i + 1)
                    if not first:
                        dve.wait_ge(stored[b], 16 * ((i - b) // 2))
                    h = slice(GRP * j, GRP * j + GRP)
                    O = OP[j][:, 0:GRP * SVW].rearrange("p (h e) -> p h e", h=GRP)
                    steps = 3 * (2 * i + j)
                    nc.vector.tensor_tensor(DN[:, 0, :].unsqueeze(2), O[:, :, HD:SVW], SX[b][:, 0, h].unsqueeze(2), ALU.mult).then_inc(d_step, 1)
                    dve.wait_ge(d_step, steps + 1)
                    nc.vector.tensor_tensor(DN[:, 1, :], DN[:, 0, :], SX[b][:, 1, h], ALU.add).then_inc(d_step, 1)
                    dve.wait_ge(d_step, steps + 2)
                    nc.vector.reciprocal(DN[:, 2, :], DN[:, 1, :]).then_inc(d_step, 1)
                    dve.wait_ge(d_step, steps + 3)
                    nc.vector.scalar_tensor_tensor(DN[:, 3, :], DN[:, 2, :], col(S_AI), SX[b][:, 0, h], ALU.mult, ALU.mult).then_inc(f_step, 1)
                    dve.wait_ge(f_step, 2 * i + j + 1)
                    nc.vector.tensor_tensor(AO[b][:, GRP * j * HD:GRP * (j + 1) * HD].rearrange("p (h d) -> p h d", h=GRP),
                                            O[:, :, 0:HD], DN[:, 3, :].unsqueeze(2).broadcast_to([P, GRP, HD]),
                                            ALU.mult).then_inc(o_out, 1)

                d_step, f_step = s("den_step"), s("factor_step")
                q_lo(0, 0)
                for n in range(4):
                    reduce_pair(0, n)
                maxima(0, 0)
                dve.wait_ge(n_step, 1)
                sink_args(0, 0)
                p_lo(0, 0)
                p_lo(0, 1)

                def step(i, b, first, last):
                    if not last:
                        q_lo(i + 1, 1 - b)
                    p_lo(i, 2)
                    if not first:
                        normalise(i - 1, 1 - b, 1, isinstance(i, int) and i < 3)
                    if not last:
                        reduce_pair(i + 1, 0)
                        reduce_pair(i + 1, 1)
                    p_lo(i, 3)
                    if not last:
                        reduce_pair(i + 1, 2)
                        reduce_pair(i + 1, 3)
                    p_lo(i, 4)
                    if not last:
                        maxima(i + 1, 1 - b)
                    normalise(i, b, 0, isinstance(i, int) and i < 2)
                    p_lo(i, 5)
                    if not last:
                        dve.wait_ge(n_step, i + 2)
                        sink_args(i + 1, 1 - b)
                    if not last:
                        p_lo(i + 1, 0)
                        p_lo(i + 1, 1)
                row_tiles(dve, step)
                normalise(NT, 0, 1, False)

            @block.scalar
            def _(act):
                act.wait_ge(kv_in, 16 * 6)
                act.wait_ge(zero_ok, 23)
                for j in range(KVS):
                    nc.scalar.activation(KN[:, :, j, 0:HD], KR[:, :, j * HD:(j + 1) * HD], ACT.Copy, scale=col(S_A))
                    c = (KVS + j) * HD
                    last = nc.scalar.activation(v4(SVH)[:, :, j, 0:HD], KR[:, :, c:c + HD], ACT.Copy, scale=col(S_A))
                last.then_inc(kv_hi, 1)
                for j in range(KVS):
                    for n, (a, b) in enumerate(((0, 8), (8, 16), (16, NW))):
                        act.wait_ge(kt_ok, 3 * j + n + 1)
                        nc.scalar.activation(SK[:, j, a * P:b * P], TQ[:, 0:(b - a) * P], ACT.Copy).then_inc(kt_out, 1)

                def q_hi(i, b):
                    act.wait_ge(q_in[b], x_count(i, b) * 16)
                    if not isinstance(i, int) or i > 0:
                        act.wait_ge(t1_ok, i)
                        act.wait_ge(ql_ok, i)
                    nc.scalar.activation(QH[:, :, :].rearrange("p h (r d) -> p h r d", r=2),
                                         QF[b][:, :].rearrange("p (h d) -> p h d", h=HS).unsqueeze(2).broadcast_to([P, HS, 2, HD]),
                                         ACT.Copy, scale=col(S_A)).then_inc(qh_ok, 1)

                def q1T_out(i, b):
                    act.wait_ge(t1_ok, i + 1)
                    nc.scalar.activation(Q1[b][:, :, :], TQ[:, :].rearrange("p (h n) -> p h n", h=HS), ACT.Copy).then_inc(q1_out, 1)

                def q2T_out(i, b):
                    act.wait_ge(t2_ok, i + 1)
                    nc.scalar.activation(Q2[b][:, :, :], TQ[0:HD + 2, :].rearrange("p (h n) -> p h n", h=HS), ACT.Copy).then_inc(q2_out, 1)

                def sink_exps(i, b):
                    act.wait_ge(sx_ok, i + 1)
                    nc.scalar.activation(SX[b][:, :, :], SX[b][:, :, :], ACT.Exp).then_inc(ex_ok, 1)

                def exps(i, u, first):
                    S = SP[u % 3][:, :].rearrange("p (h n) -> p h n", h=GRP)
                    act.wait_ge(s_ok, 6 * i + u + 1)
                    if not first:
                        act.wait_ge(av_ok, 6 * i + u - 5)
                    parts = {0: ((slice(HD, HD + META), slice(0, P)),),
                             1: ((slice(HD, P), slice(0, HD)),),
                             2: ((slice(0, HD), slice(0, P)), (slice(HD, P), slice(HD, P)))}[u % 3]
                    for rows, q in parts:
                        nc.scalar.activation(PH[u][rows, :, q], S[rows, :, q], ACT.Exp, scale=SC[rows, S_SC:S_SC + 1])
                        last = nc.scalar.activation(PF[u][rows, :, q], S[rows, :, q], ACT.Exp, scale=SC[rows, S_SC:S_SC + 1])
                    last.then_inc(e_ok, 1)

                q_hi(0, 0)
                q1T_out(0, 0)
                q2T_out(0, 0)
                sink_exps(0, 0)
                exps(0, 0, True)
                exps(0, 1, True)

                def step(i, b, first, last):
                    if not last:
                        q_hi(i + 1, 1 - b)
                    exps(i, 2, first)
                    if not last:
                        q1T_out(i + 1, 1 - b)
                    exps(i, 3, first)
                    exps(i, 4, first)
                    exps(i, 5, first)
                    if not last:
                        q2T_out(i + 1, 1 - b)
                        sink_exps(i + 1, 1 - b)
                        exps(i + 1, 0, False)
                        exps(i + 1, 1, False)
                row_tiles(act, step)

            @block.tensor
            def _(pe):
                pe.wait_ge(kv_lo, 1)
                for j in range(KVS):
                    for n, (a, b) in enumerate(((0, 8), (8, 16), (16, NW))):
                        if n + j:
                            pe.wait_ge(kt_out, 3 * j + n)
                        for t in range(a, b):
                            last = nc.tensor.transpose(TQ[:, (t - a) * P:(t - a + 1) * P], KN[:, t, j, :], g.ident[:, :])
                        last.then_inc(kt_ok, 1)
                pe.wait_ge(kt_out, 6)

                def q1T(i):
                    pe.wait_ge(qh_ok, i + 1)
                    if not isinstance(i, int) or i > 0:
                        pe.wait_ge(q2_out, i)
                    for h in range(HS):
                        last = nc.tensor.transpose(TQ[:, h * P:(h + 1) * P], QH[:, h, :], g.ident[:, :])
                    last.then_inc(t1_ok, 1)

                def q2T(i):
                    pe.wait_ge(m_ok, i + 1)
                    pe.wait_ge(q1_out, i + 1)
                    for h in range(HS):
                        last = nc.tensor.transpose(TQ[0:HD + 2, h * P:(h + 1) * P], QL[:, h, :], g.ident[:, :])
                    last.then_inc(t2_ok, 1)

                def row_max(i, b, rounds=range(4)):
                    own, before, meta = key_tiles(i)
                    if 0 in rounds:
                        pe.wait_ge(q1_out, i + 1)
                    for r in rounds:
                        if not (isinstance(i, int) and i == 0 and r == 0):
                            pe.wait_ge(red_ok, 4 * i + r - 1)
                        for n in range(2):
                            h, o = 2 * r + n, 208 * n
                            k = SK[:, h // GRP, :]
                            for a, w, c in ((0, HD, before * P + HD), (HD, META, meta * P + HD), (HD + META, P, own * P)):
                                last = nc.tensor.matmul(MP[r % 2][:, o + a:o + a + w], Q1[b][:, h, :], k[:, bass.ds(c, w)],
                                                        start=True, stop=True)
                        last.then_inc(mx_ok, 1)

                def scores(i, b, u, first):
                    j = u // 3
                    if not first:
                        pe.wait_ge(e_ok, 6 * i + u - 2)
                    if u == 0:
                        pe.wait_ge(q2_out, i + 1)
                    t = unit_tile(i, u)
                    h = slice(GRP * j, GRP * j + GRP)
                    nc.tensor.matmul(SP[u % 3][:, :], SK[:, j, bass.ds(t * P, P)], Q1[b][:, h, :], start=True, stop=False)
                    nc.tensor.matmul(SP[u % 3][:, :], SK2[:, j, bass.ds(t * P, P)], Q2[b][:, h, :],
                                     start=False, stop=True).then_inc(s_ok, 1)

                def values(i, u, first):
                    j = u // 3
                    pe.wait_ge(pl_ok, 6 * i + u + 1)
                    if u % 3 == 0 and not first:
                        pe.wait_ge(o_out, 2 * i + j - 1)
                    t = unit_tile(i, u)
                    for h in range(GRP):
                        out = OP[j][:, h * SVW:(h + 1) * SVW]
                        lead = u % 3 == 0 and h == 0
                        nc.tensor.matmul(out, PH[u][:, h, :], vt(SVH, t, j), start=lead, stop=False, skip_group_check=True)
                        nc.tensor.matmul(out, PH[u][:, h, :], vt(SVL, t, j), start=False, stop=False, skip_group_check=True)
                        last = nc.tensor.matmul(out, PL[u][:, h, :], vt(SVH, t, j), start=False, stop=u % 3 == 2,
                                                skip_group_check=True)
                    last.then_inc(av_ok, 1)

                q1T(0)
                pe.wait_ge(k2_ok, 1)
                row_max(0, 0)
                q2T(0)
                scores(0, 0, 0, True)
                scores(0, 0, 1, True)

                def step(i, b, first, last):
                    for u in range(6):
                        if u < 4:
                            scores(i, b, u + 2, first and u + 2 < 3)
                        if not last:
                            if u == 5:
                                q2T(i + 1)
                                scores(i + 1, 1 - b, 0, False)
                            if u == 0:
                                q1T(i + 1)
                            if u == 2:
                                row_max(i + 1, 1 - b, (0, 1))
                            if u == 3:
                                row_max(i + 1, 1 - b, (2, 3))
                        values(i, u, first)
                    if not last:
                        scores(i + 1, 1 - b, 1, False)
                row_tiles(pe, step)


HI_FROM, HI_EVERY = (1, 1, 1, 1, 1), (3, 3, 3, 2, 2)
POOL_EVERY = 3


class Stage:

    def __init__(self, n, unit_base, piece_base, store_base, dve_base, pool_base, hi_base):
        self.n, self.unit_base, self.piece_base, self.store_base = n, unit_base, piece_base, store_base
        self.dve_base, self.pool_base, self.hi_base = dve_base, pool_base, hi_base
        rows, every = slice(0, P), slice(0, 4 * P)
        if n < NT // 4:
            t0 = 4 * n
            self.tile0, self.nq = t0, 4
            self.units = [(TS, "meta", 0, ((slice(DEC, DEC + META), every),))]
            self.units += [(t, f"full{t % 4}", 0, ((rows, every),)) for t in range(t0)]
            self.units += [(t0 + j, f"diag{j}", j, ((slice(0, CH), slice(0, (4 - j) * P)),
                                                    (slice(CH, P), slice(CH, (4 - j) * P)))) for j in range(4)]
            self.pieces = []
            for q in range(4):
                keys = (t0 + q + 1) * P
                k = -(-(keys + META) // 512)
                others = min(512 * (k - 1), keys - P)
                at = 0
                for m in range(k - 1):
                    w = min(512, others - at)
                    self.pieces.append((q, m, [(at, w)], w, w))
                    at += w
                self.pieces.append((q, k - 1, [(TS * P + DEC, META), (at, keys - at)], META + keys - at - CH,
                                    META + keys - at))
            self.slots = [1 + max(p[1] for p in self.pieces if p[0] == q) for q in range(4)]
        else:
            self.tile0, self.nq = TS, 1
            c = slice(0, P)
            self.units = [(NT + 1, "full0", 0, ((rows, c),)), (NT + 2, "full1", 0, ((rows, c),)),
                          (NT + 3, "cached", 0, ((slice(0, META), c),)), (TS, "new", 0, ((slice(0, DEC), c),))]
            self.pieces = [(0, 0, [((NT + 1) * P, PAST + META), (TS * P, DEC)], PAST + META + DEC, PAST + META + DEC)]
            self.slots = [1]
        self.U, self.NP = len(self.units), len(self.pieces)
        self.pool_lo = list(range(2, self.U - 4, POOL_EVERY))
        self.dve_lo = [u for u in range(self.U) if u not in self.pool_lo]
        self.dve_hi = list(range(HI_FROM[n], self.U - 4, HI_EVERY[n]))

    def lo_count(self, h, c, u):
        by_pool = u in self.pool_lo
        mine, base = (self.pool_lo, self.pool_base) if by_pool else (self.dve_lo, self.dve_base)
        return by_pool, base + h * (2 * len(mine)) + (c * len(mine) + mine.index(u) + 1)

    def hi_count(self, h, c, u):
        n = len(self.dve_hi)
        return self.hi_base + h * (2 * n) + (c * n + self.dve_hi.index(u) + 1)

    def cols(self, u):
        return (self.nq - self.units[u][2]) * P


def phase_differential(g, K1, VH, VL):
    nc, dram = g.nc, g.dram
    stages, ub, pb, sb_, db, gb, hb = [], 1, 1, 0, 1, 0, 0
    for n in range(NT // 4 + 1):
        st = Stage(n, ub, pb, sb_, db, gb, hb)
        stages.append(st)
        ub, pb, sb_ = ub + HC * st.U, pb + HC * st.NP, sb_ + HDIF
        db, gb, hb = db + HC * len(st.dve_lo), gb + HC * len(st.pool_lo), hb + HC * len(st.dve_hi)
    with ExitStack() as ctx:
        K2 = g.sb("kT_hi_max", [HD + 2, HC, NKT * P], f16, ctx)
        QF = g.sb("dq_rows", [P, 4, HC * HD], f32, ctx)
        QH = [g.sb(f"dq_hi_hi{n}", [P, HC, P], f16, ctx) for n in range(2)]
        QL = g.sb("dq_lo_max", [P, 4, HC, HD + 2], f16, ctx)
        Q1 = [g.sb(f"dqT_hi_hi{n}", [P, HC, 4 * P], f16, ctx) for n in range(2)]
        Q2 = g.sb("dqT_lo_max", [HD + 2, HC, 4 * P], f16, ctx)
        widths = {"meta": 4 * P, "cached": P, "new": P}
        widths |= {f"full{n}": 4 * P for n in range(4)} | {f"diag{j}": (4 - j) * P for j in range(4)}
        PF = {n: g.sb(f"dp_{n}", [P, w], f32, ctx) for n, w in widths.items()}
        PH = {n: g.sb(f"dp_hi_{n}", [P, w], f16, ctx) for n, w in widths.items()}
        PL = {n: g.sb(f"dp_lo_{n}", [P, w], f16, ctx) for n, w in widths.items()}
        MP_ = g.sb("drow_max_parts", [P, 4, HC, 5], f32, ctx)
        MX = g.sb("drow_max", [P, 4, HC], f32, ctx)
        RD = g.sb("dden", [P, 3, 4], f32, ctx)
        O1 = g.sb("dfirst", [P, 4, VD], f32, ctx)
        OD = [g.sb(f"ddiff{n}", [P, 4, VD], f32, ctx) for n in range(2)]
        SQ = g.sb("dsquares", [P, VD], bf16, ctx)
        RS = g.sb("dstats", [P, 4, 4], f32, ctx)
        CO = g.sb("dconsts", [P, 3, 4], f32, ctx)
        TQ = g.ps("dqT_ps", [P, HC * P], f16, ctx)
        MB = [g.ps("dmax_ps", [P, 512], f32, ctx), TQ[:, :].bitcast(f32)]
        SP = [g.ps(f"ds_ps{n}", [P, 512], f32, ctx) for n in range(2)]
        OP = [[g.ps(f"do_ps{c}{n}", [P, 512], f32, ctx) for n in range(2)] for c in range(2)]
        SC = g.SC
        col = lambda c: SC[:, c:c + 1]
        s = lambda n: g.sem("d_" + n)
        (q_in, zero_ok, k2_ok, qh_ok, ql_ok, t1_ok, t2_ok, q1_out, q2_out, mx_ok, red_ok, m_ok, m_step, s_ok,
         e_ok, pl_ok, av_ok, r_step, o_out, od_ok, sq_ok, rs_step, f_ok, const_ok) = (s(n) for n in (
             "q_in", "zero", "k2", "qh", "ql", "q1T", "q2T", "q1_out", "q2_out", "max_ps", "reduced", "max",
             "max_step", "scores", "exp", "p_lo", "av", "recip_step", "o_out", "diff", "squares", "stat_step", "normed",
             "consts"))
        stored = [s("stored0"), s("stored1")]
        pool_lo_ok, hi_step = s("pool_p_lo"), s("p_hi_by_dve")
        vt = lambda V, t, h: V[:, bass.ds((t * HDIF + h) * VW, VW)]
        kt = lambda K, h, c, t: K[:, :, :].rearrange("p h n -> p (h n)")[:, bass.ds((2 * h + c) * NKT * P + t * P, P)]
        q0 = [0, 4, 8, 12, 16, 17]

        def heads(eng, body):
            with eng.Fori(0, HDIF) as h:
                body(h)

        with nc.Block() as block:
            @block.sync
            def _(sp):
                def load(st):
                    if st.n > 0:
                        sp.wait_ge(ql_ok, q0[st.n])
                    r = st.tile0 * P
                    sp.dma_start(QF[:, 0:st.nq, :], g.scr[r:r + st.nq * P, C_QD:C_KD].rearrange("(q p) c -> p q c", p=P))\
                        .then_inc(q_in, 16)
                for x in range(2):
                    sp.sem_inc(stored[x], 16)
                load(stages[0])
                for st in stages:
                    if st.n + 1 < len(stages):
                        load(stages[st.n + 1])
                    with sp.Fori(0, HDIF // 2) as pair:
                        hh = pair * 2
                        for x in range(2):
                            c = sp.snap(HS * HD + (hh + x) * VD)
                            sp.wait_ge(f_ok, st.store_base + hh + x + 1)
                            r = st.tile0 * P
                            sp.dma_start(g.mix[r:r + st.nq * P, bass.ds(c, VD)].rearrange("(q p) c -> p q c", p=P),
                                         OD[x][:, 0:st.nq, :]).then_inc(stored[x], 16)
                for x in range(2):
                    sp.wait_ge(stored[x], 16 * (2 * len(stages) + 1))

            @block.gpsimd
            def _(pool):
                link = Chain(pool, zero_ok)
                link(nc.gpsimd.memset(K2[HD:HD + 2, :, :], MROW))
                for name in widths:
                    if name[:4] != "full":
                        for buf in (PF, PH, PL):
                            link(nc.gpsimd.memset(buf[name][:, :], 0.0))
                link(nc.gpsimd.memset(CO[:, 1, :], EPS))
                link(nc.gpsimd.memset(CO[:, 2, :], -0.5))
                pool.wait_ge(const_ok, 2)

                def pool_lo(st, h, c, u):
                    b = st.units[u][1]
                    w = st.cols(u)
                    if u in st.dve_hi:
                        pool.wait_ge(hi_step, st.hi_count(h, c, u))
                    else:
                        pool.wait_ge(e_ok, st.unit_base + h * (2 * st.U) + (c * st.U + u + 1))
                    nc.gpsimd.tensor_tensor(PL[b][:, 0:w], PF[b][:, 0:w], PH[b][:, 0:w], ALU.subtract).then_inc(pool_lo_ok, 1)

                def finish(st, h, x):
                    n = st.store_base + h + x
                    nq = slice(0, st.nq)
                    pool.wait_ge(sq_ok, n + 1)
                    nc.gpsimd.tensor_tensor(RS[:, 1, nq], RS[:, 0, nq], CO[:, 0, nq], ALU.mult).then_inc(rs_step, 1)
                    pool.wait_ge(rs_step, 4 * n + 2)
                    nc.gpsimd.tensor_tensor(RS[:, 2, nq], RS[:, 1, nq], CO[:, 1, nq], ALU.add).then_inc(rs_step, 1)
                    pool.wait_ge(rs_step, 4 * n + 3)
                    nc.gpsimd.tensor_tensor(RS[:, 3, nq], RS[:, 2, nq], CO[:, 2, nq], ALU.pow).then_inc(rs_step, 1)
                    pool.wait_ge(rs_step, 4 * n + 4)
                    nc.gpsimd.tensor_tensor(RS[:, 2, nq], RS[:, 3, nq], g.AI4[:, nq], ALU.mult).then_inc(rs_step, 1)
                    pool.wait_ge(rs_step, 4 * n + 5)
                    nc.gpsimd.tensor_tensor(OD[x][:, nq, :], OD[x][:, nq, :],
                                            RS[:, 2, nq].unsqueeze(2).broadcast_to([P, st.nq, VD]), ALU.mult).then_inc(f_ok, 1)

                pool.sem_inc(rs_step, 1)
                for st in stages:
                    with pool.Fori(0, HDIF // 2) as pair:
                        hh = pair * 2
                        for x in range(2):
                            for c in range(2):
                                for u in range(st.U):
                                    if u in st.pool_lo:
                                        pool_lo(st, hh + x, c, u)
                                    if x and not c and u == min(SQUARE_LAG + 1, st.U - 1):
                                        finish(st, hh, 0)
                        finish(st, hh, 1)

            @block.vector
            def _(dve):
                dve.wait_ge(zero_ok, 1)
                nc.vector.tensor_copy(K2[0:HD, :, :], K1[0:HD, :, :]).then_inc(k2_ok, 1)
                for q in range(4):
                    nc.vector.tensor_copy(g.AI4[:, q:q + 1], col(S_AI))
                nc.vector.memset(RS[:, :, :], 1.0).then_inc(const_ok, 1)
                dve.wait_ge(const_ok, 1)
                nc.vector.tensor_scalar(CO[:, 0, :], g.AI4[:, :], col(S_AI), 1.0 / VD, ALU.mult, ALU.mult).then_inc(const_ok, 1)

                def q_lo(st):
                    for q in range(st.nq):
                        n = q0[st.n] + q
                        dve.wait_ge(qh_ok, n + 1)
                        if q == 0 and st.n:
                            dve.wait_ge(t2_ok, q0[st.n])
                        nc.vector.scalar_tensor_tensor(QL[:, q, :, 0:HD], QF[:, q, :].rearrange("p (h d) -> p h d", h=HC),
                                                       col(S_A), QH[n % 2][:, :, 0:HD], ALU.mult, ALU.subtract).then_inc(ql_ok, 1)

                def reduce_piece(st, h, c, p):
                    q, slot, _, wa, wb = st.pieces[p]
                    B = MB[(c * st.NP + p) % 2]
                    dve.wait_ge(mx_ok, st.piece_base + h * (2 * st.NP) + (c * st.NP + p + 1))
                    out = MP_[:, :, :, :].rearrange("p q h s -> p (q h s)")
                    at = lambda: bass.ds((q * HC + 2 * h + c) * 5 + slot, 1)
                    if wa == wb:
                        last = nc.vector.tensor_reduce(out[:, at()], B[:, 0:wa], AX.X, ALU.max)
                    else:
                        nc.vector.tensor_reduce(out[0:CH, at()], B[0:CH, 0:wa], AX.X, ALU.max)
                        last = nc.vector.tensor_reduce(out[CH:P, at()], B[CH:P, 0:wb], AX.X, ALU.max)
                    last.then_inc(red_ok, 1)

                def maxima(st):
                    nq = slice(0, st.nq)
                    dve.wait_ge(red_ok, st.piece_base + HC * st.NP)
                    for q in range(st.nq):
                        last = nc.vector.tensor_reduce(MX[:, q, :], MP_[:, q, :, 0:st.slots[q]], AX.X, ALU.max)
                    last.then_inc(m_step, 1)
                    dve.wait_ge(m_step, 2 * st.n + 1)
                    nc.vector.tensor_scalar(QL[:, nq, :, HD:HD + 1], MX[:, nq, :].unsqueeze(3), -1.0 / MROW, None, ALU.mult).then_inc(m_step, 1)
                    dve.wait_ge(m_step, 2 * st.n + 2)
                    for q in range(st.nq):
                        last = nc.vector.scalar_tensor_tensor(QL[:, q, :, HD + 1:HD + 2], MX[:, q, :].unsqueeze(2), -1.0 / MROW,
                                                              QL[:, q, :, HD:HD + 1], ALU.mult, ALU.subtract)
                    last.then_inc(m_ok, 1)

                def p_lo(st, h, c, u):
                    b = st.units[u][1]
                    w = st.cols(u)
                    if u not in st.dve_hi:
                        dve.wait_ge(e_ok, st.unit_base + h * (2 * st.U) + (c * st.U + u + 1))
                    nc.vector.tensor_tensor(PL[b][:, 0:w], PF[b][:, 0:w], PH[b][:, 0:w], ALU.subtract).then_inc(pl_ok, 1)

                def p_hi(st, h, c, u):
                    b = st.units[u][1]
                    w = st.cols(u)
                    dve.wait_ge(e_ok, st.unit_base + h * (2 * st.U) + (c * st.U + u + 1))
                    nc.vector.tensor_copy(PH[b][:, 0:w], PF[b][:, 0:w]).then_inc(hi_step, 1)
                    dve.wait_ge(hi_step, st.hi_count(h, c, u))

                def normalise(st, h, c, x):
                    n = 2 * st.store_base + 2 * (h + x) + c
                    dve.wait_ge(av_ok, st.unit_base + (h + x) * (2 * st.U) + (c * st.U + st.U))
                    banks = 2 if st.nq == 4 else 1
                    per = min(2, st.nq)
                    O = [OP[c][k][:, 0:per * VW].rearrange("p (q e) -> p q e", q=per) for k in range(banks)]
                    for k in range(banks):
                        last = nc.vector.reciprocal(RD[:, 0, 2 * k:2 * k + per].unsqueeze(2), O[k][:, :, VD:VW])
                    last.then_inc(r_step, 1)
                    if c == 0:
                        dve.wait_ge(r_step, 3 * (st.store_base + h + x) + 1)
                        for k in range(banks):
                            r = RD[:, 0, 2 * k:2 * k + per].unsqueeze(2).broadcast_to([P, per, VD])
                            last = nc.vector.tensor_tensor(O1[:, 2 * k:2 * k + per, :], O[k][:, :, 0:VD], r, ALU.mult)
                        last.then_inc(o_out, 1)
                        return
                    dve.wait_ge(r_step, 3 * (st.store_base + h + x) + 2)
                    nc.vector.tensor_scalar(RD[:, 1, 0:st.nq], RD[:, 0, 0:st.nq], col(S_LAM), None, ALU.mult).then_inc(r_step, 1)
                    dve.wait_ge(r_step, 3 * (st.store_base + h + x) + 3)
                    dve.wait_ge(o_out, n + 1)
                    dve.wait_ge(stored[x], 16 * (2 * st.n + 1) + 8 * h)
                    for q in range(st.nq):
                        last = nc.vector.scalar_tensor_tensor(OD[x][:, q, :], O[q // 2][:, q % 2, 0:VD], RD[:, 1, q:q + 1],
                                                              O1[:, q, :], ALU.mult, ALU.add)
                    last.then_inc(o_out, 1)

                for sem in (pl_ok, red_ok, o_out):
                    dve.sem_inc(sem, 1)
                q_lo(stages[0])
                with dve.Fori(0, HDIF) as h:
                    for c in range(2):
                        for p in range(stages[0].NP):
                            reduce_piece(stages[0], h, c, p)
                maxima(stages[0])
                for st in stages:
                    nxt = stages[st.n + 1] if st.n + 1 < len(stages) else None
                    if nxt:
                        q_lo(nxt)
                    with dve.Fori(0, HDIF // 2) as pair:
                        hh = pair * 2
                        for x in range(2):
                            for c in range(2):
                                for u in range(st.U):
                                    if u in st.dve_hi:
                                        p_hi(st, hh + x, c, u)
                                    if u not in st.pool_lo:
                                        p_lo(st, hh + x, c, u)
                                    if u == NORM_LAG and x + c:
                                        normalise(st, hh, 1 - c, x + c - 1)
                                    for p in pieces_after(st, nxt, u):
                                        reduce_piece(nxt, hh + x, c, p)
                        normalise(st, hh, 1, 1)
                    if nxt:
                        maxima(nxt)

            @block.scalar
            def _(act):
                def q_hi(st, q):
                    n = q0[st.n] + q
                    if q == 0:
                        act.wait_ge(q_in, 16 * (st.n + 1))
                    if n >= 2:
                        act.wait_ge(t1_ok, n - 1)
                        act.wait_ge(ql_ok, n - 1)
                    nc.scalar.activation(QH[n % 2][:, :, :].rearrange("p h (r d) -> p h r d", r=2),
                                         QF[:, q, :].rearrange("p (h d) -> p h d", h=HC).unsqueeze(2).broadcast_to([P, HC, 2, HD]),
                                         ACT.Copy, scale=col(S_A)).then_inc(qh_ok, 1)

                def q_prepare(st):
                    for q in range(st.nq):
                        q_hi(st, q)
                        if q:
                            q1T_out(st, q - 1)
                    q1T_out(st, st.nq - 1)

                def q1T_out(st, q):
                    act.wait_ge(t1_ok, q0[st.n] + q + 1)
                    nc.scalar.activation(Q1[st.n % 2][:, :, q * P:(q + 1) * P], TQ[:, :].rearrange("p (h n) -> p h n", h=HC),
                                         ACT.Copy).then_inc(q1_out, 1)

                def q2T_out(st, q):
                    act.wait_ge(t2_ok, q0[st.n] + q + 1)
                    nc.scalar.activation(Q2[:, :, q * P:(q + 1) * P], TQ[0:HD + 2, :].rearrange("p (h n) -> p h n", h=HC),
                                         ACT.Copy).then_inc(q2_out, 1)

                def exps(st, h, idx):
                    _, b, _, parts = st.units[idx % st.U]
                    act.wait_ge(s_ok, st.unit_base + h * (2 * st.U) + (idx + 1))
                    act.wait_ge(av_ok, st.unit_base + h * (2 * st.U) + max(idx - 3, 1 - st.unit_base))
                    S = SP[idx % 2]
                    for rows, q in parts:
                        if idx % st.U not in st.dve_hi:
                            nc.scalar.activation(PH[b][rows, q], S[rows, q], ACT.Exp, scale=SC[rows, S_SC:S_SC + 1])
                        last = nc.scalar.activation(PF[b][rows, q], S[rows, q], ACT.Exp, scale=SC[rows, S_SC:S_SC + 1])
                    last.then_inc(e_ok, 1)

                def squares(st, h, c, x):
                    n = st.store_base + h + x
                    act.wait_ge(o_out, 2 * n + 3)
                    act.wait_ge(rs_step, 4 * n + 1)
                    for q in range(st.nq):
                        if q:
                            act.wait_ge(od_ok, sq_base(st) + (st.nq - 1) * (h + x) + q)
                        last = nc.scalar.activation(SQ[:, :], OD[x][:, q, :], ACT.Square, accum_out=RS[:, 0, q:q + 1])
                        if q < st.nq - 1:
                            last.then_inc(od_ok, 1)
                    last.then_inc(sq_ok, 1)

                act.sem_inc(e_ok, 1)
                q_prepare(stages[0])
                act.wait_ge(zero_ok, 24)
                for q in range(4):
                    q2T_out(stages[0], q)
                for st in stages:
                    nxt = stages[st.n + 1] if st.n + 1 < len(stages) else None
                    if nxt:
                        q_prepare(nxt)
                    with act.Fori(0, HDIF // 2) as pair:
                        hh = pair * 2
                        for x in range(2):
                            for c in range(2):
                                for u in range(st.U):
                                    exps(st, hh, (2 * x + c) * st.U + u)
                                    if x and not c and u == min(SQUARE_LAG, st.U - 1):
                                        squares(st, hh, 1, 0)
                        squares(st, hh, 1, 1)
                    if nxt:
                        for q in range(nxt.nq):
                            q2T_out(nxt, q)

            @block.tensor
            def _(pe):
                def q1T(st, q):
                    n = q0[st.n] + q
                    pe.wait_ge(qh_ok, n + 1)
                    if n:
                        pe.wait_ge(q1_out, n)
                    if st.n >= 1 and q == 0:
                        pe.wait_ge(q2_out, q0[st.n])
                    for h in range(HC):
                        last = nc.tensor.transpose(TQ[:, h * P:(h + 1) * P], QH[n % 2][:, h, :], g.ident[:, :])
                    last.then_inc(t1_ok, 1)

                def q2T(st, q):
                    n = q0[st.n] + q
                    if q == 0:
                        pe.wait_ge(m_ok, st.n + 1)
                        pe.wait_ge(q1_out, q0[st.n + 1])
                    else:
                        pe.wait_ge(q2_out, n)
                    for h in range(HC):
                        last = nc.tensor.transpose(TQ[0:HD + 2, h * P:(h + 1) * P], QL[:, q, h, :], g.ident[:, :])
                    last.then_inc(t2_ok, 1)

                def q1_at(st, h, c, q, w):
                    return Q1[st.n % 2][:, :, :].rearrange("p h n -> p (h n)")[:, bass.ds((2 * h + c) * 4 * P + q * P, w)]

                def q2_at(h, c, q, w):
                    return Q2[:, :, :].rearrange("p h n -> p (h n)")[:, bass.ds((2 * h + c) * 4 * P + q * P, w)]

                def max_piece(st, h, c, p):
                    q, _, runs, _, _ = st.pieces[p]
                    B = MB[(c * st.NP + p) % 2]
                    pe.wait_ge(red_ok, st.piece_base + h * (2 * st.NP) + max(c * st.NP + p - 1, 1 - st.piece_base))
                    at = 0
                    K = K1[:, :, :].rearrange("p h n -> p (h n)")
                    for k0, w in runs:
                        last = nc.tensor.matmul(B[:, at:at + w], q1_at(st, h, c, q, P), K[:, bass.ds((2 * h + c) * NKT * P + k0, w)],
                                                start=True, stop=True)
                        at += w
                    last.then_inc(mx_ok, 1)

                def scores(st, h, idx):
                    e = st.unit_base + h * (2 * st.U) + max(idx - 1, 1 - st.unit_base)
                    h = h + idx // (2 * st.U)
                    c, u = divmod(idx % (2 * st.U), st.U)
                    t, _, q, _ = st.units[u]
                    w = st.cols(u)
                    pe.wait_ge(e_ok, e)
                    out = SP[idx % 2][:, 0:w]
                    nc.tensor.matmul(out, kt(K1, h, c, t), q1_at(st, h, c, q, w), start=True, stop=False)
                    nc.tensor.matmul(out, kt(K2, h, c, t), q2_at(h, c, q, w), start=False, stop=True).then_inc(s_ok, 1)

                def values(st, h, idx):
                    order = max(idx // st.U, 0 if st.n else 1)
                    o = 2 * st.store_base + 2 * h + order
                    by_pool, lo = st.lo_count(h, idx // st.U, idx % st.U)
                    h = h + idx // (2 * st.U)
                    c, u = divmod(idx % (2 * st.U), st.U)
                    t, b, q_first, _ = st.units[u]
                    pe.wait_ge(pool_lo_ok if by_pool else pl_ok, lo)
                    if u == 0:
                        pe.wait_ge(o_out, o)
                    for q in range(q_first, st.nq):
                        out = OP[c][q // 2][:, (q % 2) * VW:(q % 2 + 1) * VW]
                        ph, pl = (buf[b][:, (q - q_first) * P:(q - q_first + 1) * P] for buf in (PH, PL))
                        end = u == (st.U - st.nq + q if st.nq == 4 else st.U - 1)
                        nc.tensor.matmul(out, ph, vt(VH, t, h), start=u == 0 and q % 2 == 0, stop=False, skip_group_check=True)
                        nc.tensor.matmul(out, ph, vt(VL, t, h), start=False, stop=False, skip_group_check=True)
                        last = nc.tensor.matmul(out, pl, vt(VH, t, h), start=False, stop=end, skip_group_check=True)
                    last.then_inc(av_ok, 1)

                for sem in (s_ok, av_ok, mx_ok):
                    pe.sem_inc(sem, 1)
                for q in range(4):
                    q1T(stages[0], q)
                pe.wait_ge(q1_out, 4)
                with pe.Fori(0, HDIF) as h:
                    for c in range(2):
                        for p in range(stages[0].NP):
                            max_piece(stages[0], h, c, p)
                for q in range(4):
                    q2T(stages[0], q)
                pe.wait_ge(k2_ok, 1)
                for st in stages:
                    nxt = stages[st.n + 1] if st.n + 1 < len(stages) else None
                    if nxt:
                        for q in range(nxt.nq):
                            q1T(nxt, q)
                        pe.wait_ge(q1_out, q0[nxt.n + 1])
                    pe.wait_ge(q2_out, q0[st.n + 1])
                    with pe.Fori(0, HDIF // 2) as pair:
                        hh = pair * 2
                        scores(st, hh, 0)
                        scores(st, hh, 1)
                        for idx in range(4 * st.U):
                            x, c, u = idx // (2 * st.U), idx // st.U % 2, idx % st.U
                            if idx + 2 < 4 * st.U:
                                scores(st, hh, idx + 2)
                            for p in pieces_after(st, nxt, u):
                                max_piece(nxt, hh + x, c, p)
                            if idx:
                                values(st, hh, idx - 1)
                        values(st, hh, 4 * st.U - 1)
                    if nxt:
                        for q in range(nxt.nq):
                            q2T(nxt, q)


NORM_LAG = 2
SQUARE_LAG = 4


def pieces_after(st, nxt, u):
    return range(u * nxt.NP // st.U, (u + 1) * nxt.NP // st.U) if nxt else ()


def sq_base(st):
    return 3 * HDIF * st.n


def phase_scales(g, WO, WOL, MW, GF):
    nc, dram = g.nc, g.dram
    with ExitStack() as ctx:
        W32 = g.sb("wout32", [P, KC, D], f32, ctx)
        SG = g.sb("gain_sub", [P, 1], f32, ctx)
        MK = g.sb("wout_max_by_chunk", [P, KC], f32, ctx)
        TI = g.sb("tmp_int2", [P, 1], i32, ctx)
        MA = g.sb("max_parts", [P, 4], f32, ctx)
        MB = g.sb("max_everywhere", [P, 4], f32, ctx)
        EX = g.sb("exponents", [P, 4], f32, ctx)
        s = lambda n: g.sem("o0_" + n)
        w_k = [s(f"chunk_in{k}") for k in range(KC)]
        small_in, local, everywhere, step, scales_ok, hi_ok = (
            s(n) for n in ("small_in", "max_local", "max_all", "dve_step", "scales", "hi"))
        SC = g.SC
        col = lambda c: SC[:, c:c + 1]
        with nc.Block() as block:
            @block.sync
            def _(sp):
                sp.dma_start(SG[:, :], dram["subln_g"]).then_inc(small_in, 16)
                sp.dma_start(GF[:, :], dram["norm_ffn_g"]).then_inc(small_in, 16)
                for k in range(KC):
                    sp.dma_start(W32[:, k, :], dram["w_out"][0, k * P:(k + 1) * P, :]).then_inc(w_k[k], 16)

            @block.gpsimd
            def _(pool):
                pool.wait_ge(local, 1)
                nc.gpsimd.partition_all_reduce(MB[:, :], MA[:, :], P, RMAX).then_inc(everywhere, 1)

            @block.vector
            def _(dve):
                link = Chain(dve, step)
                dve.wait_ge(small_in, 32)
                link(nc.vector.tensor_scalar(SG[:, :], SG[:, :], 1.0 - LAM_INIT, None, ALU.mult))
                mw = MW[:, :].rearrange("p (i w) -> p i w", w=3)
                link(nc.vector.tensor_reduce(MA[:, 1:2], mw[:, :, 0:2], AX.XY, ALU.max))
                link(nc.vector.tensor_reduce(MA[:, 2:3], mw[:, :, 2:3], AX.XY, ALU.max))
                link(nc.vector.tensor_reduce(MA[:, 3:4], GF[:, :], AX.X, ALU.max, apply_absolute_value=True))
                for k in range(KC):
                    dve.wait_ge(w_k[k], 16)
                    if k >= KC // 2:
                        link(nc.vector.tensor_scalar(W32[:, k, :], W32[:, k, :], SG[:, :], None, ALU.mult))
                    link(nc.vector.tensor_reduce(MK[:, k:k + 1], W32[:, k, :], AX.X, ALU.max, apply_absolute_value=True))
                nc.vector.tensor_reduce(MA[:, 0:1], MK[:, :], AX.X, ALU.max).then_inc(local, 1)
                dve.wait_ge(everywhere, 1)
                for n in range(4):
                    exponent(nc, link, EX[:, n:n + 1], TI[:, :], MB[:, n:n + 1])
                link(nc.vector.tensor_scalar(EX[:, :], EX[:, :], 30.0, 220.0, ALU.max, ALU.min))
                E_o, E_gu, E_d, E_g = (EX[:, n:n + 1] for n in range(4))
                pow2(nc, link, col(S_O), col(S_F0), col(S_T), TI[:, :], E_o, -1.0, 265.0)
                pow2(nc, link, col(S_OD), col(S_F2), col(S_T), TI[:, :], col(S_F0), -1.0, 245.0)
                link(nc.vector.tensor_tensor(col(S_F2), col(S_F0), col(S_F1), ALU.add))
                pow2(nc, link, col(S_OA), col(S_F2), col(S_T), TI[:, :], col(S_F2), -1.0, 381.0)
                link(nc.vector.tensor_tensor(col(S_F3), E_g, E_gu, ALU.add))
                pow2(nc, link, col(S_G), col(S_F4), col(S_T), TI[:, :], col(S_F3), -1.0, 393.0)
                pow2(nc, link, col(S_GI), col(S_F5), col(S_T), TI[:, :], col(S_F4), -1.0, 246.0)
                pow2(nc, link, col(S_ACT), col(S_F6), col(S_T), TI[:, :], col(S_F3), -2.0, 626.0)
                link(nc.vector.tensor_tensor(col(S_F5), col(S_F5), col(S_F6), ALU.add))
                pow2(nc, link, col(S_CU), col(S_F5), col(S_T), TI[:, :], col(S_F5), 1.0, -127.0)
                pow2(nc, link, col(S_D), col(S_F7), col(S_T), TI[:, :], E_d, -1.0, 266.0)
                link(nc.vector.tensor_tensor(col(S_F7), col(S_F7), col(S_F6), ALU.add))
                pow2(nc, link, col(S_YI), col(S_F7), col(S_T), TI[:, :], col(S_F7), -1.0, 381.0)
                nc.vector.tensor_scalar(GF[:, :], GF[:, :], col(S_G), None, ALU.mult).then_inc(scales_ok, 1)
                for k in range(KC):
                    dve.wait_ge(hi_ok, k + 1)
                    link(nc.vector.scalar_tensor_tensor(WOL[:, k, :], W32[:, k, :], col(S_O), WO[:, k, :],
                                                        ALU.mult, ALU.subtract))

            @block.scalar
            def _(act):
                act.wait_ge(scales_ok, 1)
                for k in range(KC):
                    nc.scalar.activation(WO[:, k, :], W32[:, k, :], ACT.Copy, scale=col(S_O)).then_inc(hi_ok, 1)


DSC = 512.0


def phase_output(g, WO, WOL, H, N2):
    nc, dram = g.nc, g.dram
    with ExitStack() as ctx:
        M = [g.sb(f"mix_tile{n}", [P, D], f32, ctx) for n in range(2)]
        X = [g.sb(f"x_again{n}", [P, D], f32, ctx) for n in range(2)]
        SH, SL = (g.sb(n, [P, D], f16, ctx) for n in ("mix_hi", "mix_lo"))
        MT = [g.sb(f"mixT_{h}", [P, KC, P], f16, ctx) for h in ("hi", "lo")]
        NH, NL = (g.sb(n, [P, D], f16, ctx) for n in ("hnorm_hi", "hnorm_lo"))
        ST = g.sb("h_stats", [P, 8], f32, ctx)
        TM = [g.ps(f"mixT_ps{n}", [P, KC * P], f16, ctx) for n in range(2)]
        TN = [g.ps(f"hnT_ps{n}", [P, KC * P], f16, ctx) for n in range(2)]
        YP = [[g.ps(f"y_ps{n}{m}", [P, 512], f32, ctx) for m in range(2)] for n in range(2)]
        SC = g.SC
        col = lambda c: SC[:, c:c + 1]
        s = lambda n: g.sem("o_" + n)
        in_ = [s("in0"), s("in1")]
        (const_ok, mh_ok, ml_ok, tm_ok, mt_hi, mt_lo, y_ok, h_ok, sq_ok, step_p, rs_ok, nh_ok, nl_ok, tn_ok, n2_hi, n2_lo,
         a_ok) = (s(n) for n in ("consts", "mix_hi", "mix_lo", "mixT", "mixT_hi_out", "mixT_lo_out", "y", "h", "squares",
                                 "pool_step", "rstd", "norm_hi", "norm_lo", "normT", "n2_hi", "n2_lo", "window_part"))
        act_turns = s("act_turns")
        half = slice(0, D // 2), slice(D // 2, D)
        with nc.Block() as block:
            @block.sync
            def _(sp):
                def load(i, b):
                    row = i * P if isinstance(i, int) else sp.snap(i * P)
                    if not isinstance(i, int) or i > 1:
                        sp.wait_ge(h_ok, 2 * i - 2)
                    sp.dma_start(M[b][:, :], g.mix[bass.ds(row, P), :]).then_inc(in_[b], 16)
                    sp.dma_start(X[b][:, :], dram["x"][bass.ds(row, P), :]).then_inc(in_[b], 16)
                load(0, 0)
                row_tiles(sp, lambda i, b, first, last: None if last else load(i + 1, 1 - b))

            @block.gpsimd
            def _(pool):
                for c, value in ((4, -0.5), (5, EPS), (6, XSC)):
                    nc.gpsimd.memset(ST[:, c:c + 1], value).then_inc(const_ok, 1)
                pool.wait_ge(const_ok, 3)

                def rstd(i):
                    pool.wait_ge(sq_ok, i + 1)
                    nc.gpsimd.tensor_tensor(ST[:, 1:2], ST[:, 0:1], ST[:, 5:6], ALU.add).then_inc(step_p, 1)
                    pool.wait_ge(step_p, 2 * i + 1)
                    nc.gpsimd.tensor_tensor(ST[:, 2:3], ST[:, 1:2], ST[:, 4:5], ALU.pow).then_inc(step_p, 1)
                    pool.wait_ge(step_p, 2 * i + 2)
                    pool.wait_ge(nl_ok, i)
                    nc.gpsimd.tensor_tensor(ST[:, 3:4], ST[:, 2:3], ST[:, 6:7], ALU.mult).then_inc(rs_ok, 1)
                row_tiles(pool, lambda i, b, first, last: rstd(i))

            @block.vector
            def _(dve):
                def mix_lo(i, b):
                    dve.wait_ge(mh_ok, i + 1)
                    if not isinstance(i, int) or i > 0:
                        dve.wait_ge(tm_ok, i)
                    nc.vector.scalar_tensor_tensor(SL[:, half[0]], M[b][:, half[0]], col(S_A), SH[:, half[0]], ALU.mult, ALU.subtract)
                    nc.vector.scalar_tensor_tensor(SL[:, half[1]], M[b][:, half[1]], DSC, SH[:, half[1]],
                                                   ALU.mult, ALU.subtract).then_inc(ml_ok, 1)

                def mixT_lo_out(i):
                    dve.wait_ge(tm_ok, i + 1)
                    if not isinstance(i, int) or i > 0:
                        dve.wait_ge(y_ok, 2 * i)
                    nc.vector.tensor_copy(MT[1][:, :, :], TM[1][:, :].rearrange("p (k n) -> p k n", k=KC)).then_inc(mt_lo, 1)

                def residual(i, b, n):
                    dve.wait_ge(y_ok, 2 * i + n + 1)
                    out = H[:, bass.ds(i * D + n * 512, 512)]
                    nc.vector.scalar_tensor_tensor(out, YP[n][0][:, :], col(S_OA), X[b][:, half[n]], ALU.mult, ALU.add).then_inc(a_ok, 1)
                    dve.wait_ge(a_ok, 2 * i + n + 1)
                    nc.vector.scalar_tensor_tensor(out, YP[n][1][:, :], col(S_OD), out, ALU.mult, ALU.add).then_inc(h_ok, 1)

                def norm_lo(i):
                    dve.wait_ge(nh_ok, i + 1)
                    nc.vector.scalar_tensor_tensor(NL[:, :], H[:, bass.ds(i * D, D)], ST[:, 3:4], NH[:, :],
                                                   ALU.mult, ALU.subtract).then_inc(nl_ok, 1)

                def n2_lo_out(i):
                    dve.wait_ge(tn_ok, i + 1)
                    nc.vector.tensor_copy(N2[1][:, :, bass.ds(i * P, P)], TN[1][:, :].rearrange("p (k n) -> p k n", k=KC)).then_inc(n2_lo, 1)

                dve.wait_ge(in_[0], 32)
                mix_lo(0, 0)
                mixT_lo_out(0)

                def step(i, b, first, last):
                    if not first:
                        norm_lo(i - 1)
                    if not last:
                        mix_lo(i + 1, 1 - b)
                    residual(i, b, 0)
                    if not first:
                        n2_lo_out(i - 1)
                    residual(i, b, 1)
                    if not last:
                        mixT_lo_out(i + 1)
                row_tiles(dve, step)
                norm_lo(NT)
                n2_lo_out(NT)

            @block.scalar
            def _(act):
                def mix_hi(i, b):
                    act.wait_ge(in_[b], x_count(i, b) * 32)
                    if not isinstance(i, int) or i > 0:
                        act.wait_ge(tm_ok, i)
                    nc.scalar.activation(SH[:, half[0]], M[b][:, half[0]], ACT.Copy, scale=col(S_A))
                    nc.scalar.activation(SH[:, half[1]], M[b][:, half[1]], ACT.Copy, scale=DSC).then_inc(mh_ok, 1)

                def mixT_hi_out(i):
                    act.wait_ge(tm_ok, i + 1)
                    if not isinstance(i, int) or i > 0:
                        act.wait_ge(y_ok, 2 * i)
                    nc.scalar.activation(MT[0][:, :, :], TM[0][:, :].rearrange("p (k n) -> p k n", k=KC), ACT.Copy).then_inc(mt_hi, 1)

                def squares(i):
                    act.wait_ge(h_ok, 2 * i + 2)
                    act.sem_inc(act_turns, 1)
                    nc.scalar.activation(NH[:, :].bitcast(bf16), H[:, bass.ds(i * D, D)], ACT.Square, scale=D ** -0.5,
                                         accum_out=ST[:, 0:1]).then_inc(sq_ok, 1)

                def norm_hi(i):
                    act.wait_ge(rs_ok, i + 1)
                    act.sem_inc(act_turns, 1)
                    nc.scalar.activation(NH[:, :], H[:, bass.ds(i * D, D)], ACT.Copy, scale=ST[:, 3:4]).then_inc(nh_ok, 1)

                def n2_hi_out(i):
                    act.wait_ge(tn_ok, i + 1)
                    nc.scalar.activation(N2[0][:, :, bass.ds(i * P, P)], TN[0][:, :].rearrange("p (k n) -> p k n", k=KC),
                                         ACT.Copy).then_inc(n2_hi, 1)
                mix_hi(0, 0)
                mixT_hi_out(0)

                def step(i, b, first, last):
                    if not first:
                        norm_hi(i - 1)
                    if not last:
                        mix_hi(i + 1, 1 - b)
                    if not first:
                        n2_hi_out(i - 1)
                    if not last:
                        mixT_hi_out(i + 1)
                    squares(i)
                row_tiles(act, step)
                norm_hi(NT)
                n2_hi_out(NT)

            @block.tensor
            def _(pe):
                def mixT(i):
                    pe.wait_ge(ml_ok, i + 1)
                    pe.wait_ge(mt_hi, i)
                    pe.wait_ge(mt_lo, i)
                    for src, dst in ((SH, TM[0]), (SL, TM[1])):
                        for k in range(KC):
                            last = nc.tensor.transpose(dst[:, k * P:(k + 1) * P], src[:, k * P:(k + 1) * P], g.ident[:, :])
                    last.then_inc(tm_ok, 1)

                def normT(i):
                    pe.wait_ge(nl_ok, i + 1)
                    pe.wait_ge(n2_hi, i)
                    pe.wait_ge(n2_lo, i)
                    for src, dst in ((NH, TN[0]), (NL, TN[1])):
                        for k in range(KC):
                            last = nc.tensor.transpose(dst[:, k * P:(k + 1) * P], src[:, k * P:(k + 1) * P], g.ident[:, :])
                    last.then_inc(tn_ok, 1)

                def product(i, n):
                    if not isinstance(i, int) or i > 0:
                        pe.wait_ge(h_ok, 2 * i + n - 1)
                    for m in range(2):
                        for k in range(4 * m, 4 * m + 4):
                            hi, lo = MT[0][:, k, :], MT[1][:, k, :]
                            out = YP[n][m][:, :]
                            nc.tensor.matmul(out, hi, WO[:, k, half[n]], start=k % 4 == 0, stop=False)
                            nc.tensor.matmul(out, hi, WOL[:, k, half[n]], start=False, stop=False)
                            last = nc.tensor.matmul(out, lo, WO[:, k, half[n]], start=False, stop=k % 4 == 3)
                    last.then_inc(y_ok, 1)

                mixT(0)

                def step(i, b, first, last):
                    pe.wait_ge(mt_hi, i + 1)
                    pe.wait_ge(mt_lo, i + 1)
                    product(i, 0)
                    if not first:
                        normT(i - 1)
                    product(i, 1)
                    if not last:
                        mixT(i + 1)
                row_tiles(pe, step)
                normT(NT)


NTOK = SEQ + DEC
TB = 6
TBW = NTOK // TB
PAIRS = FF // (2 * P)
YS = 2 * NTT


def phase_ffn(g, H, N2, GF):
    nc, dram = g.nc, g.dram
    with ExitStack() as ctx:
        F = [g.sb(f"{n}32", [P, KC, 2 * P], f32, ctx) for n in ("gate", "up")]
        FH = [g.sb(f"{n}_hi", [P, KC, 2 * P], f16, ctx) for n in ("gate", "up")]
        FL = [g.sb(f"{n}_lo", [P, KC, 2 * P], f16, ctx) for n in ("gate", "up")]
        DW = g.sb("down32", [P, D], f32, ctx)
        DH, DL = (g.sb(n, [P, 2, D], f16, ctx) for n in ("down_hi", "down_lo"))
        AH, AL = (g.sb(n, [P, 2, NTOK], f16, ctx) for n in ("act_hi", "act_lo"))
        SI = [g.sb(f"silu{n}", [P, TBW], f32, ctx) for n in range(2)]
        AF = [g.sb(f"act{n}", [P, TBW], f32, ctx) for n in range(2)]
        GP = [[g.ps(f"{n}_ps{f}", [P, 512], f32, ctx) for n in ("gate", "up")] for f in range(2)]
        YP = [g.ps(f"down_ps{n}", [P, 512], f32, ctx) for n in range(4)]
        SC = g.SC
        col = lambda c: SC[:, c:c + 1]
        s = lambda n: g.sem("f_" + n)
        gu_in, gu_hi, gu_lo, gu_used, d_in, d_hi, d_lo, al_ok, y_ok, h_ok, down_done = (
            s(n) for n in ("gu_in", "gu_hi", "gu_lo", "gu_used", "down_in", "down_hi", "down_lo", "act_lo", "y", "h", "down_done"))
        up_ok, si_ok, mul_ok, ah_ok = ([s(f"{n}{f}") for f in range(2)] for n in ("gate_up", "silu", "act", "act_hi"))
        pe_turns = s("pe_turns")
        src = [dram[n].rearrange("a (k p) f -> p (a k) f", p=P) for n in ("w_gate", "w_up")]
        down = dram["w_down"].rearrange("a f d -> (a f) d")

        def steps(eng, body):
            with eng.Fori(0, PAIRS - 1) as i:
                body(i, False)
            body(PAIRS - 1, True)

        with nc.Block() as block:
            @block.sync
            def _(sp):
                with sp.Fori(0, PAIRS) as i:
                    c, r0, r1, n = (sp.snap(x) for x in (i * (2 * P), i * (2 * P), i * (2 * P) + P, KC * i))
                    sp.wait_ge(gu_lo, n)
                    for w in range(2):
                        sp.dma_start(F[w][:, :, :], src[w][:, :, bass.ds(c, 2 * P)]).then_inc(gu_in, 16)
                    sp.wait_ge(d_lo, 2 * i)
                    sp.dma_start(DW[:, :], down[bass.ds(r0, P), :]).then_inc(d_in, 16)
                    sp.wait_ge(d_lo, 2 * i + 1)
                    sp.dma_start(DW[:, :], down[bass.ds(r1, P), :]).then_inc(d_in, 16)

            @block.vector
            def _(dve):
                def split_lo(i, k):
                    dve.wait_ge(gu_hi, KC * i + k + 1)
                    for w in range(2):
                        last = nc.vector.scalar_tensor_tensor(FL[w][:, k, :], F[w][:, k, :], GF[:, k:k + 1], FH[w][:, k, :],
                                                              ALU.mult, ALU.subtract)
                    last.then_inc(gu_lo, 1)

                def down_lo(i, f):
                    dve.wait_ge(d_hi, 2 * i + f + 1)
                    nc.vector.scalar_tensor_tensor(DL[:, f, :], DW[:, :], col(S_D), DH[:, f, :], ALU.mult, ALU.subtract).then_inc(d_lo, 1)

                def act_mul(i, t, f):
                    if t:
                        dve.wait_ge(al_ok, 2 * (TB * i + t) + f - 1)
                    dve.wait_ge(si_ok[f], TB * i + t + 1)
                    nc.vector.scalar_tensor_tensor(AF[f][:, :], GP[f][1][:, 0:TBW], col(S_CU), SI[f][:, :],
                                                   ALU.mult, ALU.mult).then_inc(mul_ok[f], 1)

                def act_lo(i, t, f):
                    dve.wait_ge(ah_ok[f], TB * i + t + 1)
                    v = slice(t * TBW, (t + 1) * TBW)
                    nc.vector.tensor_tensor(AL[:, f, v], AF[f][:, :], AH[:, f, v], ALU.subtract).then_inc(al_ok, 1)

                def add(i, t, n):
                    dve.wait_ge(y_ok, YS * i + 2 * t + n + 1)
                    rows = P if t < NT else DEC
                    at = t * D + n * 512
                    nc.vector.scalar_tensor_tensor(H[0:rows, at:at + 512], YP[(2 * t + n) % 4][0:rows, :], SC[0:rows, S_YI:S_YI + 1],
                                                   H[0:rows, at:at + 512], ALU.mult, ALU.add).then_inc(h_ok, 1)
                for k in range(KC):
                    split_lo(0, k)

                def step(i, last):
                    for t in range(TB):
                        act_mul(i, t, 0)
                        act_mul(i, t, 1)
                        act_lo(i, t, 0)
                        act_lo(i, t, 1)
                        if t < 2:
                            down_lo(i, t)
                    for t in range(NTT):
                        add(i, t, 0)
                        add(i, t, 1)
                        if t % 2 == 0 and t // 2 < KC and not last:
                            split_lo(i + 1, t // 2)
                steps(dve, step)

            @block.scalar
            def _(act):
                def split_hi(i, k):
                    if k == 0:
                        act.wait_ge(gu_in, 32 * i + 32)
                        act.wait_ge(gu_used, i)
                    for w in range(2):
                        last = nc.scalar.activation(FH[w][:, k, :], F[w][:, k, :], ACT.Copy, scale=GF[:, k:k + 1])
                    last.then_inc(gu_hi, 1)

                def down_hi(i, f):
                    act.wait_ge(d_in, 32 * i + 16 * f + 16)
                    if f == 0:
                        act.wait_ge(down_done, i)
                    nc.scalar.activation(DH[:, f, :], DW[:, :], ACT.Copy, scale=col(S_D)).then_inc(d_hi, 1)

                def silu(i, t, f):
                    act.wait_ge(up_ok[f], TB * i + t + 1)
                    nc.scalar.activation(SI[f][:, :], GP[f][0][:, 0:TBW], ACT.Silu, scale=col(S_GI)).then_inc(si_ok[f], 1)

                def act_hi(i, t, f):
                    act.wait_ge(mul_ok[f], TB * i + t + 1)
                    nc.scalar.activation(AH[:, f, t * TBW:(t + 1) * TBW], AF[f][:, :], ACT.Copy).then_inc(ah_ok[f], 1)
                for k in range(KC):
                    split_hi(0, k)

                def step(i, last):
                    for t in range(TB):
                        silu(i, t, 0)
                        silu(i, t, 1)
                        act_hi(i, t, 0)
                        act_hi(i, t, 1)
                        if t < 2:
                            down_hi(i, t)
                    if not last:
                        for k in range(KC):
                            split_hi(i + 1, k)
                steps(act, step)

            @block.tensor
            def _(pe):
                def gate_up(i, t, f):
                    pe.wait_ge(mul_ok[f], TB * i + t)
                    for w in range(2):
                        for k in range(KC):
                            c = slice(f * P, (f + 1) * P)
                            nh, nl = (N2[x][:, k, bass.ds(t * TBW, TBW)] for x in range(2))
                            out = GP[f][w][:, 0:TBW]
                            nc.tensor.matmul(out, FH[w][:, k, c], nh, start=k == 0, stop=False)
                            nc.tensor.matmul(out, FH[w][:, k, c], nl, start=False, stop=False)
                            last = nc.tensor.matmul(out, FL[w][:, k, c], nh, start=False, stop=k == KC - 1)
                    last.then_inc(up_ok[f], 1)

                def down(i, t, n, bank, rows):
                    out = YP[bank][0:rows, :]
                    c = slice(n * 512, (n + 1) * 512)
                    for f in range(2):
                        ah, al = (A[:, f, bass.ds(t * P, rows)] for A in (AH, AL))
                        nc.tensor.matmul(out, ah, DH[:, f, c], start=f == 0, stop=False)
                        nc.tensor.matmul(out, ah, DL[:, f, c], start=False, stop=False)
                        last = nc.tensor.matmul(out, al, DH[:, f, c], start=False, stop=f == 1)
                    last.then_inc(y_ok, 1)

                def step(i, last):
                    pe.wait_ge(gu_lo, KC * i + KC)
                    pe.sem_inc(pe_turns, 1)
                    with pe.Fori(0, TB) as t:
                        for f in range(2):
                            gate_up(i, t, f)
                    pe.wait_ge(up_ok[1], TB * i + TB)
                    pe.sem_inc(gu_used, 1)
                    pe.wait_ge(d_lo, 2 * i + 2)
                    pe.wait_ge(al_ok, 2 * TB * i + 2 * TB)
                    pe.wait_ge(h_ok, YS * i)
                    for j in range(2):
                        for n in range(2):
                            down(i, j, n, 2 * j + n, P)
                    with pe.Fori(1, NT // 2) as k:
                        for j in range(2):
                            for n in range(2):
                                pe.wait_ge(h_ok, YS * i + 4 * k + (2 * j + n - 3))
                                down(i, 2 * k + j, n, 2 * j + n, P)
                    for n in range(2):
                        pe.wait_ge(h_ok, YS * i + 2 * NT + n - 3)
                        down(i, NT, n, n, DEC)
                    pe.wait_ge(y_ok, YS * i + YS)
                    pe.sem_inc(down_done, 1)
                steps(pe, step)


def phase_final(g, H):
    nc, dram = g.nc, g.dram
    with ExitStack() as ctx:
        GN = g.sb("gain_final", [P, D], f32, ctx)
        Y = [g.sb(f"y_tile{n}", [P, D], f32, ctx) for n in range(4)]
        SQ = g.sb("final_squares", [P, D], bf16, ctx)
        ST = g.sb("final_stats", [P, 4, NTT], f32, ctx)
        s = lambda n: g.sem("n_" + n)
        g_in, sq_ok, sq_step, step_p, rs_ok, y_ok, const_ok = (
            s(n) for n in ("gain_in", "squares", "square_step", "pool_step", "rstd", "y", "const"))
        stored = [s(f"stored{n}") for n in range(4)]
        with nc.Block() as block:
            @block.sync
            def _(sp):
                sp.dma_start(GN[:, :], dram["final_norm_g"].broadcast_to([P, D])).then_inc(g_in, 16)
                for i in range(NTT):
                    sp.wait_ge(y_ok, i + 1)
                    if i < NT:
                        sp.dma_start(dram["y_prompt"][i * P:(i + 1) * P, :], Y[i % 4][:, :]).then_inc(stored[i % 4], 16)
                    else:
                        sp.dma_start(dram["y_sample"], Y[i % 4][0:DEC, :]).then_inc(stored[i % 4], 16)
                for n in range(4):
                    sp.wait_ge(stored[n], 16 * len(range(n, NTT, 4)))

            @block.gpsimd
            def _(pool):
                nc.gpsimd.memset(ST[:, 3, 0:1], -0.5).then_inc(const_ok, 1)
                nc.gpsimd.memset(ST[:, 3, 1:2], EPS).then_inc(const_ok, 1)
                pool.wait_ge(const_ok, 2)
                for i in range(NTT):
                    pool.wait_ge(sq_ok, i + 1)
                    nc.gpsimd.tensor_tensor(ST[:, 1, i:i + 1], ST[:, 0, i:i + 1], ST[:, 3, 1:2], ALU.add).then_inc(step_p, 1)
                    pool.wait_ge(step_p, i + 1)
                    nc.gpsimd.tensor_tensor(ST[:, 2, i:i + 1], ST[:, 1, i:i + 1], ST[:, 3, 0:1], ALU.pow).then_inc(rs_ok, 1)

            @block.scalar
            def _(act):
                for i in range(NTT):
                    if i:
                        act.wait_ge(sq_ok, i)
                    nc.scalar.activation(SQ[:, :], H[:, i * D:(i + 1) * D], ACT.Square, scale=D ** -0.5,
                                         accum_out=ST[:, 0, i:i + 1]).then_inc(sq_ok, 1)

            @block.vector
            def _(dve):
                dve.wait_ge(g_in, 16)
                for i in range(NTT):
                    dve.wait_ge(rs_ok, i + 1)
                    if i >= 4:
                        dve.wait_ge(stored[i % 4], 16 * (i // 4))
                    nc.vector.scalar_tensor_tensor(Y[i % 4][:, :], H[:, i * D:(i + 1) * D], ST[:, 2, i:i + 1], GN[:, :],
                                                   ALU.mult, ALU.mult).then_inc(y_ok, 1)


def build(nc, dram):
    g = Prog(nc, dram, ExitStack())
    with g.ctx:
        g.SC = g.sb("scales", [P, NSC], f32)
        g.AI4 = g.sb("inverse_scale4", [P, 4], f32)
        g.ident = g.sb("identity", [P, P], f16)
        g.w0_k = [g.sem(f"w0_chunk_in{k}") for k in range(KC)]
        g.scr = nc.dram_tensor("q_scratch", (NTT * P, SCR), f32).ap()
        g.mix = nc.dram_tensor("mix_scratch", (NTT * P, D), f32).ap()
        MW = g.sb("ffn_weight_max", [P, 48], f32)
        with ExitStack() as att:
            nk, nv = HC * NKT * P, NKT * HDIF * VW
            KV = g.sb("keys_values", [P, nk + 2 * nv], f16, att)
            K1 = KV[:, 0:nk].rearrange("p (h n) -> p h n", h=HC)
            VH, VL = KV[:, nk:nk + nv], KV[:, nk + nv:nk + 2 * nv]
            W32 = KV[:, 0:2 * KC * PROJ].bitcast(f32).rearrange("p (k n) -> p k n", k=KC)
            with ExitStack() as win:
                WH = g.sb("w_in_hi", [P, KC, PROJ], f16, win)
                WL = g.sb("w_in_lo", [P, KC, PROJ], f16, win)
                phase_weights_in(g, W32, WH, WL)
                phase_project(g, WH, WL, K1, VH, VL, MW)
            phase_window(g)
            g.phase_end()
            phase_differential(g, K1, VH, VL)
        GF = g.sb("gain_ffn", [P, KC], f32)
        H = g.sb("residual_rows", [P, NTT * D], f32)
        with ExitStack() as ffn:
            N2 = [g.sb(f"ffn_inT_{h}", [P, KC, NTT * P], f16, ffn) for h in ("hi", "lo")]
            with ExitStack() as out:
                WO, WOL = (g.sb(n, [P, KC, D], f16, out) for n in ("w_out_hi", "w_out_lo"))
                phase_scales(g, WO, WOL, MW, GF)
                phase_output(g, WO, WOL, H, N2)
            phase_ffn(g, H, N2, GF)
        phase_final(g, H)


_OUT = [("y_prompt", (SEQ, D), (1, SEQ, D)), ("y_sample", (DEC, D), (1, DEC, D)),
        ("p_swa_k", (META + WIN, KVS * HD), (1, 1, META + WIN, KVS, HD)),
        ("p_swa_v", (META + WIN, KVS * HD), (1, 1, META + WIN, KVS, HD)),
        ("p_diff_k", (META + SEQ, HC * HD), (1, 1, META + SEQ, HDIF, 2, HD)),
        ("p_diff_v", (META + SEQ, HDIF * VD), (1, 1, META + SEQ, HDIF, VD)),
        ("s_swa_k", (META + WIN, KVS * HD), (1, 1, META + WIN, KVS, HD)),
        ("s_swa_v", (META + WIN, KVS * HD), (1, 1, META + WIN, KVS, HD)),
        ("s_diff_k", (DEC, HC * HD), (1, 1, DEC, HDIF, 2, HD)),
        ("s_diff_v", (DEC, HDIF * VD), (1, 1, DEC, HDIF, VD))]


def _tables():
    pos = np.zeros(NTT * P, np.float32)
    pos[:SEQ] = META + np.arange(SEQ)
    pos[SEQ:SEQ + DEC] = META + PAST + np.arange(DEC)
    pos[SEQ + DEC:SEQ + DEC + META] = np.arange(META)
    inv = (10000.0 ** (-np.arange(0, HD, 2) / HD)).astype(np.float32)
    ang = (pos[:, None] * inv[None, :]).astype(np.float64)
    cos, sin = np.cos(ang), np.sin(ang)
    return np.concatenate([cos, cos, -sin, sin], axis=1).astype(np.float32)


def kernel(**inputs):
    import concourse.bacc as _bacc
    from concourse.bass_utils import run_bass_kernel_spmd as _run

    a = {n: np.asarray(v) for n, v in inputs.items()}
    rows = [a["x_prompt"][0], a["x_sample"][0], a["meta_tokens"],
            np.zeros((NTT * P - SEQ - DEC - META, D), np.float32)]
    arrays = {"x": np.concatenate(rows, axis=0), "cos_sin": _tables(), "ident": np.eye(P, dtype=np.float16),
              "lambdas": np.stack([a[n] for n in ("lambda_q1", "lambda_k1", "lambda_q2", "lambda_k2")], axis=1)}
    for n in ("cache_swa_k", "cache_swa_v", "cache_diff_k", "cache_diff_v", "w_in", "attn_sinks",
              "w_out", "w_gate", "w_up", "w_down"):
        arrays[n] = np.ascontiguousarray(a[n])
    for n in ("norm_mix_g", "norm_ffn_g", "subln_g"):
        arrays[n] = np.ascontiguousarray(a[n][0].reshape(-1, P).T)
    arrays["final_norm_g"] = np.ascontiguousarray(a["final_norm_g"])[None, :]
    nc = _bacc.Bacc("TRN2", target_bir_lowering=False, num_devices=1)
    dram = {n: nc.dram_tensor(f"in_{n}", v.shape, mybir.dt.from_np(v.dtype), kind="ExternalInput").ap()
            for n, v in arrays.items()}
    for n, shape, _ in _OUT:
        dram[n] = nc.dram_tensor(f"out_{n}", shape, f32, kind="ExternalOutput").ap()
    build(nc, dram)
    r = _run(nc, [{f"in_{n}": v for n, v in arrays.items()}], core_ids=[0])
    return tuple(np.reshape(r.results[0][f"out_{n}"], shape) for n, _, shape in _OUT)
```

```python
import math
from contextlib import ExitStack

import numpy as np

import concourse.bass as bass
from concourse import mybir

f32 = mybir.dt.float32
f16 = mybir.dt.float16
bf16 = mybir.dt.bfloat16
i32 = mybir.dt.int32
ACT = mybir.ActivationFunctionType
ALU = mybir.AluOpType
AX = mybir.AxisListType
RMAX = bass.bass_isa.ReduceOp.max

P = 128
D = 1024
KC = D // P
SEQ = 2048
META = 16
DEC = 64
PAST = 256
HD = 64
HS = 8
KVS = 2
GRP = HS // KVS
HDIF = 4
HC = 2 * HDIF
VD = 2 * HD
FF = 2816
WIN = 128
CH = 64
EPS = 1e-6
PROJ = 2304
NT = SEQ // P
TS = NT
NTT = NT + 1
C_QA, C_KA, C_VA, C_QD, C_KD, C_VD = 0, 512, 640, 768, 1280, 1792
NQ = HS + HC
LAM_INIT = 0.8 - 0.6 * math.exp(-0.3 * 0)
XSC = 256.0
MROW = 32768.0
NKT = NT + 4
VW = VD + 1
WCH = 1408


class Prog:

    def __init__(self, nc, dram, ctx):
        self.nc, self.dram, self.ctx, self.sems = nc, dram, ctx, []

    def sb(self, name, shape, dt, ctx=None):
        return (ctx or self.ctx).enter_context(self.nc.sbuf_tensor(name, shape, dt))

    def ps(self, name, shape, dt, ctx):
        return ctx.enter_context(self.nc.psum_tensor(name, shape, dt))

    def sem(self, name):
        self.sems.append(self.nc.alloc_semaphore(name=name))
        return self.sems[-1]

    def phase_end(self):
        self.nc.clear_and_free_semaphores(self.sems)
        self.nc.all_engine_barrier()
        self.sems = []


class Chain:

    def __init__(self, eng, sem, start=0):
        self.eng, self.sem, self.n = eng, sem, start

    def __call__(self, ins):
        self.n += 1
        ins.then_inc(self.sem, 1)
        self.eng.wait_ge(self.sem, self.n)


def pow2(nc, link, out, field, tmp_f, tmp_i, src_f, mult, add, lo=1.0, hi=254.0):
    link(nc.vector.tensor_scalar(tmp_f, src_f, float(mult), float(add), ALU.mult, ALU.add))
    link(nc.vector.tensor_scalar(field, tmp_f, float(lo), float(hi), ALU.max, ALU.min))
    pow2_of(nc, link, out, field, tmp_i)


def pow2_of(nc, link, out, field, tmp_i):
    link(nc.vector.tensor_copy(tmp_i, field))
    link(nc.vector.tensor_scalar(out.bitcast(i32), tmp_i, 23, None, ALU.arith_shift_left))


def exponent(nc, link, out_f, tmp_i, value):
    link(nc.vector.tensor_scalar(tmp_i, value.bitcast(i32), 23, None, ALU.arith_shift_right))
    link(nc.vector.tensor_copy(out_f, tmp_i))


(S_MXW, S_MXC, S_AW, S_AC, S_EW, S_EC, S_W, S_ZI, S_A, S_AI, S_SC, S_F0, S_F1, S_F2,
 S_F3, S_T, S_LAM, S_L1, S_L2, S_G, S_GI, S_ACT, S_CU, S_D, S_YI, S_F4, S_F5, S_F6,
 S_O, S_OA, S_OD, S_F7, S_NAI) = range(33)
NSC = 33


def phase_weights_in(g, W32, WH, WL):
    nc, dram = g.nc, g.dram
    with ExitStack() as ctx:
        CA = g.sb("cache_rows", [P, 2464], f32, ctx)
        GM = g.sb("gain_mix", [P, KC], f32, ctx)
        LV = g.sb("lambda_vecs", [P, 4, HD], f32, ctx)
        LP = g.sb("lambda_prod", [P, 2, HD], f32, ctx)
        MK = g.sb("max_by_chunk", [P, KC], f32, ctx)
        TI = g.sb("tmp_int", [P, 2], i32, ctx)
        SC = g.SC
        small_in, cache_in = (g.sem(n) for n in ("w0_small_in", "w0_cache_in"))
        max_local, max_all, dve_step = (g.sem(n) for n in ("w0_max_local", "w0_max_all", "w0_dve_step"))
        scales_ok, hi_ok, lam_dot, lam_exp = (g.sem(n) for n in ("w0_scales", "w0_hi", "w0_lam_dot", "w0_lam_exp"))
        col = lambda c: SC[:, c:c + 1]
        with nc.Block() as block:
            @block.sync
            def _(sp):
                sp.dma_start(GM[:, :], dram["norm_mix_g"]).then_inc(small_in, 16)
                sp.dma_start(g.ident[:, :], dram["ident"]).then_inc(small_in, 16)
                sp.dma_start(LV[:, :, :], dram["lambdas"].rearrange("a n d -> a (n d)").broadcast_to([P, 4 * HD])
                             .rearrange("p (n d) -> p n d", n=4)).then_inc(small_in, 16)
                for k in range(KC):
                    sp.dma_start(W32[:, k, :], dram["w_in"][0, k * P:(k + 1) * P, :]).then_inc(g.w0_k[k], 16)
                at = 0
                for name, width in (("cache_diff_k", 1088), ("cache_diff_v", 1088), ("cache_swa_k", 144), ("cache_swa_v", 144)):
                    sp.dma_start(CA[:, at:at + width], dram[name]
                                 .rearrange("a b r h c d -> (a b r h c d)" if name == "cache_diff_k" else
                                            "a b r h d -> (a b r h d)")
                                 .rearrange("(p n) -> p n", p=P)).then_inc(cache_in, 16)
                    at += width

            @block.gpsimd
            def _(pool):
                for n, (src, dst) in enumerate(((S_MXW, S_AW), (S_MXC, S_AC))):
                    pool.wait_ge(max_local, n + 1)
                    nc.gpsimd.partition_all_reduce(col(dst), col(src), P, RMAX).then_inc(max_all, 1)

            @block.vector
            def _(dve):
                link = Chain(dve, dve_step)
                dve.wait_ge(small_in, 48)
                for n in range(2):
                    link(nc.vector.tensor_tensor(LP[:, n, :], LV[:, 2 * n, :], LV[:, 2 * n + 1, :], ALU.mult))
                    nc.vector.tensor_reduce(col(S_L1 + n), LP[:, n, :], AX.X, ALU.add).then_inc(lam_dot, 1)
                for k in range(KC):
                    dve.wait_ge(g.w0_k[k], 16)
                    link(nc.vector.tensor_reduce(MK[:, k:k + 1], W32[:, k, :], AX.X, ALU.max,
                                                 apply_absolute_value=True))
                link(nc.vector.tensor_tensor(MK[:, :], MK[:, :], GM[:, :], ALU.mult))
                nc.vector.tensor_reduce(col(S_MXW), MK[:, :], AX.X, ALU.max, apply_absolute_value=True).then_inc(max_local, 1)
                dve.wait_ge(cache_in, 64)
                nc.vector.tensor_reduce(col(S_MXC), CA[:, :], AX.X, ALU.max, apply_absolute_value=True).then_inc(max_local, 1)
                dve.wait_ge(lam_exp, 2)
                link(nc.vector.scalar_tensor_tensor(col(S_LAM), col(S_L1), -1.0, col(S_L2), ALU.mult, ALU.add))
                link(nc.vector.tensor_scalar(col(S_LAM), col(S_LAM), -LAM_INIT, None, ALU.add))
                dve.wait_ge(max_all, 2)
                exponent(nc, link, col(S_EW), TI[:, 0:1], col(S_AW))
                exponent(nc, link, col(S_EC), TI[:, 0:1], col(S_AC))
                link(nc.vector.tensor_scalar(col(S_EW), col(S_EW), 30.0, 220.0, ALU.max, ALU.min))
                pow2(nc, link, col(S_W), col(S_F0), col(S_T), TI[:, 0:1], col(S_EW), -1.0, 265.0)
                pow2(nc, link, col(S_ZI), col(S_F0), col(S_T), TI[:, 0:1], col(S_EW), 1.0, -19.0)
                link(nc.vector.tensor_scalar(col(S_F1), col(S_EW), -1.0, 254.0, ALU.mult, ALU.add))
                link(nc.vector.tensor_scalar(col(S_F2), col(S_EC), -1.0, 265.0, ALU.mult, ALU.add))
                link(nc.vector.tensor_tensor(col(S_F2), col(S_F1), col(S_F2), ALU.min))
                pow2(nc, link, col(S_A), col(S_F1), col(S_T), TI[:, 0:1], col(S_F2), 1.0, 0.0, 97.0, 157.0)
                pow2(nc, link, col(S_AI), col(S_F2), col(S_T), TI[:, 0:1], col(S_F1), -1.0, 254.0)
                pow2(nc, link, col(S_SC), col(S_F2), col(S_T), TI[:, 0:1], col(S_F1), -2.0, 378.0)
                link(nc.vector.tensor_scalar(GM[:, :], GM[:, :], col(S_W), None, ALU.mult))
                nc.vector.tensor_scalar(col(S_NAI), col(S_SC), MROW, None, ALU.mult).then_inc(scales_ok, 1)
                for k in range(KC):
                    dve.wait_ge(hi_ok, k + 1)
                    link(nc.vector.scalar_tensor_tensor(WL[:, k, :], W32[:, k, :], GM[:, k:k + 1], WH[:, k, :],
                                                        ALU.mult, ALU.subtract))

            @block.scalar
            def _(act):
                for n in range(2):
                    act.wait_ge(lam_dot, n + 1)
                    nc.scalar.activation(col(S_L1 + n), col(S_L1 + n), ACT.Exp).then_inc(lam_exp, 1)
                act.wait_ge(scales_ok, 1)
                for k in range(KC):
                    nc.scalar.activation(WH[:, k, :], W32[:, k, :], ACT.Copy, scale=GM[:, k:k + 1]).then_inc(hi_ok, 1)


V_COUNT = {0: 0, 1: 1, 2: 1, 3: 1, 4: 2, 5: 3}


def phase_project(g, WH, WL, K1, VH, VL, MW):
    nc, dram = g.nc, g.dram
    with ExitStack() as ctx:
        X = [g.sb(f"x_tile{n}", [P, D], f32, ctx) for n in range(2)]
        CS = [g.sb(f"cos_sin{n}", [P, 2 * HD], f32, ctx) for n in range(2)]
        NH, NL = (g.sb(n, [P, D], f16, ctx) for n in ("norm_hi", "norm_lo"))
        XT = [[g.sb(f"normT_{h}{n}", [P, KC, P], f16, ctx) for h in ("hi", "lo")] for n in range(2)]
        Z = g.sb("z_tile", [P, PROJ], f32, ctx)
        RT = [g.sb(f"rot_tmp{n}", [P, 384], f32, ctx) for n in range(2)]
        KN = g.sb("k_split", [P, HC, P], f16, ctx)
        WS = [g.sb(f"w_scan{n}", [P, WCH], f32, ctx) for n in range(2)]
        ST = g.sb("row_stats", [P, 8], f32, ctx)
        QH = g.sb("q_hi_hi", [P, NQ, P], f16, ctx)
        QL = g.sb("q_lo", [P, NQ, HD], f16, ctx)
        QO = g.sb("qT_hi_hi", [P, HS, P], f16, ctx)
        QT = [g.ps(f"qT_ps{n}", [P, HS * P], f16, ctx) for n in range(2)]
        TH = g.ps("xT_hi_ps", [P, KC * P], f16, ctx)
        TL = g.ps("xT_lo_ps", [P, KC * P], f16, ctx)
        ZP = [g.ps(f"z_ps{n}", [P, 512], f32, ctx) for n in range(3)]
        KT = g.ps("kT_ps", [P, HC * P], f16, ctx)
        SC = g.SC
        col = lambda c: SC[:, c:c + 1]
        s = g.sem
        x_in = [s(f"p1_x_in{n}") for n in range(2)]
        ws_in = [s(f"p1_wscan_in{n}") for n in range(2)]
        stat_ok, rs_ok = s("p1_stat"), s("p1_rs")
        hi_ok, lo_ok, t_ok, th_out, tl_out = s("p1_hi"), s("p1_lo"), s("p1_transposed"), s("p1_th_out"), s("p1_tl_out")
        z_ok, rot_mul, rot_add, v_ok, stored = s("p1_z"), s("p1_rot_mul"), s("p1_rot_add"), s("p1_v"), s("p1_stored")
        kv_hi, kv_lo, kt_ok, kt_out, scanned = s("p1_kv_hi"), s("p1_kv_lo"), s("p1_kt"), s("p1_kt_out"), s("p1_scanned")
        pool_step, ones_ok = s("p1_pool_step"), s("p1_ones")
        cache_in = [s(f"p1_cache_in{n}") for n in range(3)]
        cached = [X[0], X[1], WS[0]]
        qh_ok, ql_ok, qt_ok, qt_out, q1_stored, ql_stored = (
            s(n) for n in ("p1_qh", "p1_ql", "p1_qT", "p1_qT_out", "p1_qT_stored", "p1_ql_stored"))
        STORES = 16 * 3
        sp_turns = s("p1_sp_turns")
        vtile = lambda V, i: V[:, bass.ds(i * HDIF * VW, HDIF * VW)].rearrange("p (h e) -> p h e", h=HDIF)
        scan = [dram[n].rearrange("a r c -> (a r c)").rearrange("(p n) -> p n", p=P) for n in ("w_gate", "w_up", "w_down")]

        with nc.Block() as block:
            @block.sync
            def _(sp):
                def reg(x):
                    return x if isinstance(x, int) else sp.snap(x)

                def load(i, b):
                    row = reg(i * P)
                    if not isinstance(i, int) or i > 1:
                        n_lo, n_rot = reg(i - 1), reg(5 * i - 5)
                        sp.wait_ge(lo_ok, n_lo)
                        sp.wait_ge(rot_mul, n_rot)
                    sp.dma_start(X[b][:, :], dram["x"][bass.ds(row, P), :]).then_inc(x_in[b], 16)
                    sp.dma_start(CS[b][:, :], dram["cos_sin"][bass.ds(row, P), :]).then_inc(x_in[b], 16)

                def store(i, last):
                    row, row_kv, n_rot, n_v = (reg(x) for x in (i * P, META + i * P, 5 * i + 5, 3 * i + 3))
                    sp.wait_ge(rot_add, n_rot)
                    sp.sem_inc(sp_turns, 1)
                    sp.wait_ge(v_ok, n_v)
                    sp.dma_start(g.scr[bass.ds(row, P), :], Z[:, C_KA:C_QD]).then_inc(stored, 16)
                    if not last:
                        sp.dma_start(dram["p_diff_k"][bass.ds(row_kv, P), :], Z[:, C_KD:C_VD]).then_inc(stored, 16)
                        sp.dma_start(dram["p_diff_v"][bass.ds(row_kv, P), :], Z[:, C_VD:PROJ]).then_inc(stored, 16)
                        return
                    m = slice(DEC, DEC + META)
                    for name, a, b in (("diff_k", C_KD, C_VD), ("diff_v", C_VD, PROJ)):
                        sp.dma_start(dram[f"s_{name}"], Z[0:DEC, a:b]).then_inc(stored, 16)
                        sp.dma_start(dram[f"p_{name}"][0:META, :], Z[m, a:b]).then_inc(stored, 16)
                    for name, a, b in (("swa_k", C_KA, C_VA), ("swa_v", C_VA, C_QD)):
                        sp.dma_start(dram[f"p_{name}"][0:META, :], Z[m, a:b]).then_inc(stored, 16)
                        sp.dma_start(dram[f"s_{name}"][META + WIN - DEC:META + WIN, :], Z[0:DEC, a:b]).then_inc(stored, 16)

                def store_ql(i):
                    row, n = reg(i * P), reg(2 * i + 2)
                    sp.wait_ge(ql_ok, n)
                    sp.sem_inc(sp_turns, 1)
                    sp.dma_start(g.ql[bass.ds(row, P), :], QL[:, :, :].rearrange("p h d -> p (h d)")).then_inc(ql_stored, 16)

                def store_q1(i):
                    row, *n = (reg(x) for x in (i * P, 2 * i + 3, 2 * i + 4))
                    for part in range(2):
                        sp.wait_ge(qt_out, n[part])
                        sp.sem_inc(sp_turns, 1)
                        sp.dma_start(g.q1[bass.ds(row, P), HS * P * part:HS * P * (part + 1)],
                                     QO[:, :, :].rearrange("p h d -> p (h d)")).then_inc(q1_stored, 16)

                sp.sem_inc(q1_stored, 16)
                load(0, 0)

                def load_cached():
                    sp.wait_ge(lo_ok, NTT)
                    sp.wait_ge(scanned, 3 * NT)
                    for n, (at, rows) in enumerate(((0, P), (P, P), (2 * P, META))):
                        for name, a, b in (("cache_diff_k", 0, HC * HD), ("cache_diff_v", HC * HD, D)):
                            src = dram[name].rearrange("a b r h c d -> (a b r) (h c d)" if name[-1] == "k"
                                                       else "a b r h d -> (a b r) (h d)")
                            sp.dma_start(cached[n][0:rows, a:b], src[at:at + rows, :]).then_inc(cache_in[n], 16)

                def step(i, b, first, last):
                    if last:
                        load_cached()
                        store_q1(i - 1)
                        store(i, True)
                        store_ql(i)
                        return store_q1(i)
                    load(i + 1, 1 - b)
                    for w in range(3):
                        n = (b + w) % 2
                        at, used = reg(i * WCH), reg(3 * i + w - 1)
                        if not (first and w == 0):
                            sp.wait_ge(scanned, used)
                        sp.dma_start(WS[n][:, :], scan[w][:, bass.ds(at, WCH)]).then_inc(ws_in[n], 16)
                    if not first:
                        store_q1(i - 1)
                    store(i, False)
                    store_ql(i)
                row_tiles(sp, step)
                sp.wait_ge(q1_stored, 16 * 2 * NTT + 16)
                sp.wait_ge(ql_stored, 16 * NTT)
                n = 0
                for name, c in (("swa_k", C_KA), ("swa_v", C_VA)):
                    sp.dma_start(dram[f"p_{name}"][META:META + WIN, :],
                                 g.scr[SEQ - WIN:SEQ, c - C_KA:c - C_KA + KVS * HD]).then_inc(stored, 16)
                    old = dram[f"cache_{name}"].rearrange("a b r h d -> (a b r) (h d)")
                    sp.dma_start(dram[f"s_{name}"][0:META, :], old[0:META, :]).then_inc(stored, 16)
                    sp.dma_start(dram[f"s_{name}"][META:META + WIN - DEC, :],
                                 old[META + DEC:META + WIN, :]).then_inc(stored, 16)
                    n += 3
                sp.wait_ge(stored, STORES * NT + 16 * (9 + n))

            @block.gpsimd
            def _(pool):
                for c, value in ((4, -0.5), (5, EPS), (6, XSC)):
                    nc.gpsimd.memset(ST[:, c:c + 1], value).then_inc(ones_ok, 1)
                nc.gpsimd.memset(VH[:, :].rearrange("p (n e) -> p n e", e=VW)[:, :, VD:VW], 1.0).then_inc(ones_ok, 1)
                nc.gpsimd.memset(VL[:, :].rearrange("p (n e) -> p n e", e=VW)[:, :, VD:VW], 0.0).then_inc(ones_ok, 1)
                pool.wait_ge(ones_ok, 5)

                def rstd(i):
                    pool.wait_ge(stat_ok, i + 1)
                    nc.gpsimd.tensor_tensor(ST[:, 1:2], ST[:, 0:1], ST[:, 5:6], ALU.add).then_inc(pool_step, 1)
                    pool.wait_ge(pool_step, 2 * i + 1)
                    nc.gpsimd.tensor_tensor(ST[:, 2:3], ST[:, 1:2], ST[:, 4:5], ALU.pow).then_inc(pool_step, 1)
                    pool.wait_ge(pool_step, 2 * i + 2)
                    pool.wait_ge(lo_ok, i)
                    nc.gpsimd.tensor_tensor(ST[:, 3:4], ST[:, 2:3], ST[:, 6:7], ALU.mult).then_inc(rs_ok, 1)
                rstd(0)

                def step(i, b, first, last):
                    if not last:
                        rstd(i + 1)
                    for k, n in enumerate((384, 256, 384, 384, 256)):
                        pool.wait_ge(rot_mul, 5 * i + k + 1)
                        nc.gpsimd.tensor_tensor(Z[:, 384 * k:384 * k + n], Z[:, 384 * k:384 * k + n],
                                                RT[(b + k) % 2][:, 0:n], ALU.add).then_inc(rot_add, 1)
                row_tiles(pool, step)

            @block.vector
            def _(dve):
                def norm_lo(i, b):
                    dve.wait_ge(hi_ok, i + 1)
                    dve.wait_ge(t_ok, i)
                    nc.vector.scalar_tensor_tensor(NL[:, :], X[b][:, :], ST[:, 3:4], NH[:, :],
                                                   ALU.mult, ALU.subtract).then_inc(lo_ok, 1)

                def xT_lo_out(i, b, early):
                    dve.wait_ge(t_ok, i + 1)
                    if not early:
                        dve.wait_ge(z_ok, 6 * (i - 1))
                    nc.vector.tensor_copy(XT[b][1][:, :, :], TL[:, :].rearrange("p (k n) -> p k n", k=KC)).then_inc(tl_out, 1)

                def rotary(i, k, b):
                    n = 256 if k in (1, 4) else 384
                    q = (b + k) % 2
                    dve.wait_ge(z_ok, 6 * i + k + 1)
                    cos = CS[b][:, 0:HD].unsqueeze(1).broadcast_to([P, n // HD, HD])
                    src = ZP[k % 3][:, 0:n].rearrange("p (h d) -> p h d", d=HD)
                    dst = Z[:, 384 * k:384 * k + n].rearrange("p (h d) -> p h d", d=HD)
                    tmp = RT[q][:, 0:n].rearrange("p (h d) -> p h d", d=HD)
                    nc.vector.scalar_tensor_tensor(dst, src, col(S_ZI), cos, ALU.mult, ALU.mult)
                    H2 = HD // 2
                    for half in range(2):
                        sin = CS[b][:, HD + half * H2:HD + (half + 1) * H2].unsqueeze(1).broadcast_to([P, n // HD, H2])
                        last = nc.vector.scalar_tensor_tensor(tmp[:, :, half * H2:(half + 1) * H2],
                                                              src[:, :, (1 - half) * H2:(2 - half) * H2],
                                                              col(S_ZI), sin, ALU.mult, ALU.mult)
                    last.then_inc(rot_mul, 1)

                def scan_max(i, b, w):
                    n = (b + w) % 2
                    dve.wait_ge(ws_in[n], scan_count(i, b, w) * 16)
                    nc.vector.tensor_reduce(MW[:, bass.ds(i * 3 + w, 1)], WS[n][:, :], AX.X, ALU.max,
                                            apply_absolute_value=True).then_inc(scanned, 1)

                def q_lo(i, part, first):
                    dve.wait_ge(qh_ok, 2 * i + part + 1)
                    if part == 0 and not first:
                        dve.wait_ge(ql_stored, 16 * i)
                    h = slice(HS * part, HS * part + HS)
                    c = (C_QA, C_QD)[part]
                    nc.vector.scalar_tensor_tensor(QL[:, h, :], Z[:, c:c + HS * HD].rearrange("p (h d) -> p h d", d=HD), col(S_A),
                                                   QH[:, h, 0:HD], ALU.mult, ALU.subtract).then_inc(ql_ok, 1)

                def split_lo(i, ks, vs):
                    dve.wait_ge(kv_hi, i + 1)
                    nc.vector.scalar_tensor_tensor(KN[:, :, HD:P], ks.rearrange("p (h d) -> p h d", d=HD),
                                                   col(S_A), KN[:, :, 0:HD], ALU.mult, ALU.subtract)
                    nc.vector.scalar_tensor_tensor(vtile(VL, i)[:, :, 0:VD],
                                                   vs.rearrange("p (h e) -> p h e", e=VD), col(S_A),
                                                   vtile(VH, i)[:, :, 0:VD], ALU.mult, ALU.subtract).then_inc(kv_lo, 1)

                dve.wait_ge(x_in[0], 32)
                dve.wait_ge(ones_ok, 5)
                norm_lo(0, 0)
                xT_lo_out(0, 0, True)

                def step(i, b, first, last):
                    if not last:
                        norm_lo(i + 1, 1 - b)
                    if not first:
                        dve.wait_ge(ql_ok, 2 * i)
                        dve.wait_ge(stored, STORES * i)
                        dve.wait_ge(kt_ok, i)
                    for k in range(5):
                        if k >= 2:
                            dve.wait_ge(rot_add, 5 * i + k - 1)
                        elif not first:
                            dve.wait_ge(rot_add, 5 * i + k - 1)
                        rotary(i, k, b)
                        if k == 2 and not last:
                            xT_lo_out(i + 1, 1 - b, first)
                        if k < 3 and not last:
                            scan_max(i, b, k)
                    dve.wait_ge(rot_add, 5 * i + 5)
                    dve.wait_ge(v_ok, 3 * i + 3)
                    q_lo(i, 0, first)
                    q_lo(i, 1, first)
                    split_lo(i, Z[:, C_KD:C_VD], Z[:, C_VD:PROJ])
                row_tiles(dve, step)
                for n in range(3):
                    dve.wait_ge(cache_in[n], 32)
                    dve.wait_ge(kt_ok, NTT + n)
                    split_lo(NTT + n, cached[n][:, 0:HC * HD], cached[n][:, HC * HD:D])

            @block.scalar
            def _(act):
                def norm_hi(i, b):
                    act.wait_ge(x_in[b], x_count(i, b) * 32)
                    if not isinstance(i, int) or i > 0:
                        act.wait_ge(t_ok, i)
                    nc.scalar.activation(NH[:, :].bitcast(bf16), X[b][:, :], ACT.Square, scale=D ** -0.5,
                                         accum_out=ST[:, 0:1]).then_inc(stat_ok, 1)
                    act.wait_ge(rs_ok, i + 1)
                    nc.scalar.activation(NH[:, :], X[b][:, :], ACT.Copy, scale=ST[:, 3:4]).then_inc(hi_ok, 1)

                def xT_hi_out(i, b, early):
                    act.wait_ge(t_ok, i + 1)
                    if not early:
                        act.wait_ge(z_ok, 6 * (i - 1))
                    nc.scalar.activation(XT[b][0][:, :, :], TH[:, :].rearrange("p (k n) -> p k n", k=KC), ACT.Copy).then_inc(th_out, 1)

                def values(i, k):
                    lo, hi = {1: (C_VA, C_QD), 4: (C_VD, 1920), 5: (1920, PROJ)}[k]
                    act.wait_ge(z_ok, 6 * i + k + 1)
                    if k < 5:
                        act.wait_ge(rot_mul, 5 * i + k + 1)
                    nc.scalar.activation(Z[:, lo:hi], ZP[k % 3][:, lo - 384 * k:hi - 384 * k], ACT.Copy,
                                         scale=col(S_ZI)).then_inc(v_ok, 1)

                def split_hi(i, ks, vs):
                    nc.scalar.activation(KN[:, :, 0:HD], ks.rearrange("p (h d) -> p h d", d=HD),
                                         ACT.Copy, scale=col(S_A))
                    nc.scalar.activation(vtile(VH, i)[:, :, 0:VD], vs.rearrange("p (h e) -> p h e", e=VD),
                                         ACT.Copy, scale=col(S_A)).then_inc(kv_hi, 1)

                def q_hi(i, part, first):
                    if not first:
                        act.wait_ge(qt_ok, 2 * i + part - 1)
                        act.wait_ge(ql_ok, 2 * i + part - 1)
                    act.wait_ge(rot_add, 5 * i + (2, 4)[part])
                    c = (C_QA, C_QD)[part]
                    nc.scalar.activation(QH[:, HS * part:HS * part + HS, :].rearrange("p h (r d) -> p h r d", r=2),
                                         Z[:, c:c + HS * HD].rearrange("p (h d) -> p h d", d=HD).unsqueeze(2)
                                         .broadcast_to([P, HS, 2, HD]), ACT.Copy, scale=col(S_A)).then_inc(qh_ok, 1)

                def qT_out(i, part):
                    act.wait_ge(qt_ok, 2 * i + part + 1)
                    act.wait_ge(q1_stored, 16 * (2 * i + part) + 16)
                    nc.scalar.activation(QO[:, :, :], QT[part][:, :].rearrange("p (h n) -> p h n", h=HS),
                                         ACT.Copy).then_inc(qt_out, 1)

                def kT_out(i):
                    act.wait_ge(kt_ok, i + 1)
                    nc.scalar.activation(K1[:, :, bass.ds(i * P, P)], KT[:, :].rearrange("p (h n) -> p h n", h=HC),
                                         ACT.Copy).then_inc(kt_out, 1)

                act.sem_inc(qt_out, 2)
                act.sem_inc(kt_out, 1)
                norm_hi(0, 0)
                xT_hi_out(0, 0, True)

                def step(i, b, first, last):
                    if not last:
                        norm_hi(i + 1, 1 - b)
                    if not first:
                        act.wait_ge(stored, STORES * i)
                        act.wait_ge(kv_lo, i)
                    values(i, 1)
                    if not first:
                        kT_out(i - 1)
                    if not last:
                        xT_hi_out(i + 1, 1 - b, first)
                    if not first:
                        qT_out(i - 1, 0)
                    q_hi(i, 0, first)
                    values(i, 4)
                    if not first:
                        qT_out(i - 1, 1)
                    q_hi(i, 1, first)
                    values(i, 5)
                    act.wait_ge(rot_add, 5 * i + 5)
                    act.wait_ge(v_ok, 3 * i + 3)
                    if not first:
                        act.wait_ge(kt_ok, i)
                    split_hi(i, Z[:, C_KD:C_VD], Z[:, C_VD:PROJ])
                row_tiles(act, step)
                kT_out(NT)
                for part in range(2):
                    qT_out(NT, part)
                for n in range(3):
                    act.wait_ge(cache_in[n], 32)
                    act.wait_ge(kv_lo, NTT + n)
                    act.wait_ge(kt_ok, NTT + n)
                    split_hi(NTT + n, cached[n][:, 0:HC * HD], cached[n][:, HC * HD:D])
                    kT_out(NTT + n)

            @block.tensor
            def _(pe):
                def transposes(i):
                    pe.wait_ge(hi_ok, i + 1)
                    pe.wait_ge(th_out, i)
                    for k in range(KC):
                        nc.tensor.transpose(TH[:, k * P:(k + 1) * P], NH[:, k * P:(k + 1) * P], g.ident[:, :])
                    pe.wait_ge(lo_ok, i + 1)
                    pe.wait_ge(tl_out, i)
                    for k in range(KC):
                        last = nc.tensor.transpose(TL[:, k * P:(k + 1) * P], NL[:, k * P:(k + 1) * P], g.ident[:, :])
                    last.then_inc(t_ok, 1)

                def k_transposes(i):
                    pe.wait_ge(kv_lo, i + 1)
                    pe.wait_ge(kt_out, i + 1)
                    for h in range(HC):
                        last = nc.tensor.transpose(KT[:, h * P:(h + 1) * P], KN[:, h, :], g.ident[:, :])
                    last.then_inc(kt_ok, 1)

                def q_transposes(i):
                    for part in range(2):
                        pe.wait_ge(qh_ok, 2 * i + part + 1)
                        pe.wait_ge(qt_out, 2 * i + part + 1)
                        for h in range(HS):
                            last = nc.tensor.transpose(QT[part][:, h * P:(h + 1) * P], QH[:, HS * part + h, :], g.ident[:, :])
                        last.then_inc(qt_ok, 1)

                def product(i, b, k, first):
                    if k >= 3:
                        pe.wait_ge(rot_mul, 5 * i + k - 2)
                        pe.wait_ge(v_ok, 3 * i + V_COUNT[k - 3])
                    elif not first:
                        pe.wait_ge(rot_mul, 5 * i - 5 + min(k + 3, 4) + 1)
                        pe.wait_ge(v_ok, 3 * i - 3 + V_COUNT[k + 3])
                    out = ZP[k % 3][:, 0:384]
                    c = slice(384 * k, 384 * (k + 1))
                    for kc in range(KC):
                        xh, xl = XT[b][0][:, kc, :], XT[b][1][:, kc, :]
                        nc.tensor.matmul(out, xh, WH[:, kc, c], start=kc == 0, stop=False)
                        nc.tensor.matmul(out, xh, WL[:, kc, c], start=False, stop=False)
                        last = nc.tensor.matmul(out, xl, WH[:, kc, c], start=False, stop=kc == KC - 1)
                    last.then_inc(z_ok, 1)

                transposes(0)

                def step(i, b, first, last):
                    pe.wait_ge(th_out, i + 1)
                    pe.wait_ge(tl_out, i + 1)
                    for k in range(3):
                        product(i, b, k, first)
                    if not first:
                        k_transposes(i - 1)
                        q_transposes(i - 1)
                    if not last:
                        transposes(i + 1)
                    for k in range(3, 6):
                        product(i, b, k, first)
                row_tiles(pe, step)
                k_transposes(NT)
                q_transposes(NT)
                for n in range(1, 4):
                    k_transposes(NT + n)


def x_count(i, b):
    return (i - b) // 2 + 1 if isinstance(i, int) else (i - b + 2) // 2


def scan_count(i, b, w):
    before = {0: {0: 1, 1: 1, 2: 2}, 1: {0: 2, 1: 3, 2: 3}}[b][w]
    return ((i - b) // 2) * 3 + before


def row_tiles(eng, body):
    body(0, 0, True, False)
    with eng.Fori(1, NT - 1, 2) as i:
        body(i, 1, False, False)
        body(i + 1, 0, False, False)
    body(NT - 1, 1, False, False)
    body(NT, 0, False, True)


def phase_window(g):
    nc, dram = g.nc, g.dram
    with ExitStack() as ctx:
        NW = NT + 4
        W_S, W_CW, W_CM = NT + 1, NT + 2, NT + 3
        SVW = HD + 1
        KR = g.sb("wkv_rows", [P, NW, 2 * KVS * HD], f32, ctx)
        KN = g.sb("wk_split", [P, NW, KVS, P], f16, ctx)
        SVH, SVL = (g.sb(n, [P, NW * KVS * SVW], f16, ctx) for n in ("wv_hi", "wv_lo"))
        SK = g.sb("wkT_hi_lo", [P, KVS, NW * P], f16, ctx)
        SK2 = g.sb("wkT_hi_max", [HD + 2, KVS, NW * P], f16, ctx)
        QL = g.sb("wq_lo_max", [P, HS, HD + 2], f16, ctx)
        Q1 = [g.sb(f"wqT_hi_hi{n}", [P, HS, P], f16, ctx) for n in range(2)]
        Q2 = [g.sb(f"wqT_lo_max{n}", [HD + 2, HS, P], f16, ctx) for n in range(2)]
        PF = [g.sb(f"wp{n}", [P, GRP, P], f32, ctx) for n in range(6)]
        PH = [g.sb(f"wp_hi{n}", [P, GRP, P], f16, ctx) for n in range(6)]
        PL = [g.sb(f"wp_lo{n}", [P, GRP, P], f16, ctx) for n in range(6)]
        SINK = g.sb("sinks", [P, HS], f32, ctx)
        MX = g.sb("wrow_max", [P, HS], f32, ctx)
        MU = g.sb("wrow_max_used", [P, 3, HS], f32, ctx)
        SX = [g.sb(f"wsink_exps{n}", [P, 2, HS], f32, ctx) for n in range(2)]
        DN = g.sb("wden", [P, 4, GRP], f32, ctx)
        AO = [g.sb(f"wout{n}", [P, HS * HD], f32, ctx) for n in range(2)]
        TQ = g.ps("wqT_ps", [P, HS * P], f16, ctx)
        MP = [g.ps(f"wmax_ps{n}", [P, 512], f32, ctx) for n in range(2)]
        SP = [g.ps(f"ws_ps{n}", [P, 512], f32, ctx) for n in range(3)]
        OP = [g.ps(f"wo_ps{n}", [P, 512], f32, ctx) for n in range(2)]
        SC = g.SC
        col = lambda c: SC[:, c:c + 1]
        s = lambda n: g.sem("w_" + n)
        q_in = [s("q_in0"), s("q_in1")]
        zero_ok, kv_in, kv_hi, kv_lo, kt_ok, kt_out, pad_ok, k2_ok = (
            s(n) for n in ("zero", "kv_in", "kv_hi", "kv_lo", "kt", "kt_out", "pad", "k2"))
        t2_ok, q2_out = s("q2T"), s("q2_out")
        sp_turns = s("sp_turns")
        mx_ok, red_ok, m_ok, m_step, sx_ok, ex_ok = (s(n) for n in ("max_ps", "reduced", "max", "max_step", "sx", "ex"))
        s_ok, e_ok, pl_ok, av_ok, o_out, n_step = (
            s(n) for n in ("scores", "exp", "p_lo", "av", "o_out", "norm_step"))
        stored = [s("stored0"), s("stored1")]
        vt = lambda V, t, j: V[:, bass.ds((t * KVS + j) * SVW, SVW)]
        v4 = lambda V: V[:, :].rearrange("p (t j e) -> p t j e", t=NW, j=KVS)

        def key_tiles(i):
            if isinstance(i, int) and i == TS:
                return W_S, W_CW, W_CM
            return i + 1, i, W_S

        def unit_tile(i, u):
            own, before, meta = key_tiles(i)
            return (meta, before, own)[u % 3]

        with nc.Block() as block:
            @block.sync
            def _(sp):
                sp.dma_start(KR[:, 1:NT + 2, :], g.scr[:, :].rearrange("(t p) c -> p t c", p=P)).then_inc(kv_in, 16)
                sp.dma_start(SINK[:, :], dram["attn_sinks"].broadcast_to([P, HS])).then_inc(kv_in, 16)
                sp.wait_ge(zero_ok, 1)
                for c, name in ((0, "cache_swa_k"), (KVS * HD, "cache_swa_v")):
                    old = dram[name].rearrange("a b r h d -> (a b r) (h d)")
                    sp.dma_start(KR[:, W_CW, c:c + KVS * HD], old[META:META + WIN, :]).then_inc(kv_in, 16)
                    sp.dma_start(KR[DEC:DEC + META, W_CM, c:c + KVS * HD], old[0:META, :]).then_inc(kv_in, 16)

                def load(i, b):
                    row = i * P if isinstance(i, int) else sp.snap(i * P)
                    n_s, n_t = (6 * i - 6, i) if isinstance(i, int) else (sp.snap(6 * i - 6), sp.snap(i))
                    if not isinstance(i, int) or i > 1:
                        sp.wait_ge(s_ok, n_s)
                        sp.sem_inc(sp_turns, 1)
                    sp.dma_start(Q1[b][:, :, :].rearrange("p h n -> p (h n)"), g.q1[bass.ds(row, P), 0:HS * P]).then_inc(q_in[b], 16)
                    if not isinstance(i, int) or i > 0:
                        sp.wait_ge(t2_ok, n_t)
                        sp.sem_inc(sp_turns, 1)
                    sp.dma_start(QL[:, :, 0:HD], g.ql[bass.ds(row, P), 0:HS * HD].rearrange("p (h d) -> p h d", d=HD))\
                        .then_inc(q_in[b], 16)

                load(0, 0)

                def store(i, b):
                    row = i * P if isinstance(i, int) else sp.snap(i * P)
                    sp.wait_ge(o_out, 2 * i + 2)
                    sp.dma_start(g.mix[bass.ds(row, P), 0:HS * HD], AO[b][:, :]).then_inc(stored[b], 16)

                def step(i, b, first, last):
                    if not last:
                        load(i + 1, 1 - b)
                    if not first:
                        store(i - 1, 1 - b)
                row_tiles(sp, step)
                store(NT, 0)
                sp.wait_ge(stored[0], 16 * (NT // 2 + 1))
                sp.wait_ge(stored[1], 16 * (NT // 2))

            @block.gpsimd
            def _(pool):
                link = Chain(pool, zero_ok)
                link(nc.gpsimd.memset(KR[:, W_CM, :], 0.0))
                link(nc.gpsimd.memset(KR[:, 0, :], 0.0))
                link(nc.gpsimd.memset(v4(SVH)[:, :, :, HD:SVW], 1.0))
                link(nc.gpsimd.memset(v4(SVL)[:, :, :, HD:SVW], 0.0))
                link(nc.gpsimd.memset(SK2[HD:HD + 2, :, :], MROW))
                for n in range(6):
                    for buf in (PF, PH, PL):
                        link(nc.gpsimd.memset(buf[n][:, :, :], 0.0))

            @block.vector
            def _(dve):
                dve.wait_ge(kv_hi, 1)
                for j in range(KVS):
                    nc.vector.scalar_tensor_tensor(KN[:, :, j, HD:P], KR[:, :, j * HD:(j + 1) * HD], col(S_A),
                                                   KN[:, :, j, 0:HD], ALU.mult, ALU.subtract)
                    c = (KVS + j) * HD
                    last = nc.vector.scalar_tensor_tensor(v4(SVL)[:, :, j, 0:HD], KR[:, :, c:c + HD], col(S_A),
                                                          v4(SVH)[:, :, j, 0:HD], ALU.mult, ALU.subtract)
                last.then_inc(kv_lo, 1)
                dve.wait_ge(kt_out, KVS * 3)
                dve.wait_ge(zero_ok, 4)
                nc.vector.tensor_copy(SK[:, :, HD:P], SK[:, :, P:P + HD]).then_inc(pad_ok, 1)
                nc.vector.memset(v4(SVH)[:, 0, :, HD:SVW], 0.0).then_inc(pad_ok, 1)
                dve.wait_ge(pad_ok, 2)
                nc.vector.tensor_copy(SK2[0:HD, :, :], SK[0:HD, :, :]).then_inc(k2_ok, 1)

                def reduce_pair(i, r):
                    dve.wait_ge(mx_ok, 4 * i + r + 1)
                    v = MP[r % 2][:, 0:416].rearrange("p (h n) -> p h n", h=2)
                    nc.vector.tensor_reduce(MX[0:HD, 2 * r:2 * r + 2], v[0:HD, :, 0:144], AX.X, ALU.max)
                    nc.vector.tensor_reduce(MX[HD:P, 2 * r:2 * r + 2], v[HD:P, :, 64:208], AX.X, ALU.max).then_inc(red_ok, 1)

                def maxima(i, b):
                    if not isinstance(i, int) or i > 0:
                        dve.wait_ge(t2_ok, i)
                    dve.wait_ge(red_ok, 4 * i + 4)
                    nc.vector.tensor_scalar(QL[:, :, HD:HD + 1], MX[:, :].unsqueeze(2), -1.0 / MROW, None, ALU.mult).then_inc(m_step, 1)
                    dve.wait_ge(m_step, 3 * i + 1)
                    nc.vector.scalar_tensor_tensor(QL[:, :, HD + 1:HD + 2], MX[:, :].unsqueeze(2), -1.0 / MROW,
                                                   QL[:, :, HD:HD + 1], ALU.mult, ALU.subtract).then_inc(m_ok, 1)
                    dve.wait_ge(m_ok, i + 1)
                    nc.vector.tensor_tensor(MU[:, 0, :].unsqueeze(2), QL[:, :, HD:HD + 1], QL[:, :, HD + 1:HD + 2], ALU.add).then_inc(m_step, 1)
                    dve.wait_ge(m_step, 3 * i + 2)
                    nc.vector.tensor_scalar(MU[:, 1, :], MU[:, 0, :], col(S_NAI), -1.0, ALU.mult, ALU.mult).then_inc(m_step, 1)
                    dve.wait_ge(m_step, 3 * i + 3)
                    nc.vector.tensor_tensor(MU[:, 2, :], MU[:, 1, :], SINK[:, :], ALU.max).then_inc(n_step, 1)

                def sink_args(i, b):
                    if not isinstance(i, int) or i > 1:
                        dve.wait_ge(o_out, 2 * i - 2)
                    nc.vector.tensor_tensor(SX[b][:, 0, :], MU[:, 1, :], MU[:, 2, :], ALU.subtract)
                    nc.vector.tensor_tensor(SX[b][:, 1, :], SINK[:, :], MU[:, 2, :], ALU.subtract).then_inc(sx_ok, 1)

                def p_lo(i, u):
                    v = slice(0, HD) if u % 3 == 1 else slice(0, P)
                    dve.wait_ge(e_ok, 6 * i + u + 1)
                    nc.vector.tensor_tensor(PL[u][:, :, v], PF[u][:, :, v], PH[u][:, :, v], ALU.subtract).then_inc(pl_ok, 1)

                def normalise(i, b, j, first):
                    n0 = 6 * i + 3 * j
                    dve.wait_ge(av_ok, n0 + 3)
                    dve.wait_ge(ex_ok, i + 1)
                    if not first:
                        dve.wait_ge(stored[b], 16 * ((i - b) // 2))
                    h = slice(GRP * j, GRP * j + GRP)
                    O = OP[j][:, 0:GRP * SVW].rearrange("p (h e) -> p h e", h=GRP)
                    steps = 3 * (2 * i + j)
                    nc.vector.tensor_tensor(DN[:, 0, :].unsqueeze(2), O[:, :, HD:SVW], SX[b][:, 0, h].unsqueeze(2), ALU.mult).then_inc(d_step, 1)
                    dve.wait_ge(d_step, steps + 1)
                    nc.vector.tensor_tensor(DN[:, 1, :], DN[:, 0, :], SX[b][:, 1, h], ALU.add).then_inc(d_step, 1)
                    dve.wait_ge(d_step, steps + 2)
                    nc.vector.reciprocal(DN[:, 2, :], DN[:, 1, :]).then_inc(d_step, 1)
                    dve.wait_ge(d_step, steps + 3)
                    nc.vector.scalar_tensor_tensor(DN[:, 3, :], DN[:, 2, :], col(S_AI), SX[b][:, 0, h], ALU.mult, ALU.mult).then_inc(f_step, 1)
                    dve.wait_ge(f_step, 2 * i + j + 1)
                    nc.vector.tensor_tensor(AO[b][:, GRP * j * HD:GRP * (j + 1) * HD].rearrange("p (h d) -> p h d", h=GRP),
                                            O[:, :, 0:HD], DN[:, 3, :].unsqueeze(2).broadcast_to([P, GRP, HD]),
                                            ALU.mult).then_inc(o_out, 1)

                d_step, f_step = s("den_step"), s("factor_step")
                for n in range(4):
                    reduce_pair(0, n)
                maxima(0, 0)
                dve.wait_ge(n_step, 1)
                sink_args(0, 0)
                p_lo(0, 0)
                p_lo(0, 1)

                def step(i, b, first, last):
                    p_lo(i, 2)
                    if not first:
                        normalise(i - 1, 1 - b, 1, isinstance(i, int) and i < 3)
                    if not last:
                        reduce_pair(i + 1, 0)
                        reduce_pair(i + 1, 1)
                    p_lo(i, 3)
                    if not last:
                        reduce_pair(i + 1, 2)
                        reduce_pair(i + 1, 3)
                        maxima(i + 1, 1 - b)
                    p_lo(i, 4)
                    normalise(i, b, 0, isinstance(i, int) and i < 2)
                    p_lo(i, 5)
                    if not last:
                        dve.wait_ge(n_step, i + 2)
                        sink_args(i + 1, 1 - b)
                    if not last:
                        p_lo(i + 1, 0)
                        p_lo(i + 1, 1)
                row_tiles(dve, step)
                normalise(NT, 0, 1, False)

            @block.scalar
            def _(act):
                act.wait_ge(kv_in, 16 * 6)
                act.wait_ge(zero_ok, 2)
                for j in range(KVS):
                    nc.scalar.activation(KN[:, :, j, 0:HD], KR[:, :, j * HD:(j + 1) * HD], ACT.Copy, scale=col(S_A))
                    c = (KVS + j) * HD
                    last = nc.scalar.activation(v4(SVH)[:, :, j, 0:HD], KR[:, :, c:c + HD], ACT.Copy, scale=col(S_A))
                last.then_inc(kv_hi, 1)
                for j in range(KVS):
                    for n, (a, b) in enumerate(((0, 8), (8, 16), (16, NW))):
                        act.wait_ge(kt_ok, 3 * j + n + 1)
                        nc.scalar.activation(SK[:, j, a * P:b * P], TQ[:, 0:(b - a) * P], ACT.Copy).then_inc(kt_out, 1)

                def q2T_out(i, b):
                    act.wait_ge(t2_ok, i + 1)
                    nc.scalar.activation(Q2[b][:, :, :], TQ[0:HD + 2, :].rearrange("p (h n) -> p h n", h=HS), ACT.Copy).then_inc(q2_out, 1)

                def sink_exps(i, b):
                    act.wait_ge(sx_ok, i + 1)
                    nc.scalar.activation(SX[b][:, :, :], SX[b][:, :, :], ACT.Exp).then_inc(ex_ok, 1)

                def exps(i, u, first):
                    S = SP[u % 3][:, :].rearrange("p (h n) -> p h n", h=GRP)
                    act.wait_ge(s_ok, 6 * i + u + 1)
                    if not first:
                        act.wait_ge(av_ok, 6 * i + u - 5)
                    parts = {0: ((slice(HD, HD + META), slice(0, P)),),
                             1: ((slice(HD, P), slice(0, HD)),),
                             2: ((slice(0, HD), slice(0, P)), (slice(HD, P), slice(HD, P)))}[u % 3]
                    for rows, q in parts:
                        nc.scalar.activation(PH[u][rows, :, q], S[rows, :, q], ACT.Exp, scale=SC[rows, S_SC:S_SC + 1])
                        last = nc.scalar.activation(PF[u][rows, :, q], S[rows, :, q], ACT.Exp, scale=SC[rows, S_SC:S_SC + 1])
                    last.then_inc(e_ok, 1)

                act.wait_ge(zero_ok, 23)
                q2T_out(0, 0)
                sink_exps(0, 0)
                exps(0, 0, True)
                exps(0, 1, True)

                def step(i, b, first, last):
                    exps(i, 2, first)
                    exps(i, 3, first)
                    exps(i, 4, first)
                    exps(i, 5, first)
                    if not last:
                        q2T_out(i + 1, 1 - b)
                        exps(i + 1, 0, False)
                        sink_exps(i + 1, 1 - b)
                        exps(i + 1, 1, False)
                row_tiles(act, step)

            @block.tensor
            def _(pe):
                pe.wait_ge(kv_lo, 1)
                for j in range(KVS):
                    for n, (a, b) in enumerate(((0, 8), (8, 16), (16, NW))):
                        if n + j:
                            pe.wait_ge(kt_out, 3 * j + n)
                        for t in range(a, b):
                            last = nc.tensor.transpose(TQ[:, (t - a) * P:(t - a + 1) * P], KN[:, t, j, :], g.ident[:, :])
                        last.then_inc(kt_ok, 1)
                pe.wait_ge(kt_out, 6)

                def q2T(i):
                    pe.wait_ge(m_ok, i + 1)
                    if not isinstance(i, int) or i > 0:
                        pe.wait_ge(q2_out, i)
                    for h in range(HS):
                        last = nc.tensor.transpose(TQ[0:HD + 2, h * P:(h + 1) * P], QL[:, h, :], g.ident[:, :])
                    last.then_inc(t2_ok, 1)

                def row_max(i, b, rounds=range(4)):
                    own, before, meta = key_tiles(i)
                    if 0 in rounds:
                        pe.wait_ge(q_in[b], 32 * x_count(i, b))
                    for r in rounds:
                        if not (isinstance(i, int) and i == 0 and r == 0):
                            pe.wait_ge(red_ok, 4 * i + r - 1)
                        for n in range(2):
                            h, o = 2 * r + n, 208 * n
                            k = SK[:, h // GRP, :]
                            for a, w, c in ((0, HD, before * P + HD), (HD, META, meta * P + HD), (HD + META, P, own * P)):
                                last = nc.tensor.matmul(MP[r % 2][:, o + a:o + a + w], Q1[b][:, h, :], k[:, bass.ds(c, w)],
                                                        start=True, stop=True)
                        last.then_inc(mx_ok, 1)

                def scores(i, b, u, first):
                    j = u // 3
                    if not first:
                        pe.wait_ge(e_ok, 6 * i + u - 2)
                    if u == 0:
                        pe.wait_ge(q2_out, i + 1)
                    t = unit_tile(i, u)
                    h = slice(GRP * j, GRP * j + GRP)
                    nc.tensor.matmul(SP[u % 3][:, :], SK[:, j, bass.ds(t * P, P)], Q1[b][:, h, :], start=True, stop=False)
                    nc.tensor.matmul(SP[u % 3][:, :], SK2[:, j, bass.ds(t * P, P)], Q2[b][:, h, :],
                                     start=False, stop=True).then_inc(s_ok, 1)

                def values(i, u, first):
                    j = u // 3
                    pe.wait_ge(pl_ok, 6 * i + u + 1)
                    if u % 3 == 0 and not first:
                        pe.wait_ge(o_out, 2 * i + j - 1)
                    t = unit_tile(i, u)
                    for h in range(GRP):
                        out = OP[j][:, h * SVW:(h + 1) * SVW]
                        lead = u % 3 == 0 and h == 0
                        nc.tensor.matmul(out, PH[u][:, h, :], vt(SVH, t, j), start=lead, stop=False, skip_group_check=True)
                        nc.tensor.matmul(out, PH[u][:, h, :], vt(SVL, t, j), start=False, stop=False, skip_group_check=True)
                        last = nc.tensor.matmul(out, PL[u][:, h, :], vt(SVH, t, j), start=False, stop=u % 3 == 2,
                                                skip_group_check=True)
                    last.then_inc(av_ok, 1)

                pe.wait_ge(k2_ok, 1)
                row_max(0, 0)
                q2T(0)
                scores(0, 0, 0, True)
                scores(0, 0, 1, True)

                def step(i, b, first, last):
                    for u in range(6):
                        if u < 4:
                            scores(i, b, u + 2, first and u + 2 < 3)
                        if not last:
                            if u == 1:
                                row_max(i + 1, 1 - b, (0, 1))
                            if u == 2:
                                row_max(i + 1, 1 - b, (2, 3))
                            if u == 4:
                                q2T(i + 1)
                            if u == 5:
                                scores(i + 1, 1 - b, 0, False)
                        values(i, u, first)
                    if not last:
                        scores(i + 1, 1 - b, 1, False)
                row_tiles(pe, step)


HI_FROM, HI_EVERY = (1, 1, 1, 1, 1), (3, 3, 3, 2, 2)
POOL_EVERY = 2


class Stage:

    def __init__(self, n, unit_base, piece_base, store_base, dve_base, pool_base, hi_base):
        self.n, self.unit_base, self.piece_base, self.store_base = n, unit_base, piece_base, store_base
        self.dve_base, self.pool_base, self.hi_base = dve_base, pool_base, hi_base
        rows, every = slice(0, P), slice(0, 4 * P)
        if n < NT // 4:
            t0 = 4 * n
            self.tile0, self.nq = t0, 4
            self.units = [(TS, "meta", 0, ((slice(DEC, DEC + META), every),))]
            self.units += [(t, f"full{t % 4}", 0, ((rows, every),)) for t in range(t0)]
            self.units += [(t0 + j, f"diag{j}", j, ((slice(0, CH), slice(0, (4 - j) * P)),
                                                    (slice(CH, P), slice(CH, (4 - j) * P)))) for j in range(4)]
            self.pieces = []
            for q in range(4):
                keys = (t0 + q + 1) * P
                k = -(-(keys + META) // 512)
                others = min(512 * (k - 1), keys - P)
                at = 0
                for m in range(k - 1):
                    w = min(512, others - at)
                    self.pieces.append((q, m, [(at, w)], w, w))
                    at += w
                self.pieces.append((q, k - 1, [(TS * P + DEC, META), (at, keys - at)], META + keys - at - CH,
                                    META + keys - at))
            self.slots = [1 + max(p[1] for p in self.pieces if p[0] == q) for q in range(4)]
        else:
            self.tile0, self.nq = TS, 1
            c = slice(0, P)
            self.units = [(NT + 1, "full0", 0, ((rows, c),)), (NT + 2, "full1", 0, ((rows, c),)),
                          (NT + 3, "cached", 0, ((slice(0, META), c),)), (TS, "new", 0, ((slice(0, DEC), c),))]
            self.pieces = [(0, 0, [((NT + 1) * P, PAST + META), (TS * P, DEC)], PAST + META + DEC, PAST + META + DEC)]
            self.slots = [1]
        self.U, self.NP = len(self.units), len(self.pieces)
        self.pool_lo = list(range(2, self.U - 4, POOL_EVERY))
        self.dve_lo = [u for u in range(self.U) if u not in self.pool_lo]
        self.dve_hi = list(range(HI_FROM[n], self.U - 4, HI_EVERY[n]))

    def lo_count(self, h, c, u):
        by_pool = u in self.pool_lo
        mine, base = (self.pool_lo, self.pool_base) if by_pool else (self.dve_lo, self.dve_base)
        return by_pool, base + h * (2 * len(mine)) + (c * len(mine) + mine.index(u) + 1)

    def hi_count(self, h, c, u):
        n = len(self.dve_hi)
        return self.hi_base + h * (2 * n) + (c * n + self.dve_hi.index(u) + 1)

    def cols(self, u):
        return (self.nq - self.units[u][2]) * P


def phase_differential(g, K1, VH, VL):
    nc, dram = g.nc, g.dram
    stages, ub, pb, sb_, db, gb, hb = [], 1, 1, 0, 1, 0, 0
    for n in range(NT // 4 + 1):
        st = Stage(n, ub, pb, sb_, db, gb, hb)
        stages.append(st)
        ub, pb, sb_ = ub + HC * st.U, pb + HC * st.NP, sb_ + HDIF
        db, gb, hb = db + HC * len(st.dve_lo), gb + HC * len(st.pool_lo), hb + HC * len(st.dve_hi)
    with ExitStack() as ctx:
        K2 = g.sb("kT_hi_max", [HD + 2, HC, NKT * P], f16, ctx)
        QL = g.sb("dq_lo_max", [P, 4, HC, HD + 2], f16, ctx)
        Q1 = [g.sb(f"dqT_hi_hi{n}", [P, HC, 4 * P], f16, ctx) for n in range(3)]
        Q2 = g.sb("dqT_lo_max", [HD + 2, HC, 4 * P], f16, ctx)
        widths = {"meta": 4 * P, "cached": P, "new": P}
        widths |= {f"full{n}": 4 * P for n in range(4)} | {f"diag{j}": (4 - j) * P for j in range(4)}
        PF = {n: g.sb(f"dp_{n}", [P, w], f32, ctx) for n, w in widths.items()}
        PH = {n: g.sb(f"dp_hi_{n}", [P, w], f16, ctx) for n, w in widths.items()}
        PL = {n: g.sb(f"dp_lo_{n}", [P, w], f16, ctx) for n, w in widths.items()}
        MP_ = g.sb("drow_max_parts", [P, 4, HC, 5], f32, ctx)
        MX = g.sb("drow_max", [P, 4, HC], f32, ctx)
        RD = g.sb("dden", [P, 3, 4], f32, ctx)
        O1 = g.sb("dfirst", [P, 4, VD], f32, ctx)
        OD = [g.sb(f"ddiff{n}", [P, 4, VD], f32, ctx) for n in range(2)]
        SQ = g.sb("dsquares", [P, VD], bf16, ctx)
        RS = g.sb("dstats", [P, 4, 4], f32, ctx)
        CO = g.sb("dconsts", [P, 3, 4], f32, ctx)
        WB = [g.sb(f"w_out_scan{n}", [P, D], f32, ctx) for n in range(2)]
        TQ = g.ps("dqT_ps", [P, HC * P], f16, ctx)
        MB = [g.ps("dmax_ps", [P, 512], f32, ctx)[:, :], TQ[:, :].bitcast(f32)]
        SP = [g.ps(f"ds_ps{n}", [P, 512], f32, ctx) for n in range(2)]
        OP = [[g.ps(f"do_ps{c}{n}", [P, 512], f32, ctx) for n in range(2)] for c in range(2)]
        SC = g.SC
        col = lambda c: SC[:, c:c + 1]
        s = lambda n: g.sem("d_" + n)
        (ql_in, zero_ok, k2_ok, t2_ok, q2_act, q2_dve, mx_ok, red_ok, m_ok, m_step, s_ok,
         e_ok, pl_ok, av_ok, r_step, o_out, od_ok, sq_ok, rs_step, f_ok, const_ok) = (s(n) for n in (
             "ql_in", "zero", "k2", "q2T", "q2_out_even", "q2_out_odd", "max_ps", "reduced", "max",
             "max_step", "scores", "exp", "p_lo", "av", "recip_step", "o_out", "diff", "squares", "stat_step", "normed",
             "consts"))
        stored = [s("stored0"), s("stored1")]
        q_in = [s(f"q1_in{n}") for n in range(3)]
        wo_in = [s(f"w_out_in{n}") for n in range(2)]
        wo_scanned, sp_turns = s("w_out_scanned"), s("sp_turns")
        T2 = [TQ, MB[0].bitcast(f16)]
        pool_lo_ok, hi_step = s("pool_p_lo"), s("p_hi_by_dve")
        vt = lambda V, t, h: V[:, bass.ds((t * HDIF + h) * VW, VW)]
        kt = lambda K, h, c, t: K[:, :, :].rearrange("p h n -> p (h n)")[:, bass.ds((2 * h + c) * NKT * P + t * P, P)]
        w_out = dram["w_out"].rearrange("a m d -> (a m) d")
        q0 = [0, 4, 8, 12, 16, 17]
        copies = ([0, 2, 4, 6, 8, 9], [0, 2, 4, 6, 8, 8])

        def heads(eng, body):
            with eng.Fori(0, HDIF) as h:
                body(h)

        with nc.Block() as block:
            @block.sync
            def _(sp):
                def load_q1(st):
                    if st.n > 2:
                        sp.wait_ge(s_ok, stages[st.n - 2].unit_base)
                    for q in range(st.nq):
                        r = (st.tile0 + q) * P
                        sp.dma_start(Q1[st.n % 3][:, :, q * P:(q + 1) * P],
                                     g.q1[r:r + P, HS * P:].rearrange("p (h n) -> p h n", n=P)).then_inc(q_in[st.n % 3], 16)

                def load_ql(st):
                    if st.n > 0:
                        sp.wait_ge(t2_ok, q0[st.n])
                    for q in range(st.nq):
                        r = (st.tile0 + q) * P
                        sp.dma_start(QL[:, q, :, 0:HD], g.ql[r:r + P, HS * HD:].rearrange("p (h d) -> p h d", d=HD))\
                            .then_inc(ql_in, 16)
                for x in range(2):
                    sp.sem_inc(stored[x], 16)
                load_q1(stages[0])
                sp.dma_start(K2[0:HD, :, :], K1[0:HD, :, :]).then_inc(k2_ok, 16)
                load_ql(stages[0])
                load_q1(stages[1])
                for st in stages:
                    if st.n + 2 < len(stages):
                        load_q1(stages[st.n + 2])
                    if st.n + 1 < len(stages):
                        load_ql(stages[st.n + 1])
                    with sp.Fori(0, HDIF // 2) as pair:
                        hh = pair * 2
                        if st.n == SCAN_STAGE:
                            for m in range(4):
                                k, n = sp.snap((2 * hh + m) * P), sp.snap(2 * hh + m + 1)
                                sp.wait_ge(wo_scanned, n)
                                sp.sem_inc(sp_turns, 1)
                                sp.dma_start(WB[m % 2][:, :], w_out[bass.ds(k, P), :]).then_inc(wo_in[m % 2], 16)
                        for x in range(2):
                            c = sp.snap(HS * HD + (hh + x) * VD)
                            sp.wait_ge(f_ok, st.store_base + hh + x + 1)
                            r = st.tile0 * P
                            sp.dma_start(g.mix[r:r + st.nq * P, bass.ds(c, VD)].rearrange("(q p) c -> p q c", p=P),
                                         OD[x][:, 0:st.nq, :]).then_inc(stored[x], 16)
                for x in range(2):
                    sp.wait_ge(stored[x], 16 * (2 * len(stages) + 1))

            @block.gpsimd
            def _(pool):
                link = Chain(pool, zero_ok)
                link(nc.gpsimd.memset(K2[HD:HD + 2, :, :], MROW))
                for name in widths:
                    if name[:4] != "full":
                        for buf in (PF, PH, PL):
                            link(nc.gpsimd.memset(buf[name][:, :], 0.0))
                link(nc.gpsimd.memset(CO[:, 1, :], EPS))
                link(nc.gpsimd.memset(CO[:, 2, :], -0.5))
                pool.wait_ge(const_ok, 2)

                def pool_lo(st, h, c, u):
                    b = st.units[u][1]
                    w = st.cols(u)
                    if u in st.dve_hi:
                        pool.wait_ge(hi_step, st.hi_count(h, c, u))
                    else:
                        pool.wait_ge(e_ok, st.unit_base + h * (2 * st.U) + (c * st.U + u + 1))
                    nc.gpsimd.tensor_tensor(PL[b][:, 0:w], PF[b][:, 0:w], PH[b][:, 0:w], ALU.subtract).then_inc(pool_lo_ok, 1)

                def finish(st, h, x):
                    n = st.store_base + h + x
                    nq = slice(0, st.nq)
                    pool.wait_ge(sq_ok, n + 1)
                    nc.gpsimd.tensor_tensor(RS[:, 1, nq], RS[:, 0, nq], CO[:, 0, nq], ALU.mult).then_inc(rs_step, 1)
                    pool.wait_ge(rs_step, 4 * n + 2)
                    nc.gpsimd.tensor_tensor(RS[:, 2, nq], RS[:, 1, nq], CO[:, 1, nq], ALU.add).then_inc(rs_step, 1)
                    pool.wait_ge(rs_step, 4 * n + 3)
                    nc.gpsimd.tensor_tensor(RS[:, 3, nq], RS[:, 2, nq], CO[:, 2, nq], ALU.pow).then_inc(rs_step, 1)
                    pool.wait_ge(rs_step, 4 * n + 4)
                    nc.gpsimd.tensor_tensor(RS[:, 2, nq], RS[:, 3, nq], g.AI4[:, nq], ALU.mult).then_inc(rs_step, 1)
                    pool.wait_ge(rs_step, 4 * n + 5)
                    nc.gpsimd.tensor_tensor(OD[x][:, nq, :], OD[x][:, nq, :],
                                            RS[:, 2, nq].unsqueeze(2).broadcast_to([P, st.nq, VD]), ALU.mult).then_inc(f_ok, 1)

                pool.sem_inc(rs_step, 1)
                for st in stages:
                    with pool.Fori(0, HDIF // 2) as pair:
                        hh = pair * 2
                        for x in range(2):
                            for c in range(2):
                                for u in range(st.U):
                                    if u in st.pool_lo:
                                        pool_lo(st, hh + x, c, u)
                                    if x and not c and u == min(SQUARE_LAG + 1, st.U - 1):
                                        finish(st, hh, 0)
                        finish(st, hh, 1)

            @block.vector
            def _(dve):
                for q in range(4):
                    nc.vector.tensor_copy(g.AI4[:, q:q + 1], col(S_AI))
                nc.vector.memset(RS[:, :, :], 1.0).then_inc(const_ok, 1)
                dve.wait_ge(const_ok, 1)
                nc.vector.tensor_scalar(CO[:, 0, :], g.AI4[:, :], col(S_AI), 1.0 / VD, ALU.mult, ALU.mult).then_inc(const_ok, 1)

                def reduce_piece(st, h, c, p):
                    q, slot, _, wa, wb = st.pieces[p]
                    B = MB[(c * st.NP + p) % 2]
                    dve.wait_ge(mx_ok, st.piece_base + h * (2 * st.NP) + (c * st.NP + p + 1))
                    out = MP_[:, :, :, :].rearrange("p q h s -> p (q h s)")
                    at = lambda: bass.ds((q * HC + 2 * h + c) * 5 + slot, 1)
                    if wa == wb:
                        last = nc.vector.tensor_reduce(out[:, at()], B[:, 0:wa], AX.X, ALU.max)
                    else:
                        nc.vector.tensor_reduce(out[0:CH, at()], B[0:CH, 0:wa], AX.X, ALU.max)
                        last = nc.vector.tensor_reduce(out[CH:P, at()], B[CH:P, 0:wb], AX.X, ALU.max)
                    last.then_inc(red_ok, 1)

                def maxima(st):
                    nq = slice(0, st.nq)
                    dve.wait_ge(red_ok, st.piece_base + HC * st.NP)
                    if st.n:
                        dve.wait_ge(t2_ok, q0[st.n])
                    for q in range(st.nq):
                        last = nc.vector.tensor_reduce(MX[:, q, :], MP_[:, q, :, 0:st.slots[q]], AX.X, ALU.max)
                    last.then_inc(m_step, 1)
                    dve.wait_ge(m_step, 2 * st.n + 1)
                    nc.vector.tensor_scalar(QL[:, nq, :, HD:HD + 1], MX[:, nq, :].unsqueeze(3), -1.0 / MROW, None, ALU.mult).then_inc(m_step, 1)
                    dve.wait_ge(m_step, 2 * st.n + 2)
                    for q in range(st.nq):
                        last = nc.vector.scalar_tensor_tensor(QL[:, q, :, HD + 1:HD + 2], MX[:, q, :].unsqueeze(2), -1.0 / MROW,
                                                              QL[:, q, :, HD:HD + 1], ALU.mult, ALU.subtract)
                    last.then_inc(m_ok, 1)
                    for q in range(1, st.nq, 2):
                        dve.wait_ge(t2_ok, q0[st.n] + q + 1)
                        nc.vector.tensor_copy(Q2[:, :, q * P:(q + 1) * P],
                                              T2[1][0:HD + 2, :].rearrange("p (h n) -> p h n", h=HC)).then_inc(q2_dve, 1)

                def p_lo(st, h, c, u):
                    b = st.units[u][1]
                    w = st.cols(u)
                    if u not in st.dve_hi:
                        dve.wait_ge(e_ok, st.unit_base + h * (2 * st.U) + (c * st.U + u + 1))
                    nc.vector.tensor_tensor(PL[b][:, 0:w], PF[b][:, 0:w], PH[b][:, 0:w], ALU.subtract).then_inc(pl_ok, 1)

                def p_hi(st, h, c, u):
                    b = st.units[u][1]
                    w = st.cols(u)
                    dve.wait_ge(e_ok, st.unit_base + h * (2 * st.U) + (c * st.U + u + 1))
                    nc.vector.tensor_copy(PH[b][:, 0:w], PF[b][:, 0:w]).then_inc(hi_step, 1)
                    dve.wait_ge(hi_step, st.hi_count(h, c, u))

                def normalise(st, h, c, x):
                    n = 2 * st.store_base + 2 * (h + x) + c
                    dve.wait_ge(av_ok, st.unit_base + (h + x) * (2 * st.U) + (c * st.U + st.U))
                    banks = 2 if st.nq == 4 else 1
                    per = min(2, st.nq)
                    O = [OP[c][k][:, 0:per * VW].rearrange("p (q e) -> p q e", q=per) for k in range(banks)]
                    for k in range(banks):
                        last = nc.vector.reciprocal(RD[:, 0, 2 * k:2 * k + per].unsqueeze(2), O[k][:, :, VD:VW])
                    last.then_inc(r_step, 1)
                    if c == 0:
                        dve.wait_ge(r_step, 3 * (st.store_base + h + x) + 1)
                        for k in range(banks):
                            r = RD[:, 0, 2 * k:2 * k + per].unsqueeze(2).broadcast_to([P, per, VD])
                            last = nc.vector.tensor_tensor(O1[:, 2 * k:2 * k + per, :], O[k][:, :, 0:VD], r, ALU.mult)
                        last.then_inc(o_out, 1)
                        return
                    dve.wait_ge(r_step, 3 * (st.store_base + h + x) + 2)
                    nc.vector.tensor_scalar(RD[:, 1, 0:st.nq], RD[:, 0, 0:st.nq], col(S_LAM), None, ALU.mult).then_inc(r_step, 1)
                    dve.wait_ge(r_step, 3 * (st.store_base + h + x) + 3)
                    dve.wait_ge(o_out, n + 1)
                    dve.wait_ge(stored[x], 16 * (2 * st.n + 1) + 8 * h)
                    for q in range(st.nq):
                        last = nc.vector.scalar_tensor_tensor(OD[x][:, q, :], O[q // 2][:, q % 2, 0:VD], RD[:, 1, q:q + 1],
                                                              O1[:, q, :], ALU.mult, ALU.add)
                    last.then_inc(o_out, 1)

                for sem in (pl_ok, red_ok, o_out):
                    dve.sem_inc(sem, 1)
                dve.sem_inc(wo_scanned, 2)
                with dve.Fori(0, HDIF) as h:
                    for c in range(2):
                        for p in range(stages[0].NP):
                            reduce_piece(stages[0], h, c, p)
                maxima(stages[0])
                for st in stages:
                    nxt = stages[st.n + 1] if st.n + 1 < len(stages) else None
                    with dve.Fori(0, HDIF // 2) as pair:
                        hh = pair * 2
                        for x in range(2):
                            for c in range(2):
                                for u in range(st.U):
                                    if u in st.dve_hi:
                                        p_hi(st, hh + x, c, u)
                                    if u not in st.pool_lo:
                                        p_lo(st, hh + x, c, u)
                                    if u == NORM_LAG and x + c:
                                        normalise(st, hh, 1 - c, x + c - 1)
                                    if st.n == SCAN_STAGE and u in SCAN_AT:
                                        part = SCAN_AT.index(u)
                                        if part == 0:
                                            dve.wait_ge(wo_in[c], 16 * (hh + x) + 16)
                                        last = nc.vector.tensor_reduce(g.MO[:, bass.ds(8 * (hh + x) + (4 * c + part), 1)],
                                                                       WB[c][:, part * (D // 4):(part + 1) * (D // 4)],
                                                                       AX.X, ALU.max, apply_absolute_value=True)
                                        if part == 3:
                                            last.then_inc(wo_scanned, 1)
                                    for p in pieces_after(st, nxt, u):
                                        reduce_piece(nxt, hh + x, c, p)
                        normalise(st, hh, 1, 1)
                    if nxt:
                        maxima(nxt)

            @block.scalar
            def _(act):
                def q2T_out(st):
                    for q in range(0, st.nq, 2):
                        act.wait_ge(t2_ok, q0[st.n] + q + 1)
                        nc.scalar.activation(Q2[:, :, q * P:(q + 1) * P], T2[0][0:HD + 2, :].rearrange("p (h n) -> p h n", h=HC),
                                             ACT.Copy).then_inc(q2_act, 1)

                def exps(st, h, idx):
                    _, b, _, parts = st.units[idx % st.U]
                    act.wait_ge(s_ok, st.unit_base + h * (2 * st.U) + (idx + 1))
                    act.wait_ge(av_ok, st.unit_base + h * (2 * st.U) + max(idx - 3, 1 - st.unit_base))
                    S = SP[idx % 2]
                    for rows, q in parts:
                        if idx % st.U not in st.dve_hi:
                            nc.scalar.activation(PH[b][rows, q], S[rows, q], ACT.Exp, scale=SC[rows, S_SC:S_SC + 1])
                        last = nc.scalar.activation(PF[b][rows, q], S[rows, q], ACT.Exp, scale=SC[rows, S_SC:S_SC + 1])
                    last.then_inc(e_ok, 1)

                def squares(st, h, c, x):
                    n = st.store_base + h + x
                    act.wait_ge(o_out, 2 * n + 3)
                    act.wait_ge(rs_step, 4 * n + 1)
                    for q in range(st.nq):
                        if q:
                            act.wait_ge(od_ok, sq_base(st) + (st.nq - 1) * (h + x) + q)
                        last = nc.scalar.activation(SQ[:, :], OD[x][:, q, :], ACT.Square, accum_out=RS[:, 0, q:q + 1])
                        if q < st.nq - 1:
                            last.then_inc(od_ok, 1)
                    last.then_inc(sq_ok, 1)

                act.sem_inc(e_ok, 1)
                act.wait_ge(zero_ok, 24)
                q2T_out(stages[0])
                for st in stages:
                    nxt = stages[st.n + 1] if st.n + 1 < len(stages) else None
                    with act.Fori(0, HDIF // 2) as pair:
                        hh = pair * 2
                        for x in range(2):
                            for c in range(2):
                                for u in range(st.U):
                                    exps(st, hh, (2 * x + c) * st.U + u)
                                    if x and not c and u == min(SQUARE_LAG, st.U - 1):
                                        squares(st, hh, 1, 0)
                        squares(st, hh, 1, 1)
                    if nxt:
                        q2T_out(nxt)

            @block.tensor
            def _(pe):
                def q2T(st, q):
                    n = q0[st.n] + q
                    if q == 0:
                        pe.wait_ge(m_ok, st.n + 1)
                        pe.wait_ge(ql_in, 16 * q0[st.n + 1])
                    if q >= 2:
                        pe.wait_ge((q2_act, q2_dve)[q % 2], copies[q % 2][st.n] + q // 2)
                    for h in range(HC):
                        last = nc.tensor.transpose(T2[q % 2][0:HD + 2, h * P:(h + 1) * P], QL[:, q, h, :], g.ident[:, :])
                    last.then_inc(t2_ok, 1)

                def q1_at(st, h, c, q, w):
                    return Q1[st.n % 3][:, :, :].rearrange("p h n -> p (h n)")[:, bass.ds((2 * h + c) * 4 * P + q * P, w)]

                def q2_at(h, c, q, w):
                    return Q2[:, :, :].rearrange("p h n -> p (h n)")[:, bass.ds((2 * h + c) * 4 * P + q * P, w)]

                def max_piece(st, h, c, p):
                    q, _, runs, _, _ = st.pieces[p]
                    B = MB[(c * st.NP + p) % 2]
                    pe.wait_ge(red_ok, st.piece_base + h * (2 * st.NP) + max(c * st.NP + p - 1, 1 - st.piece_base))
                    at = 0
                    K = K1[:, :, :].rearrange("p h n -> p (h n)")
                    for k0, w in runs:
                        last = nc.tensor.matmul(B[:, at:at + w], q1_at(st, h, c, q, P), K[:, bass.ds((2 * h + c) * NKT * P + k0, w)],
                                                start=True, stop=True)
                        at += w
                    last.then_inc(mx_ok, 1)

                def scores(st, h, idx):
                    e = st.unit_base + h * (2 * st.U) + max(idx - 1, 1 - st.unit_base)
                    h = h + idx // (2 * st.U)
                    c, u = divmod(idx % (2 * st.U), st.U)
                    t, _, q, _ = st.units[u]
                    w = st.cols(u)
                    pe.wait_ge(e_ok, e)
                    out = SP[idx % 2][:, 0:w]
                    nc.tensor.matmul(out, kt(K1, h, c, t), q1_at(st, h, c, q, w), start=True, stop=False)
                    nc.tensor.matmul(out, kt(K2, h, c, t), q2_at(h, c, q, w), start=False, stop=True).then_inc(s_ok, 1)

                def values(st, h, idx):
                    order = max(idx // st.U, 0 if st.n else 1)
                    o = 2 * st.store_base + 2 * h + order
                    by_pool, lo = st.lo_count(h, idx // st.U, idx % st.U)
                    h = h + idx // (2 * st.U)
                    c, u = divmod(idx % (2 * st.U), st.U)
                    t, b, q_first, _ = st.units[u]
                    pe.wait_ge(pool_lo_ok if by_pool else pl_ok, lo)
                    if u == 0:
                        pe.wait_ge(o_out, o)
                    for q in range(q_first, st.nq):
                        out = OP[c][q // 2][:, (q % 2) * VW:(q % 2 + 1) * VW]
                        ph, pl = (buf[b][:, (q - q_first) * P:(q - q_first + 1) * P] for buf in (PH, PL))
                        end = u == (st.U - st.nq + q if st.nq == 4 else st.U - 1)
                        nc.tensor.matmul(out, ph, vt(VH, t, h), start=u == 0 and q % 2 == 0, stop=False, skip_group_check=True)
                        nc.tensor.matmul(out, ph, vt(VL, t, h), start=False, stop=False, skip_group_check=True)
                        last = nc.tensor.matmul(out, pl, vt(VH, t, h), start=False, stop=end, skip_group_check=True)
                    last.then_inc(av_ok, 1)

                for sem in (s_ok, av_ok, mx_ok):
                    pe.sem_inc(sem, 1)
                pe.wait_ge(q_in[0], 16 * 4)
                with pe.Fori(0, HDIF) as h:
                    for c in range(2):
                        for p in range(stages[0].NP):
                            max_piece(stages[0], h, c, p)
                for q in range(4):
                    q2T(stages[0], q)
                pe.wait_ge(k2_ok, 16)
                pe.wait_ge(zero_ok, 1)
                for st in stages:
                    nxt = stages[st.n + 1] if st.n + 1 < len(stages) else None
                    if nxt:
                        pe.wait_ge(q_in[nxt.n % 3], 16 * sum(x.nq for x in stages if x.n <= nxt.n and (x.n - nxt.n) % 3 == 0))
                    pe.wait_ge(q2_act, copies[0][st.n + 1])
                    pe.wait_ge(q2_dve, copies[1][st.n + 1])
                    with pe.Fori(0, HDIF // 2) as pair:
                        hh = pair * 2
                        scores(st, hh, 0)
                        scores(st, hh, 1)
                        for idx in range(4 * st.U):
                            x, c, u = idx // (2 * st.U), idx // st.U % 2, idx % st.U
                            if idx + 2 < 4 * st.U:
                                scores(st, hh, idx + 2)
                            for p in pieces_after(st, nxt, u):
                                max_piece(nxt, hh + x, c, p)
                            if idx:
                                values(st, hh, idx - 1)
                        values(st, hh, 4 * st.U - 1)
                    if nxt:
                        for q in range(nxt.nq):
                            q2T(nxt, q)


NORM_LAG = 2
SCAN_STAGE = 3
SCAN_AT = (5, 7, 9, 11)
SQUARE_LAG = 4


def pieces_after(st, nxt, u):
    return range(u * nxt.NP // st.U, (u + 1) * nxt.NP // st.U) if nxt else ()


def sq_base(st):
    return 3 * HDIF * st.n


def phase_scales(g, WO, WOL, MW, GF):
    nc, dram = g.nc, g.dram
    with ExitStack() as ctx:
        W32 = g.sb("wout32", [P, KC, D], f32, ctx)
        SG, SO = (g.sb(n, [P, 1], f32, ctx) for n in ("gain_sub", "gain_sub_scaled"))
        TI = g.sb("tmp_int2", [P, 4], i32, ctx)
        MA = g.sb("max_parts", [P, 4], f32, ctx)
        MB = g.sb("max_everywhere", [P, 4], f32, ctx)
        EX = g.sb("exponents", [P, 4], f32, ctx)
        s = lambda n: g.sem("o0_" + n)
        w_k = [s(f"chunk_in{k}") for k in range(KC)]
        small_in, local, everywhere, step, scales_ok, hi_ok = (
            s(n) for n in ("small_in", "max_local", "max_all", "dve_step", "scales", "hi"))
        SC = g.SC
        col = lambda c: SC[:, c:c + 1]
        scale = lambda k: col(S_O) if k < KC // 2 else SO[:, 0:1]
        with nc.Block() as block:
            @block.sync
            def _(sp):
                sp.dma_start(SG[:, :], dram["subln_g"]).then_inc(small_in, 16)
                sp.dma_start(GF[:, :], dram["norm_ffn_g"]).then_inc(small_in, 16)
                for k in range(KC):
                    sp.dma_start(W32[:, k, :], dram["w_out"][0, k * P:(k + 1) * P, :]).then_inc(w_k[k], 16)

            @block.gpsimd
            def _(pool):
                pool.wait_ge(local, 1)
                nc.gpsimd.partition_all_reduce(MB[:, :], MA[:, :], P, RMAX).then_inc(everywhere, 1)

            @block.vector
            def _(dve):
                link = Chain(dve, step)
                dve.wait_ge(small_in, 32)
                link(nc.vector.tensor_scalar(SG[:, :], SG[:, :], 1.0 - LAM_INIT, None, ALU.mult))
                link(nc.vector.tensor_scalar(g.MO[:, 2 * KC:4 * KC], g.MO[:, 2 * KC:4 * KC], SG[:, :], None, ALU.mult))
                link(nc.vector.tensor_reduce(MA[:, 0:1], g.MO[:, :], AX.X, ALU.max, apply_absolute_value=True))
                mw = MW[:, :].rearrange("p (i w) -> p i w", w=3)
                link(nc.vector.tensor_reduce(MA[:, 1:2], mw[:, :, 0:2], AX.XY, ALU.max))
                link(nc.vector.tensor_reduce(MA[:, 2:3], mw[:, :, 2:3], AX.XY, ALU.max))
                nc.vector.tensor_reduce(MA[:, 3:4], GF[:, :], AX.X, ALU.max, apply_absolute_value=True).then_inc(local, 1)
                dve.wait_ge(everywhere, 1)
                exponent(nc, link, EX[:, :], TI[:, :], MB[:, :])
                link(nc.vector.tensor_scalar(EX[:, :], EX[:, :], 30.0, 220.0, ALU.max, ALU.min))
                E_o, E_gu, E_d, E_g = (EX[:, n:n + 1] for n in range(4))
                pow2(nc, link, col(S_O), col(S_F0), col(S_T), TI[:, 0:1], E_o, -1.0, 265.0)
                pow2(nc, link, col(S_OD), col(S_F2), col(S_T), TI[:, 0:1], col(S_F0), -1.0, 245.0)
                link(nc.vector.tensor_tensor(col(S_F2), col(S_F0), col(S_F1), ALU.add))
                pow2(nc, link, col(S_OA), col(S_F2), col(S_T), TI[:, 0:1], col(S_F2), -1.0, 381.0)
                link(nc.vector.tensor_tensor(SO[:, 0:1], SG[:, :], col(S_O), ALU.mult))
                dve.sem_inc(scales_ok, 1)
                link(nc.vector.tensor_tensor(col(S_F3), E_g, E_gu, ALU.add))
                pow2(nc, link, col(S_G), col(S_F4), col(S_T), TI[:, 0:1], col(S_F3), -1.0, 393.0)
                pow2(nc, link, col(S_GI), col(S_F5), col(S_T), TI[:, 0:1], col(S_F4), -1.0, 246.0)
                pow2(nc, link, col(S_ACT), col(S_F6), col(S_T), TI[:, 0:1], col(S_F3), -2.0, 626.0)
                link(nc.vector.tensor_tensor(col(S_F5), col(S_F5), col(S_F6), ALU.add))
                pow2(nc, link, col(S_CU), col(S_F5), col(S_T), TI[:, 0:1], col(S_F5), 1.0, -127.0)
                pow2(nc, link, col(S_D), col(S_F7), col(S_T), TI[:, 0:1], E_d, -1.0, 266.0)
                link(nc.vector.tensor_tensor(col(S_F7), col(S_F7), col(S_F6), ALU.add))
                pow2(nc, link, col(S_YI), col(S_F7), col(S_T), TI[:, 0:1], col(S_F7), -1.0, 381.0)
                link(nc.vector.tensor_scalar(GF[:, :], GF[:, :], col(S_G), None, ALU.mult))
                for k in range(KC):
                    dve.wait_ge(hi_ok, k + 1)
                    link(nc.vector.scalar_tensor_tensor(WOL[:, k, :], W32[:, k, :], scale(k), WO[:, k, :],
                                                        ALU.mult, ALU.subtract))

            @block.scalar
            def _(act):
                act.wait_ge(scales_ok, 1)
                for k in range(KC):
                    act.wait_ge(w_k[k], 16)
                    nc.scalar.activation(WO[:, k, :], W32[:, k, :], ACT.Copy, scale=scale(k)).then_inc(hi_ok, 1)


DSC = 512.0


def phase_output(g, WO, WOL, H, N2):
    nc, dram = g.nc, g.dram
    with ExitStack() as ctx:
        M = [g.sb(f"mix_tile{n}", [P, D], f32, ctx) for n in range(2)]
        X = [g.sb(f"x_again{n}", [P, D], f32, ctx) for n in range(2)]
        SH, SL = (g.sb(n, [P, D], f16, ctx) for n in ("mix_hi", "mix_lo"))
        MT = [[g.sb(f"mixT_{h}{n}", [P, KC, P], f16, ctx) for h in ("hi", "lo")] for n in range(2)]
        NH, NL = (g.sb(n, [P, D], f16, ctx) for n in ("hnorm_hi", "hnorm_lo"))
        ST = g.sb("h_stats", [P, 8], f32, ctx)
        TM = [g.ps(f"mixT_ps{n}", [P, KC * P], f16, ctx) for n in range(2)]
        TN = [g.ps(f"hnT_ps{n}", [P, KC * P], f16, ctx) for n in range(2)]
        YP = [[g.ps(f"y_ps{n}{m}", [P, 512], f32, ctx) for m in range(2)] for n in range(2)]
        SC = g.SC
        col = lambda c: SC[:, c:c + 1]
        s = lambda n: g.sem("o_" + n)
        m_in, x_in = ([s(f"{n}_in{b}") for b in range(2)] for n in ("mix", "x"))
        sp_turns = s("sp_turns")
        (const_ok, mh_ok, ml_ok, tm_ok, mt_hi, mt_lo, y_ok, h_ok, sq_ok, step_p, rs_ok, nh_ok, nl_ok, tn_ok, n2_hi, n2_lo,
         a_ok) = (s(n) for n in ("consts", "mix_hi", "mix_lo", "mixT", "mixT_hi_out", "mixT_lo_out", "y", "h", "squares",
                                 "pool_step", "rstd", "norm_hi", "norm_lo", "normT", "n2_hi", "n2_lo", "window_part"))
        act_turns = s("act_turns")
        half = slice(0, D // 2), slice(D // 2, D)
        with nc.Block() as block:
            @block.sync
            def _(sp):
                def load(i, b):
                    row, n_m, n_x = (x if isinstance(x, int) else sp.snap(x) for x in (i * P, i - 1, 2 * i - 2))
                    if not isinstance(i, int) or i > 1:
                        sp.wait_ge(ml_ok, n_m)
                        sp.sem_inc(sp_turns, 1)
                    sp.dma_start(M[b][:, :], g.mix[bass.ds(row, P), :]).then_inc(m_in[b], 16)
                    if not isinstance(i, int) or i > 1:
                        sp.wait_ge(h_ok, n_x)
                        sp.sem_inc(sp_turns, 1)
                    sp.dma_start(X[b][:, :], dram["x"][bass.ds(row, P), :]).then_inc(x_in[b], 16)
                load(0, 0)
                row_tiles(sp, lambda i, b, first, last: None if last else load(i + 1, 1 - b))

            @block.gpsimd
            def _(pool):
                for c, value in ((4, -0.5), (5, EPS), (6, XSC)):
                    nc.gpsimd.memset(ST[:, c:c + 1], value).then_inc(const_ok, 1)
                pool.wait_ge(const_ok, 3)

                def rstd(i):
                    pool.wait_ge(sq_ok, i + 1)
                    nc.gpsimd.tensor_tensor(ST[:, 1:2], ST[:, 0:1], ST[:, 5:6], ALU.add).then_inc(step_p, 1)
                    pool.wait_ge(step_p, 2 * i + 1)
                    nc.gpsimd.tensor_tensor(ST[:, 2:3], ST[:, 1:2], ST[:, 4:5], ALU.pow).then_inc(step_p, 1)
                    pool.wait_ge(step_p, 2 * i + 2)
                    pool.wait_ge(nl_ok, i)
                    nc.gpsimd.tensor_tensor(ST[:, 3:4], ST[:, 2:3], ST[:, 6:7], ALU.mult).then_inc(rs_ok, 1)
                row_tiles(pool, lambda i, b, first, last: rstd(i))

            @block.vector
            def _(dve):
                def mix_lo(i, b):
                    dve.wait_ge(mh_ok, i + 1)
                    if not isinstance(i, int) or i > 0:
                        dve.wait_ge(tm_ok, i)
                    nc.vector.scalar_tensor_tensor(SL[:, half[0]], M[b][:, half[0]], col(S_A), SH[:, half[0]], ALU.mult, ALU.subtract)
                    nc.vector.scalar_tensor_tensor(SL[:, half[1]], M[b][:, half[1]], DSC, SH[:, half[1]],
                                                   ALU.mult, ALU.subtract).then_inc(ml_ok, 1)

                def mixT_lo_out(i, b):
                    dve.wait_ge(tm_ok, i + 1)
                    if not isinstance(i, int) or i > 1:
                        dve.wait_ge(y_ok, 2 * i - 2)
                    nc.vector.tensor_copy(MT[b][1][:, :, :], TM[1][:, :].rearrange("p (k n) -> p k n", k=KC)).then_inc(mt_lo, 1)

                def residual(i, b, n):
                    dve.wait_ge(y_ok, 2 * i + n + 1)
                    if n == 0:
                        dve.wait_ge(x_in[b], x_count(i, b) * 16)
                    out = H[:, bass.ds(i * D + n * 512, 512)]
                    nc.vector.scalar_tensor_tensor(out, YP[n][0][:, :], col(S_OA), X[b][:, half[n]], ALU.mult, ALU.add).then_inc(a_ok, 1)
                    dve.wait_ge(a_ok, 2 * i + n + 1)
                    nc.vector.scalar_tensor_tensor(out, YP[n][1][:, :], col(S_OD), out, ALU.mult, ALU.add).then_inc(h_ok, 1)

                def norm_lo(i):
                    dve.wait_ge(nh_ok, i + 1)
                    nc.vector.scalar_tensor_tensor(NL[:, :], H[:, bass.ds(i * D, D)], ST[:, 3:4], NH[:, :],
                                                   ALU.mult, ALU.subtract).then_inc(nl_ok, 1)

                def n2_lo_out(i):
                    dve.wait_ge(tn_ok, i + 1)
                    nc.vector.tensor_copy(N2[1][:, :, bass.ds(i * P, P)], TN[1][:, :].rearrange("p (k n) -> p k n", k=KC)).then_inc(n2_lo, 1)

                dve.wait_ge(m_in[0], 16)
                dve.sem_inc(n2_lo, 1)
                mix_lo(0, 0)
                mixT_lo_out(0, 0)

                def step(i, b, first, last):
                    if not last:
                        mix_lo(i + 1, 1 - b)
                    if not first:
                        norm_lo(i - 1)
                    residual(i, b, 0)
                    if not last:
                        mixT_lo_out(i + 1, 1 - b)
                    residual(i, b, 1)
                    if not first:
                        n2_lo_out(i - 1)
                row_tiles(dve, step)
                norm_lo(NT)
                n2_lo_out(NT)

            @block.scalar
            def _(act):
                def mix_hi(i, b):
                    act.wait_ge(m_in[b], x_count(i, b) * 16)
                    if not isinstance(i, int) or i > 0:
                        act.wait_ge(tm_ok, i)
                    nc.scalar.activation(SH[:, half[0]], M[b][:, half[0]], ACT.Copy, scale=col(S_A))
                    nc.scalar.activation(SH[:, half[1]], M[b][:, half[1]], ACT.Copy, scale=DSC).then_inc(mh_ok, 1)

                def mixT_hi_out(i, b):
                    act.wait_ge(tm_ok, i + 1)
                    if not isinstance(i, int) or i > 1:
                        act.wait_ge(y_ok, 2 * i - 2)
                    nc.scalar.activation(MT[b][0][:, :, :], TM[0][:, :].rearrange("p (k n) -> p k n", k=KC), ACT.Copy).then_inc(mt_hi, 1)

                def squares(i):
                    act.wait_ge(h_ok, 2 * i + 2)
                    act.sem_inc(act_turns, 1)
                    nc.scalar.activation(NH[:, :].bitcast(bf16), H[:, bass.ds(i * D, D)], ACT.Square, scale=D ** -0.5,
                                         accum_out=ST[:, 0:1]).then_inc(sq_ok, 1)

                def norm_hi(i):
                    act.wait_ge(rs_ok, i + 1)
                    act.sem_inc(act_turns, 1)
                    nc.scalar.activation(NH[:, :], H[:, bass.ds(i * D, D)], ACT.Copy, scale=ST[:, 3:4]).then_inc(nh_ok, 1)

                def n2_hi_out(i):
                    act.wait_ge(tn_ok, i + 1)
                    nc.scalar.activation(N2[0][:, :, bass.ds(i * P, P)], TN[0][:, :].rearrange("p (k n) -> p k n", k=KC),
                                         ACT.Copy).then_inc(n2_hi, 1)
                act.sem_inc(n2_hi, 1)
                mix_hi(0, 0)
                mixT_hi_out(0, 0)

                def step(i, b, first, last):
                    if not last:
                        mix_hi(i + 1, 1 - b)
                    if not first:
                        norm_hi(i - 1)
                    if not last:
                        mixT_hi_out(i + 1, 1 - b)
                    if not first:
                        n2_hi_out(i - 1)
                    squares(i)
                row_tiles(act, step)
                norm_hi(NT)
                n2_hi_out(NT)

            @block.tensor
            def _(pe):
                def mixT(i):
                    pe.wait_ge(ml_ok, i + 1)
                    pe.wait_ge(mt_hi, i)
                    pe.wait_ge(mt_lo, i)
                    for src, dst in ((SH, TM[0]), (SL, TM[1])):
                        for k in range(KC):
                            last = nc.tensor.transpose(dst[:, k * P:(k + 1) * P], src[:, k * P:(k + 1) * P], g.ident[:, :])
                    last.then_inc(tm_ok, 1)

                def normT(i):
                    pe.wait_ge(nl_ok, i + 1)
                    pe.wait_ge(n2_hi, i + 1)
                    pe.wait_ge(n2_lo, i + 1)
                    for src, dst in ((NH, TN[0]), (NL, TN[1])):
                        for k in range(KC):
                            last = nc.tensor.transpose(dst[:, k * P:(k + 1) * P], src[:, k * P:(k + 1) * P], g.ident[:, :])
                    last.then_inc(tn_ok, 1)

                def product(i, b, n):
                    if not isinstance(i, int) or i > 0:
                        pe.wait_ge(h_ok, 2 * i + n - 1)
                    for m in range(2):
                        for k in range(4 * m, 4 * m + 4):
                            hi, lo = MT[b][0][:, k, :], MT[b][1][:, k, :]
                            out = YP[n][m][:, :]
                            nc.tensor.matmul(out, hi, WO[:, k, half[n]], start=k % 4 == 0, stop=False)
                            nc.tensor.matmul(out, hi, WOL[:, k, half[n]], start=False, stop=False)
                            last = nc.tensor.matmul(out, lo, WO[:, k, half[n]], start=False, stop=k % 4 == 3)
                    last.then_inc(y_ok, 1)

                mixT(0)

                def step(i, b, first, last):
                    pe.wait_ge(mt_hi, i + 1)
                    pe.wait_ge(mt_lo, i + 1)
                    product(i, b, 0)
                    if not last:
                        mixT(i + 1)
                    product(i, b, 1)
                    if not first:
                        normT(i - 1)
                row_tiles(pe, step)
                normT(NT)


NTOK = SEQ + DEC
TB = 6
TBW = NTOK // TB
PAIRS = FF // (2 * P)
NORM_BEHIND = 2
YS = 2 * NTT


def phase_ffn(g, H, N2, GF):
    nc, dram = g.nc, g.dram
    with ExitStack() as ctx:
        F = [g.sb(f"{n}32", [P, KC, 2 * P], f32, ctx) for n in ("gate", "up")]
        FH = [g.sb(f"{n}_hi", [P, KC, 2 * P], f16, ctx) for n in ("gate", "up")]
        FL = [g.sb(f"{n}_lo", [P, KC, 2 * P], f16, ctx) for n in ("gate", "up")]
        DW = g.sb("down32", [P, D], f32, ctx)
        DH, DL = (g.sb(n, [P, 2, D], f16, ctx) for n in ("down_hi", "down_lo"))
        AH, AL = (g.sb(n, [P, 2, NTOK], f16, ctx) for n in ("act_hi", "act_lo"))
        SI = [g.sb(f"silu{n}", [P, TBW], f32, ctx) for n in range(2)]
        AF = [g.sb(f"act{n}", [P, TBW], f32, ctx) for n in range(2)]
        GP = [[g.ps(f"{n}_ps{f}", [P, 512], f32, ctx) for n in ("gate", "up")] for f in range(2)]
        YP = [g.ps(f"down_ps{n}", [P, 512], f32, ctx) for n in range(4)]
        SC = g.SC
        col = lambda c: SC[:, c:c + 1]
        s = lambda n: g.sem("f_" + n)
        gu_in = [s(f"gu_in{half}") for half in range(2)]
        gu_hi, gu_lo, d_in, d_hi, d_lo, al_ok, y_ok, h_ok = (
            s(n) for n in ("gu_hi", "gu_lo", "down_in", "down_hi", "down_lo", "act_lo", "y", "h"))
        up_ok, si_ok, mul_ok, ah_ok = ([s(f"{n}{f}") for f in range(2)] for n in ("gate_up", "silu", "act", "act_hi"))
        ST = g.sb("final_stats", [P, 4, NTT], f32, ctx)
        Y = [F[n // 2][:, 4 * (n % 2):4 * (n % 2) + 4, :].rearrange("p k n -> p (k n)") for n in range(4)]
        SQ = FH[0][:, 0:4, :].rearrange("p k n -> p (k n)").bitcast(bf16)
        GN = DW
        g_in, sq_ok, step_p, rs_ok, n_ok, const_ok = (
            s(n) for n in ("gain_in", "squares", "pool_step", "rstd", "y_final", "const"))
        stored = [s(f"stored{n}") for n in range(4)]
        pe_turns = s("pe_turns")
        src = [dram[n].rearrange("a (k p) f -> p (a k) f", p=P) for n in ("w_gate", "w_up")]
        down = dram["w_down"].rearrange("a f d -> (a f) d")

        def steps(eng, body):
            with eng.Fori(0, PAIRS - 1) as i:
                body(i, False)
            body(PAIRS - 1, True)

        with nc.Block() as block:
            @block.sync
            def _(sp):
                with sp.Fori(0, PAIRS) as i:
                    c, r0, r1, n = (sp.snap(x) for x in (i * (2 * P), i * (2 * P), i * (2 * P) + P, KC * i + 1))
                    sp.wait_ge(gu_lo, n)
                    for half in range(2):
                        for w in range(2):
                            k = slice(KC // 2 * half, KC // 2 * (half + 1))
                            sp.dma_start(F[w][:, k, :], src[w][:, k, bass.ds(c, 2 * P)]).then_inc(gu_in[half], 16)
                    sp.wait_ge(d_lo, 2 * i + 1)
                    sp.dma_start(DW[:, :], down[bass.ds(r0, P), :]).then_inc(d_in, 16)
                    sp.wait_ge(d_lo, 2 * i + 2)
                    sp.dma_start(DW[:, :], down[bass.ds(r1, P), :]).then_inc(d_in, 16)
                sp.wait_ge(d_lo, 2 * PAIRS + 1)
                sp.dma_start(GN[:, :], dram["final_norm_g"].broadcast_to([P, D])).then_inc(g_in, 16)
                for t in range(NTT):
                    sp.wait_ge(n_ok, t + 1)
                    if t < NT:
                        sp.dma_start(dram["y_prompt"][t * P:(t + 1) * P, :], Y[t % 4]).then_inc(stored[t % 4], 16)
                    else:
                        sp.dma_start(dram["y_sample"], Y[t % 4][0:DEC, :]).then_inc(stored[t % 4], 16)
                for n in range(4):
                    sp.wait_ge(stored[n], 16 * len(range(n, NTT, 4)))

            @block.gpsimd
            def _(pool):
                nc.gpsimd.memset(ST[:, 3, 0:1], -0.5).then_inc(const_ok, 1)
                nc.gpsimd.memset(ST[:, 3, 1:2], EPS).then_inc(const_ok, 1)
                pool.wait_ge(const_ok, 2)
                for t in range(NTT):
                    pool.wait_ge(sq_ok, t + 1)
                    nc.gpsimd.tensor_tensor(ST[:, 1, t:t + 1], ST[:, 0, t:t + 1], ST[:, 3, 1:2], ALU.add).then_inc(step_p, 1)
                    pool.wait_ge(step_p, t + 1)
                    nc.gpsimd.tensor_tensor(ST[:, 2, t:t + 1], ST[:, 1, t:t + 1], ST[:, 3, 0:1], ALU.pow).then_inc(rs_ok, 1)

            @block.vector
            def _(dve):
                def split_lo(i, k):
                    dve.wait_ge(gu_hi, KC * i + k + 1)
                    for w in range(2):
                        last = nc.vector.scalar_tensor_tensor(FL[w][:, k, :], F[w][:, k, :], GF[:, k:k + 1], FH[w][:, k, :],
                                                              ALU.mult, ALU.subtract)
                    last.then_inc(gu_lo, 1)

                def down_lo(i, f):
                    dve.wait_ge(d_hi, 2 * i + f + 1)
                    nc.vector.scalar_tensor_tensor(DL[:, f, :], DW[:, :], col(S_D), DH[:, f, :], ALU.mult, ALU.subtract).then_inc(d_lo, 1)

                def act_mul(i, t, f):
                    if t:
                        dve.wait_ge(al_ok, 2 * (TB * i + t) + f - 1)
                    dve.wait_ge(si_ok[f], TB * i + t + 1)
                    nc.vector.scalar_tensor_tensor(AF[f][:, :], GP[f][1][:, 0:TBW], col(S_CU), SI[f][:, :],
                                                   ALU.mult, ALU.mult).then_inc(mul_ok[f], 1)

                def act_lo(i, t, f):
                    dve.wait_ge(ah_ok[f], TB * i + t + 1)
                    v = slice(t * TBW, (t + 1) * TBW)
                    nc.vector.tensor_tensor(AL[:, f, v], AF[f][:, :], AH[:, f, v], ALU.subtract).then_inc(al_ok, 1)

                def add(i, t, n):
                    dve.wait_ge(y_ok, YS * i + 2 * t + n + 2)
                    rows = P if t < NT else DEC
                    at = t * D + n * 512
                    nc.vector.scalar_tensor_tensor(H[0:rows, at:at + 512], YP[(2 * t + n) % 4][0:rows, :], SC[0:rows, S_YI:S_YI + 1],
                                                   H[0:rows, at:at + 512], ALU.mult, ALU.add).then_inc(h_ok, 1)
                def scale_row_tile(t):
                    dve.wait_ge(rs_ok, t + 1)
                    if t >= 4:
                        dve.wait_ge(stored[t % 4], 16 * (t // 4))
                    nc.vector.scalar_tensor_tensor(Y[t % 4], H[:, t * D:(t + 1) * D], ST[:, 2, t:t + 1], GN[:, :],
                                                   ALU.mult, ALU.mult).then_inc(n_ok, 1)

                for sem in (gu_lo, d_lo, h_ok, *mul_ok):
                    dve.sem_inc(sem, 1)
                for k in range(KC):
                    split_lo(0, k)

                def step(i, last):
                    for t in range(TB):
                        act_mul(i, t, 0)
                        act_mul(i, t, 1)
                        act_lo(i, t, 0)
                        act_lo(i, t, 1)
                        if t < 2:
                            down_lo(i, t)
                    for t in range(NTT):
                        add(i, t, 0)
                        add(i, t, 1)
                        if t % 2 == 0 and t // 2 < KC and not last:
                            split_lo(i + 1, t // 2)
                        if last and t == NORM_BEHIND:
                            dve.wait_ge(g_in, 16)
                            dve.wait_ge(gu_lo, KC * PAIRS + 1)
                        if last and t >= NORM_BEHIND:
                            scale_row_tile(t - NORM_BEHIND)
                    for t in range(NTT - NORM_BEHIND, NTT) if last else ():
                        scale_row_tile(t)
                steps(dve, step)

            @block.scalar
            def _(act):
                def split_hi(i, k):
                    if k % (KC // 2) == 0:
                        act.wait_ge(gu_in[2 * k // KC], 32 * i + 32)
                    if k == 0:
                        if not isinstance(i, int) or i > 0:
                            for n in range(2):
                                act.wait_ge(up_ok[n], TB * i)
                    for w in range(2):
                        last = nc.scalar.activation(FH[w][:, k, :], F[w][:, k, :], ACT.Copy, scale=GF[:, k:k + 1])
                    last.then_inc(gu_hi, 1)

                def down_hi(i, f):
                    act.wait_ge(d_in, 32 * i + 16 * f + 16)
                    if f == 0:
                        act.wait_ge(y_ok, YS * i + 1)
                    nc.scalar.activation(DH[:, f, :], DW[:, :], ACT.Copy, scale=col(S_D)).then_inc(d_hi, 1)

                def silu(i, t, f):
                    act.wait_ge(up_ok[f], TB * i + t + 1)
                    nc.scalar.activation(SI[f][:, :], GP[f][0][:, 0:TBW], ACT.Silu, scale=col(S_GI)).then_inc(si_ok[f], 1)

                def act_hi(i, t, f):
                    act.wait_ge(mul_ok[f], TB * i + t + 2)
                    nc.scalar.activation(AH[:, f, t * TBW:(t + 1) * TBW], AF[f][:, :], ACT.Copy).then_inc(ah_ok[f], 1)
                for k in range(KC):
                    split_hi(0, k)

                def step(i, last):
                    for t in range(TB):
                        silu(i, t, 0)
                        silu(i, t, 1)
                        act_hi(i, t, 0)
                        act_hi(i, t, 1)
                        if t < 2:
                            down_hi(i, t)
                    if not last:
                        for k in range(KC):
                            split_hi(i + 1, k)
                    for t in range(NTT) if last else ():
                        act.wait_ge(h_ok, YS * i + 2 * t + 3)
                        if t:
                            act.wait_ge(sq_ok, t)
                        nc.scalar.activation(SQ, H[:, t * D:(t + 1) * D], ACT.Square, scale=D ** -0.5,
                                             accum_out=ST[:, 0, t:t + 1]).then_inc(sq_ok, 1)
                steps(act, step)

            @block.tensor
            def _(pe):
                pe.sem_inc(y_ok, 1)

                def gate_up(i, t, f):
                    pe.wait_ge(mul_ok[f], TB * i + t + 1)
                    for w in range(2):
                        for k in range(KC):
                            c = slice(f * P, (f + 1) * P)
                            nh, nl = (N2[x][:, k, bass.ds(t * TBW, TBW)] for x in range(2))
                            out = GP[f][w][:, 0:TBW]
                            nc.tensor.matmul(out, FH[w][:, k, c], nh, start=k == 0, stop=False)
                            nc.tensor.matmul(out, FH[w][:, k, c], nl, start=False, stop=False)
                            last = nc.tensor.matmul(out, FL[w][:, k, c], nh, start=False, stop=k == KC - 1)
                    last.then_inc(up_ok[f], 1)

                def down(i, t, n, bank, rows):
                    out = YP[bank][0:rows, :]
                    c = slice(n * 512, (n + 1) * 512)
                    for f in range(2):
                        ah, al = (A[:, f, bass.ds(t * P, rows)] for A in (AH, AL))
                        nc.tensor.matmul(out, ah, DH[:, f, c], start=f == 0, stop=False)
                        nc.tensor.matmul(out, ah, DL[:, f, c], start=False, stop=False)
                        last = nc.tensor.matmul(out, al, DH[:, f, c], start=False, stop=f == 1)
                    last.then_inc(y_ok, 1)

                def step(i, last):
                    pe.wait_ge(gu_lo, KC * i + KC + 1)
                    pe.sem_inc(pe_turns, 1)
                    with pe.Fori(0, TB) as t:
                        for f in range(2):
                            gate_up(i, t, f)
                    pe.wait_ge(d_lo, 2 * i + 3)
                    pe.wait_ge(al_ok, 2 * TB * i + 2 * (TB - 1))
                    pe.wait_ge(h_ok, YS * i + 1)
                    for j in range(2):
                        for n in range(2):
                            down(i, j, n, 2 * j + n, P)
                    whole = (TB - 1) * TBW // (2 * P)
                    for a, z in ((1, whole), (whole, NT // 2)):
                        if a == whole:
                            pe.wait_ge(al_ok, 2 * TB * i + 2 * TB)
                            pe.sem_inc(pe_turns, 1)
                        with pe.Fori(a, z) as k:
                            for j in range(2):
                                for n in range(2):
                                    pe.wait_ge(h_ok, YS * i + 4 * k + (2 * j + n - 2))
                                    down(i, 2 * k + j, n, 2 * j + n, P)
                    for n in range(2):
                        pe.wait_ge(h_ok, YS * i + 2 * NT + n - 2)
                        down(i, NT, n, n, DEC)
                steps(pe, step)


def build(nc, dram):
    g = Prog(nc, dram, ExitStack())
    with g.ctx:
        g.SC = g.sb("scales", [P, NSC], f32)
        g.AI4 = g.sb("inverse_scale4", [P, 4], f32)
        g.ident = g.sb("identity", [P, P], f16)
        g.w0_k = [g.sem(f"w0_chunk_in{k}") for k in range(KC)]
        g.scr = nc.dram_tensor("window_kv_scratch", (NTT * P, C_QD - C_KA), f32).ap()
        g.q1 = nc.dram_tensor("qT_scratch", (NTT * P, NQ * P), f16).ap()
        g.ql = nc.dram_tensor("q_lo_scratch", (NTT * P, NQ * HD), f16).ap()
        g.mix = nc.dram_tensor("mix_scratch", (NTT * P, D), f32).ap()
        MW = g.sb("ffn_weight_max", [P, 48], f32)
        g.MO = g.sb("w_out_max", [P, 4 * KC], f32)
        with ExitStack() as att:
            nk, nv = HC * NKT * P, NKT * HDIF * VW
            KV = g.sb("keys_values", [P, nk + 2 * nv], f16, att)
            K1 = KV[:, 0:nk].rearrange("p (h n) -> p h n", h=HC)
            VH, VL = KV[:, nk:nk + nv], KV[:, nk + nv:nk + 2 * nv]
            W32 = KV[:, 0:2 * KC * PROJ].bitcast(f32).rearrange("p (k n) -> p k n", k=KC)
            with ExitStack() as win:
                WH = g.sb("w_in_hi", [P, KC, PROJ], f16, win)
                WL = g.sb("w_in_lo", [P, KC, PROJ], f16, win)
                phase_weights_in(g, W32, WH, WL)
                phase_project(g, WH, WL, K1, VH, VL, MW)
            phase_window(g)
            g.phase_end()
            phase_differential(g, K1, VH, VL)
        GF = g.sb("gain_ffn", [P, KC], f32)
        H = g.sb("residual_rows", [P, NTT * D], f32)
        with ExitStack() as ffn:
            N2 = [g.sb(f"ffn_inT_{h}", [P, KC, NTT * P], f16, ffn) for h in ("hi", "lo")]
            with ExitStack() as out:
                WO, WOL = (g.sb(n, [P, KC, D], f16, out) for n in ("w_out_hi", "w_out_lo"))
                phase_scales(g, WO, WOL, MW, GF)
                phase_output(g, WO, WOL, H, N2)
            phase_ffn(g, H, N2, GF)


_OUT = [("y_prompt", (SEQ, D), (1, SEQ, D)), ("y_sample", (DEC, D), (1, DEC, D)),
        ("p_swa_k", (META + WIN, KVS * HD), (1, 1, META + WIN, KVS, HD)),
        ("p_swa_v", (META + WIN, KVS * HD), (1, 1, META + WIN, KVS, HD)),
        ("p_diff_k", (META + SEQ, HC * HD), (1, 1, META + SEQ, HDIF, 2, HD)),
        ("p_diff_v", (META + SEQ, HDIF * VD), (1, 1, META + SEQ, HDIF, VD)),
        ("s_swa_k", (META + WIN, KVS * HD), (1, 1, META + WIN, KVS, HD)),
        ("s_swa_v", (META + WIN, KVS * HD), (1, 1, META + WIN, KVS, HD)),
        ("s_diff_k", (DEC, HC * HD), (1, 1, DEC, HDIF, 2, HD)),
        ("s_diff_v", (DEC, HDIF * VD), (1, 1, DEC, HDIF, VD))]


def _tables():
    pos = np.zeros(NTT * P, np.float32)
    pos[:SEQ] = META + np.arange(SEQ)
    pos[SEQ:SEQ + DEC] = META + PAST + np.arange(DEC)
    pos[SEQ + DEC:SEQ + DEC + META] = np.arange(META)
    inv = (10000.0 ** (-np.arange(0, HD, 2) / HD)).astype(np.float32)
    ang = (pos[:, None] * inv[None, :]).astype(np.float64)
    cos, sin = np.cos(ang), np.sin(ang)
    return np.concatenate([cos, cos, -sin, sin], axis=1).astype(np.float32)


def kernel(**inputs):
    import concourse.bacc as _bacc
    from concourse.bass_utils import run_bass_kernel_spmd as _run

    a = {n: np.asarray(v) for n, v in inputs.items()}
    rows = [a["x_prompt"][0], a["x_sample"][0], a["meta_tokens"],
            np.zeros((NTT * P - SEQ - DEC - META, D), np.float32)]
    arrays = {"x": np.concatenate(rows, axis=0), "cos_sin": _tables(), "ident": np.eye(P, dtype=np.float16),
              "lambdas": np.stack([a[n] for n in ("lambda_q1", "lambda_k1", "lambda_q2", "lambda_k2")], axis=1)}
    for n in ("cache_swa_k", "cache_swa_v", "cache_diff_k", "cache_diff_v", "w_in", "attn_sinks",
              "w_out", "w_gate", "w_up", "w_down"):
        arrays[n] = np.ascontiguousarray(a[n])
    for n in ("norm_mix_g", "norm_ffn_g", "subln_g"):
        arrays[n] = np.ascontiguousarray(a[n][0].reshape(-1, P).T)
    arrays["final_norm_g"] = np.ascontiguousarray(a["final_norm_g"])[None, :]
    nc = _bacc.Bacc("TRN2", target_bir_lowering=False, num_devices=1)
    dram = {n: nc.dram_tensor(f"in_{n}", v.shape, mybir.dt.from_np(v.dtype), kind="ExternalInput").ap()
            for n, v in arrays.items()}
    for n, shape, _ in _OUT:
        dram[n] = nc.dram_tensor(f"out_{n}", shape, f32, kind="ExternalOutput").ap()
    build(nc, dram)
    r = _run(nc, [{f"in_{n}": v for n, v in arrays.items()}], core_ids=[0])
    return tuple(np.reshape(r.results[0][f"out_{n}"], shape) for n, _, shape in _OUT)
```
